# Optimizing a Trainium2 kernel written in Bass

```python
import jax, jax.numpy as jnp
from jax import lax
import numpy as np

D_MODEL = 1024
BATCH = 1
SEQ = 1024
DEPTH = 1

CHUNK = 64
N_MEM = 256
RMS_EPS = 1e-6
ATT_HEADS = 16
ATT_KV_HEADS = 2
ATT_HEAD_DIM = 64
ATT_GROUP = ATT_HEADS // ATT_KV_HEADS
ATT_DIM = ATT_HEADS * ATT_HEAD_DIM
KV_DIM = ATT_KV_HEADS * ATT_HEAD_DIM
ATT_WINDOW = 128
WIN_CHUNKS = ATT_WINDOW // CHUNK
BAND = WIN_CHUNKS * CHUNK
NEG_INF = -1e30
RWKV_HEAD = 64
RWKV_HEADS = D_MODEL // RWKV_HEAD
RWKV_DIM = RWKV_HEADS * RWKV_HEAD
LORA_W = 64
LORA_A = 64
LORA_G = 128
RWKV_SHIFT_SIZES = (RWKV_DIM, RWKV_DIM, RWKV_DIM, LORA_W, LORA_A, LORA_G)
RWKV_SHIFT_DIM = 3 * RWKV_DIM + LORA_W + LORA_A + LORA_G
GN_EPS = 64e-5
IN_SIZES = (ATT_DIM, KV_DIM, KV_DIM, RWKV_SHIFT_DIM, D_MODEL, D_MODEL)
D_IN = ATT_DIM + 2 * KV_DIM + RWKV_SHIFT_DIM + 2 * D_MODEL
X_HEADS = 4
X_HEAD_DIM = D_MODEL // X_HEADS
D_FF = 2816

kernel_name = 'hybrid_swa_sinks_rwkv7_macaron_block'

def _split(z, sizes):
    return jnp.split(z, [int(s) for s in np.cumsum(sizes)[:-1]], axis=-1)

def rmsnorm(x, g):
    xf = x.astype(jnp.float32)
    y = xf * lax.rsqrt(jnp.mean(xf * xf, axis=-1, keepdims=True) + RMS_EPS)
    return (y * g.astype(jnp.float32)).astype(x.dtype)

def swiglu(h, w_gate, w_up, w_down):
    return (jax.nn.silu(h @ w_gate) * (h @ w_up)) @ w_down

def token_shift_mix(z, mu):
    prev = jnp.pad(z, ((0, 0), (1, 0), (0, 0)))[:, :-1]
    return z + (prev - z) * mu

def alibi_slopes(n):
    return 2.0 ** (-8.0 * jnp.arange(1, n + 1, dtype=jnp.float32) / n)

def window_gqa_sinks(q, k, v, sinks):
    b, s, _ = q.shape
    nc = s // CHUNK
    pad = BAND - CHUNK
    qc = q.reshape(b, nc, CHUNK, ATT_KV_HEADS, ATT_GROUP, ATT_HEAD_DIM)
    kp = jnp.pad(k, ((0, 0), (pad, 0), (0, 0))).reshape(b, nc + WIN_CHUNKS - 1, CHUNK, ATT_KV_HEADS, ATT_HEAD_DIM)
    vp = jnp.pad(v, ((0, 0), (pad, 0), (0, 0))).reshape(b, nc + WIN_CHUNKS - 1, CHUNK, ATT_KV_HEADS, ATT_HEAD_DIM)
    kb = jnp.concatenate([kp[:, j:j + nc] for j in range(WIN_CHUNKS)], axis=2)
    vb = jnp.concatenate([vp[:, j:j + nc] for j in range(WIN_CHUNKS)], axis=2)
    scores = jnp.einsum('bcqhgd,bckhd->bchgqk', qc, kb).astype(jnp.float32) * (ATT_HEAD_DIM ** -0.5)
    qi = jnp.arange(CHUNK)[:, None]
    kj = jnp.arange(BAND)[None, :]
    dist = jnp.abs(qi + pad - kj).astype(jnp.float32)
    slopes = alibi_slopes(ATT_HEADS).reshape(ATT_KV_HEADS, ATT_GROUP)
    scores = scores - slopes[:, :, None, None] * dist
    key_pos = jnp.arange(nc)[:, None] * CHUNK + jnp.arange(BAND)[None, :] - pad
    scores = jnp.where((key_pos >= 0)[None, :, None, None, None, :], scores, NEG_INF)
    sink = jnp.broadcast_to(sinks.astype(jnp.float32).reshape(ATT_KV_HEADS, ATT_GROUP, 1, 1),
                            scores.shape[:-1] + (1,))
    probs = jax.nn.softmax(jnp.concatenate([scores, sink], axis=-1), axis=-1)[..., :BAND]
    out = jnp.einsum('bchgqk,bckhd->bcqhgd', probs.astype(v.dtype), vb)
    return out.reshape(b, s, ATT_DIM)

def rwkv7_time_mix(zr, zk, zv, uw, ua, ug, w0, w2, a0, a2, g2, k_k, k_a, r_k, ln_w, ln_b):
    b, s, _ = zr.shape
    f32 = jnp.float32

    def heads(t):
        return t.reshape(b, s, RWKV_HEADS, RWKV_HEAD)

    w_log = -jax.nn.softplus(-(w0 + jnp.tanh(uw) @ w2)) - 0.5
    decay = jnp.exp(-jnp.exp(w_log.astype(f32)))
    a = jax.nn.sigmoid(a0 + ua @ a2)
    g = jax.nn.sigmoid(ug) @ g2
    kk = heads(zk * k_k).astype(f32)
    kk = kk / jnp.maximum(jnp.sqrt(jnp.sum(kk * kk, axis=-1, keepdims=True)), 1e-12)
    k = zk * (1 + (a - 1) * k_a)
    r_h, k_h, v_h = heads(zr), heads(k), heads(zv)
    a_h = heads(a).astype(f32)
    seq_in = tuple(jnp.moveaxis(t.astype(f32), 1, 0)
                   for t in (r_h, heads(decay), k_h, v_h, -kk, kk * a_h))

    def step(state, inp):
        r_t, w_t, k_t, v_t, a_t, b_t = inp
        sa = jnp.einsum('bhvk,bhk->bhv', state, a_t)
        state = state * w_t[:, :, None, :] + sa[..., None] * b_t[:, :, None, :] + v_t[..., None] * k_t[:, :, None, :]
        return state, jnp.einsum('bhvk,bhk->bhv', state, r_t)

    s0 = jnp.zeros((b, RWKV_HEADS, RWKV_HEAD, RWKV_HEAD), f32)
    _, y = lax.scan(step, s0, seq_in)
    y = jnp.moveaxis(y, 0, 1)
    mu = jnp.mean(y, axis=-1, keepdims=True)
    var = jnp.mean(jnp.square(y - mu), axis=-1, keepdims=True)
    y = ((y - mu) * lax.rsqrt(var + GN_EPS)).reshape(b, s, RWKV_DIM)
    y = y * ln_w.astype(f32) + ln_b.astype(f32)
    bonus = jnp.sum((r_h * k_h * r_k).astype(f32), axis=-1, keepdims=True) * v_h.astype(f32)
    y = y + bonus.reshape(b, s, RWKV_DIM)
    return (y * g.astype(f32)).astype(zr.dtype)

def memory_cross_attention(h, m, w_cq, w_ckv, w_co):
    b, s, _ = h.shape
    q = (h @ w_cq).reshape(b, s, X_HEADS, X_HEAD_DIM)
    mk, mv = _split(m @ w_ckv, (D_MODEL, D_MODEL))
    mk = mk.reshape(b, -1, X_HEADS, X_HEAD_DIM)
    mv = mv.reshape(b, -1, X_HEADS, X_HEAD_DIM)
    scores = jnp.einsum('bshd,bmhd->bhsm', q, mk).astype(jnp.float32) * (X_HEAD_DIM ** -0.5)
    probs = jax.nn.softmax(scores, axis=-1)
    out = jnp.einsum('bhsm,bmhd->bshd', probs.astype(mv.dtype), mv).reshape(b, s, D_MODEL)
    return out @ w_co

def setup_inputs(seed: int = 0) -> dict:
    key = jax.random.key(seed)
    ks = jax.random.split(key, 32)
    f32 = jnp.float32

    def nrm(k, shape, scale):
        return jax.random.normal(k, shape, f32) * scale

    def gain(k, shape):
        return 1.0 + nrm(k, shape, 0.02)

    L, D = DEPTH, D_MODEL
    return {
        'x': nrm(ks[0], (BATCH, SEQ, D), 1.0),
        'mem': nrm(ks[1], (BATCH, N_MEM, D), 1.0),
        'ffn1_norm': gain(ks[2], (L, D)),
        'ffn1_w_gate': nrm(ks[3], (L, D, D_FF), D ** -0.5),
        'ffn1_w_up': nrm(ks[4], (L, D, D_FF), D ** -0.5),
        'ffn1_w_down': nrm(ks[5], (L, D_FF, D), D_FF ** -0.5),
        'mix_norm': gain(ks[6], (L, D)),
        'w_in': nrm(ks[7], (L, D, D_IN), D ** -0.5),
        'attn_sinks': nrm(ks[8], (L, ATT_HEADS), 0.5),
        'rwkv_mu': jax.random.uniform(ks[9], (L, RWKV_SHIFT_DIM), f32),
        'rwkv_w0': jax.random.uniform(ks[10], (L, RWKV_DIM), f32, -6.0, 0.0),
        'rwkv_w2': nrm(ks[11], (L, LORA_W, RWKV_DIM), 0.1 * LORA_W ** -0.5),
        'rwkv_a0': nrm(ks[12], (L, RWKV_DIM), 0.1),
        'rwkv_a2': nrm(ks[13], (L, LORA_A, RWKV_DIM), LORA_A ** -0.5),
        'rwkv_g2': nrm(ks[14], (L, LORA_G, RWKV_DIM), LORA_G ** -0.5),
        'rwkv_k_k': 0.85 + nrm(ks[15], (L, RWKV_DIM), 0.05),
        'rwkv_k_a': 1.0 + nrm(ks[16], (L, RWKV_DIM), 0.05),
        'rwkv_r_k': nrm(ks[17], (L, RWKV_HEADS, RWKV_HEAD), 0.1),
        'rwkv_ln_w': gain(ks[18], (L, RWKV_DIM)),
        'rwkv_ln_b': nrm(ks[19], (L, RWKV_DIM), 0.02),
        'w_out': nrm(ks[20], (L, D, D), D ** -0.5),
        'cross_norm': gain(ks[21], (L, D)),
        'mem_norm': gain(ks[22], (L, D)),
        'w_cq': nrm(ks[23], (L, D, D), D ** -0.5),
        'w_ckv': nrm(ks[24], (L, D, 2 * D), D ** -0.5),
        'w_co': nrm(ks[25], (L, D, D), D ** -0.5),
        'ffn2_norm': gain(ks[26], (L, D)),
        'ffn2_w_gate': nrm(ks[27], (L, D, D_FF), D ** -0.5),
        'ffn2_w_up': nrm(ks[28], (L, D, D_FF), D ** -0.5),
        'ffn2_w_down': nrm(ks[29], (L, D_FF, D), D_FF ** -0.5),
        'final_norm': gain(ks[30], (D,)),
    }

def reference(x, mem, ffn1_norm, ffn1_w_gate, ffn1_w_up, ffn1_w_down, mix_norm, w_in, attn_sinks,
              rwkv_mu, rwkv_w0, rwkv_w2, rwkv_a0, rwkv_a2, rwkv_g2, rwkv_k_k, rwkv_k_a, rwkv_r_k,
              rwkv_ln_w, rwkv_ln_b, w_out, cross_norm, mem_norm, w_cq, w_ckv, w_co,
              ffn2_norm, ffn2_w_gate, ffn2_w_up, ffn2_w_down, final_norm):
    for l in range(DEPTH):
        x = x + 0.5 * swiglu(rmsnorm(x, ffn1_norm[l]), ffn1_w_gate[l], ffn1_w_up[l], ffn1_w_down[l])
        h = rmsnorm(x, mix_norm[l])
        q, k, v, z_rwkv, gate_a, gate_b = _split(h @ w_in[l], IN_SIZES)
        zr, zk, zv, uw, ua, ug = _split(token_shift_mix(z_rwkv, rwkv_mu[l]), RWKV_SHIFT_SIZES)
        o_a = window_gqa_sinks(q, k, v, attn_sinks[l])
        o_b = rwkv7_time_mix(zr, zk, zv, uw, ua, ug, rwkv_w0[l], rwkv_w2[l], rwkv_a0[l], rwkv_a2[l],
                             rwkv_g2[l], rwkv_k_k[l], rwkv_k_a[l], rwkv_r_k[l], rwkv_ln_w[l], rwkv_ln_b[l])
        merged = jax.nn.sigmoid(gate_a) * o_a + jax.nn.sigmoid(gate_b) * o_b
        x = x + merged @ w_out[l]
        x = x + memory_cross_attention(rmsnorm(x, cross_norm[l]), rmsnorm(mem, mem_norm[l]),
                                       w_cq[l], w_ckv[l], w_co[l])
        x = x + 0.5 * swiglu(rmsnorm(x, ffn2_norm[l]), ffn2_w_gate[l], ffn2_w_up[l], ffn2_w_down[l])
    return rmsnorm(x, final_norm)


_drawn_inputs = setup_inputs


def setup_inputs(seed=0):
    import zlib

    import numpy as np

    out = dict(_drawn_inputs(seed))
    spreads = {}
    factors = {'ffn1_norm': 5.924,
     'mix_norm': 4.68,
     'attn_sinks': 64.0,
     'rwkv_w2': 27.523,
     'rwkv_a0': 5.778,
     'rwkv_k_k': 22.445,
     'rwkv_k_a': 4.031,
     'rwkv_ln_w': 64.0,
     'rwkv_ln_b': 64.0,
     'cross_norm': 8.0,
     'mem_norm': 8.0,
     'ffn2_norm': 30.035,
     'final_norm': 7.686}
    for name, (base, spread) in spreads.items():
        noise = np.random.default_rng([zlib.crc32(name.encode()), seed]).standard_normal(out[name].shape)
        drawn = base * np.exp(spread * noise) if base else spread * noise
        out[name] = __import__('jax').numpy.asarray(drawn.astype(out[name].dtype))
    for name, factor in factors.items():
        out[name] = (out[name] * factor).astype(out[name].dtype)
    return out
```

```python
import concourse.bass as bass
from concourse import mybir
from contextlib import ExitStack
import numpy as np

F32 = mybir.dt.float32
ACT = mybir.ActivationFunctionType
ALU = mybir.AluOpType
AX = mybir.AxisListType
ds = bass.ds

P = 128
SBUF_WORDS = 53000
D = 1024
KT = D // P
T = 1024
HALF = 512
NF = 2816 // P
CH = 64
NC = HALF // CH
PAIRS = 8
NMEM = 256
MT = NMEM // P
XH = 4
RMS_EPS = 1e-6
GN_EPS = 64e-5
LEVELS = [2, 4, 8, 16, 32]
C_DECAY = -0.5 * float(np.exp(-0.5))

PAR = ["ffn1_norm", "mix_norm", "cross_norm", "mem_norm", "ffn2_norm", "final_norm", "mu_r", "mu_k", "mu_v",
       "w0", "a0", "k_k", "k_a", "r_k", "ln_w", "ln_b", "sink"]
NPAR = len(PAR)
COLS = {"q": 0, "ak": 1024, "av": 1152, "r": 1280, "k": 2304, "v": 3328, "u": 4352, "ug": 4480, "ga": 4608,
        "gb": 5632}


def constants():
    row, col = np.arange(P)[:, None], np.arange(P)[None, :]
    i, j = row % CH, np.arange(CH)[None, :]
    parts = {"ident": row == col, "stack_ident": i == j, "bd_ones": row // CH == col // CH,
             "ones": np.ones((P, P)), "dist": np.abs(i + CH - col),
             "neg_slope": -2.0 ** (-8.0 * (2 * np.arange(PAIRS)[None, :] + row // CH + 1) / 16),
             "row_before_col": i < j, "row_upto_col": i <= j, "col_before_row": j < i,
             "keep": np.ones((P, 1)) * (np.arange(HALF)[None, :] % CH != 0)}

    def joins(m, a, b):
        return (a // (2 * m) == b // (2 * m)) & ((a // m) % 2 == 1) & ((b // m) % 2 == 0)

    parts["join1"] = joins(1, i, j)
    parts["join1T"] = joins(1, j, i)
    for m in LEVELS:
        parts[f"join{m}"] = joins(m, i, j)
    where, at = {}, 0
    for name, a in parts.items():
        where[name] = (at, a.shape[1])
        at += a.shape[1]
    return np.concatenate([np.asarray(a, np.float32) for a in parts.values()], 1), where


def build(nc, d, out, x_spill, m_spill):
    table, where = constants()
    ctx = ExitStack()
    with ctx:
        def sem(name):
            return ctx.enter_context(nc.semaphore(name))

        arena = ctx.enter_context(nc.sbuf_tensor("arena", [P, SBUF_WORDS], F32))
        bank = ctx.enter_context(nc.psum_tensor("bank", [P, 8, 512], F32))

        class Region:

            def __init__(self, at):
                self.at = at

            def __call__(self, *dims):
                n = int(np.prod(dims))
                v = arena[:, self.at:self.at + n]
                self.at += n
                assert self.at <= SBUF_WORDS, self.at
                if len(dims) == 2:
                    v = v.rearrange("p (a b) -> p a b", a=dims[0])
                elif len(dims) == 3:
                    v = v.rearrange("p (a b c) -> p a b c", a=dims[0], b=dims[1])
                return v

        keep = Region(0)
        cst = keep(table.shape[1])
        par = keep(NPAR, KT)
        par_u = keep(2)
        eps = keep(2)
        phase_base = keep.at
        xT_at = phase_base
        xT = keep(KT, T)
        after_x = keep.at

        def c(name):
            at, n = where[name]
            return cst[:, at:at + n]

        def gain(name, kt):
            return par[:, PAR.index(name), kt:kt + 1]

        def panels(w, rows=KT):
            return w.rearrange("(k p) n -> p k n", p=P)

        io = Region(after_x)
        x_rows = io(8, D)
        s_cst, s_xin, s_x_tr, s_x_ev = sem("consts_loaded"), sem("rows_loaded"), sem("x_transposed"), sem("x_stored")
        s_eps = sem("eps_set")
        with nc.Block() as block:
            @block.sync
            def _(sp):
                sp.dma_start(cst[:], d["consts"][:, :]).then_inc(s_cst, 16)
                sp.dma_start(par[:], d["params"].rearrange("p (a b) -> p a b", a=NPAR)).then_inc(s_cst, 16)
                sp.dma_start(par_u[:], d["params_u"][:, :]).then_inc(s_cst, 16)
                sp.dma_start(x_rows[:], d["x"].rearrange("(t p) c -> p t c", p=P)).then_inc(s_xin, 16)

            @block.gpsimd
            def _(pool):
                nc.gpsimd.memset(eps[:, 0:1], RMS_EPS).then_inc(s_eps, 1)
                nc.gpsimd.memset(eps[:, 1:2], GN_EPS).then_inc(s_eps, 1)

            @block.tensor
            def _(pe):
                pe.wait_ge(s_cst, 48)
                pe.wait_ge(s_xin, 16)
                for g in range(16):
                    if g >= 8:
                        pe.wait_ge(s_x_ev, g - 7)
                    for j in range(4):
                        last = nc.tensor.transpose(bank[:, g % 8, j * P:(j + 1) * P],
                                                   x_rows[:, 4 * (g % 2) + j, (g // 2) * P:(g // 2 + 1) * P],
                                                   c("ident"))
                    last.then_inc(s_x_tr, 1)

            @block.vector
            def _(dve):
                for g in range(16):
                    dve.wait_ge(s_x_tr, g + 1)
                    nc.vector.tensor_copy(xT[:, g // 2, (g % 2) * HALF:(g % 2 + 1) * HALF],
                                          bank[:, g % 8, :]).then_inc(s_x_ev, 1)
                dve.wait_ge(s_x_ev, 16)
                dve.wait_ge(s_eps, 2)

        class Norm:

            squared, summed, rooted = sem("norm_squared"), sem("norm_summed"), sem("norm_rooted")
            inverted, done = sem("norm_inverted"), sem("norm_done")
            uses, parts_before = 0, 0

            def __init__(self, src, dst, sq, rms, name, width):
                self.src, self.dst, self.sq, self.rms, self.name, self.width = src, dst, sq, rms, name, width
                self.parts = [(a, min(HALF, width - a)) for a in range(0, width, HALF)]
                self.n0, self.p0 = Norm.uses, Norm.parts_before
                Norm.uses += 1
                Norm.parts_before += len(self.parts)

            def act(self, act):
                for kt in range(KT):
                    nc.scalar.activation(self.sq[:, kt], self.src[:, kt], ACT.Square).then_inc(self.squared, 1)
                for n, (a, w) in enumerate(self.parts):
                    act.wait_ge(self.summed, self.p0 + n + 1)
                    nc.scalar.activation(self.rms[:, a:a + w], bank[:, 6 + n, 0:w], ACT.Sqrt, bias=eps[:, 0:1],
                                         scale=1.0 / D).then_inc(self.rooted, 1)

            def pe(self, pe):
                pe.wait_ge(self.squared, KT * (self.n0 + 1))
                for n, (a, w) in enumerate(self.parts):
                    for kt in range(KT):
                        last = nc.tensor.matmul(bank[:, 6 + n, 0:w], c("ones"), self.sq[:, kt, a:a + w],
                                                start=kt == 0, stop=kt == KT - 1)
                    last.then_inc(self.summed, 1)

            def dve(self, dve):
                for n, (a, w) in enumerate(self.parts):
                    dve.wait_ge(self.rooted, self.p0 + n + 1)
                    nc.vector.reciprocal(self.rms[:, a:a + w], self.rms[:, a:a + w]).then_inc(self.inverted, 1)
                    dve.wait_ge(self.inverted, self.p0 + n + 1)
                    for kt in range(KT):
                        nc.vector.scalar_tensor_tensor(
                            out=self.dst[:, kt, a:a + w], in0=self.src[:, kt, a:a + w], scalar=gain(self.name, kt),
                            in1=self.rms[:, a:a + w], op0=ALU.mult, op1=ALU.mult).then_inc(self.done, 1)

            def wait(self, eng, part=1):
                eng.wait_ge(self.done, KT * (self.p0 + min(part + 1, len(self.parts))))

        s_gw = [sem(f"ffn_gate_loaded{s}") for s in range(2)]
        s_uw = [sem(f"ffn_up_loaded{s}") for s in range(2)]
        s_dw = [sem(f"ffn_down_loaded{s}") for s in range(2)]
        s_gu = sem(f"ffn_gate_up_ready")
        s_silu = sem(f"ffn_silu_done")
        s_free = sem(f"ffn_gate_up_banks_free")
        s_down = sem(f"ffn_down_ready")
        s_dfree = sem(f"ffn_down_banks_free")

        def ffn(done, w_gate, w_up, w_down, norm_name):
            r = Region(after_x)
            hT = r(KT, T)
            aT = r(NF, T)
            gate_w = [r(KT, P) for _ in range(2)]
            up_w = [r(KT, P) for _ in range(2)]
            sq = aT[:, 0:KT, :]
            rms = aT[:, KT, :]
            nrm = Norm(xT, hT, sq, rms, norm_name, T)
            wg, wu, wd = panels(w_gate), panels(w_up), panels(w_down)
            sg = [r(T), r(T)]
            g0, w0, d0, dw0 = done * NF, done * NF // 2 * 16, done * KT, done * KT // 2 * 16
            dreg = Region(after_x)
            down_w = [dreg(NF, P), dreg(NF, P)]
            with nc.Block() as block:
                @block.sync
                def _(sp):
                    for s in range(2):
                        sp.dma_start(gate_w[s][:], wg[:, :, s * P:(s + 1) * P]).then_inc(s_gw[s], 16)
                        sp.dma_start(up_w[s][:], wu[:, :, s * P:(s + 1) * P]).then_inc(s_uw[s], 16)
                    with sp.Fori(1, NF // 2) as i:
                        for s in range(2):
                            sp.wait_ge(s_gu, i * 2 + (g0 + s - 1))
                            sp.dma_start(gate_w[s][:], wg[:, :, ds((i * 2 + s) * P, P)]).then_inc(s_gw[s], 16)
                            sp.dma_start(up_w[s][:], wu[:, :, ds((i * 2 + s) * P, P)]).then_inc(s_uw[s], 16)
                    sp.wait_ge(s_gu, g0 + NF)
                    for s in range(2):
                        sp.dma_start(down_w[s][:], wd[:, :, s * P:(s + 1) * P]).then_inc(s_dw[s], 16)
                    with sp.Fori(1, KT // 2) as i:
                        for s in range(2):
                            sp.wait_ge(s_down, i * 2 + (d0 + s - 1))
                            sp.dma_start(down_w[s][:], wd[:, :, ds((i * 2 + s) * P, P)]).then_inc(s_dw[s], 16)

                @block.tensor
                def _(pe):
                    nrm.pe(pe)
                    nrm.wait(pe)
                    with pe.Fori(0, NF // 2) as i:
                        for s in range(2):
                            pe.wait_ge(s_gw[s], i * 16 + (w0 + 16))
                            pe.wait_ge(s_uw[s], i * 16 + (w0 + 16))
                            pe.wait_ge(s_free, i * 2 + (g0 + s + 1))
                            for b, w in ((0, gate_w[s]), (2, up_w[s])):
                                for n in range(2):
                                    for kt in range(KT):
                                        last = nc.tensor.matmul(bank[:, 4 * s + b + n, :], w[:, kt],
                                                                hT[:, kt, n * HALF:(n + 1) * HALF],
                                                                start=kt == 0, stop=kt == KT - 1)
                            last.then_inc(s_gu, 1)
                    pe.wait_ge(s_free, 2 + g0 + NF)
                    with pe.Fori(0, KT // 2) as i:
                        for s in range(2):
                            pe.wait_ge(s_dw[s], i * 16 + (dw0 + 16))
                            pe.wait_ge(s_dfree, i * 2 + (d0 + s + 1))
                            for n in range(2):
                                for kt in range(NF):
                                    last = nc.tensor.matmul(bank[:, 2 * s + n, :], down_w[s][:, kt],
                                                            aT[:, kt, n * HALF:(n + 1) * HALF],
                                                            start=kt == 0, stop=kt == NF - 1)
                            last.then_inc(s_down, 1)

                @block.scalar
                def _(act):
                    nrm.act(act)
                    with act.Fori(0, NF // 2) as i:
                        for s in range(2):
                            act.wait_ge(s_gu, i * 2 + (g0 + s + 1))
                            act.wait_ge(s_free, i * 2 + (g0 + s + 1))
                            nc.scalar.activation(sg[s][:], bank[:, 4 * s:4 * s + 2, :].rearrange("p a b -> p (a b)"),
                                                 ACT.Silu).then_inc(s_silu, 1)

                @block.vector
                def _(dve):
                    if not done:
                        dve.sem_inc(s_free, 2)
                        dve.sem_inc(s_dfree, 2)
                    nrm.dve(dve)
                    nrm.wait(dve)
                    with dve.Fori(0, NF // 2) as i:
                        for s in range(2):
                            dve.wait_ge(s_silu, i * 2 + (g0 + s + 1))
                            nc.vector.tensor_tensor(aT[:, ds(i * 2 + s, 1), :].rearrange("p a b -> p (a b)"), sg[s][:],
                                                    bank[:, 4 * s + 2:4 * s + 4, :].rearrange("p a b -> p (a b)"),
                                                    ALU.mult).then_inc(s_free, 1)
                    with dve.Fori(0, KT // 2) as i:
                        for s in range(2):
                            dve.wait_ge(s_down, i * 2 + (d0 + s + 1))
                            xs = xT[:, ds(i * 2 + s, 1), :].rearrange("p a b -> p (a b)")
                            nc.vector.scalar_tensor_tensor(
                                out=xs, in0=bank[:, 2 * s:2 * s + 2, :].rearrange("p a b -> p (a b)"), scalar=0.5,
                                in1=xs, op0=ALU.mult, op1=ALU.add).then_inc(s_dfree, 1)
                    dve.wait_ge(s_dfree, 2 + d0 + KT)

        ffn(0, d["w_gate1"], d["w_up1"], d["w_down1"], "ffn1_norm")

        w_in = panels(d["w_in"])
        hT_at = after_x
        r = Region(hT_at)
        hT = r(KT, T)
        kd = r(2, CH + T)
        v_win = r(T // CH, P)
        uT = r(T)
        ugT = r(T)
        shared_end = r.at

        def shared():
            s = Region(shared_end)
            sq, rms = s(KT, T), s(T)
            nrm = Norm(xT, hT, sq, rms, "mix_norm", T)
            w = Region(s.at)
            panel = [w(KT, P) for _ in range(5)]
            vT = w(CH + T)
            raw = w(2, T + 1)
            diff = w(T)
            s_pan = [sem(f"shared_panel_loaded{j}") for j in range(5)]
            s_ready, s_stored = sem("shared_ready"), sem("shared_stored")
            s_pad = sem("pads_zeroed")
            s_vt, s_vw = sem("v_transposed"), sem("v_windows_stored")
            s_mix, s_u = sem("low_rank_shift"), sem("low_rank_inputs_done")
            s_spill = sem("x_spilled")
            with nc.Block() as block:
                @block.sync
                def _(sp):
                    for j, name in enumerate(["ak", "ak", "av", "u", "ug"]):
                        if name == "ak":
                            for e in range(2):
                                at = COLS[name] + j * CH
                                sp.dma_start(panel[j][:, :, e * CH:(e + 1) * CH],
                                             w_in[:, :, at:at + CH]).then_inc(s_pan[j], 16)
                        else:
                            sp.dma_start(panel[j][:], w_in[:, :, COLS[name]:COLS[name] + P]).then_inc(s_pan[j], 16)
                    sp.dma_start(x_spill[:, :], xT[:].rearrange("p a b -> p (a b)")).then_inc(s_spill, 16)
                    sp.wait_ge(s_spill, 16)

                @block.gpsimd
                def _(pool):
                    nc.gpsimd.memset(kd[:, :, 0:CH], 0.0).then_inc(s_pad, 1)
                    nc.gpsimd.memset(vT[:, 0:CH], 0.0).then_inc(s_pad, 1)
                    nc.gpsimd.memset(raw[:, :, 0:1], 0.0).then_inc(s_pad, 1)

                @block.tensor
                def _(pe):
                    nrm.pe(pe)
                    nrm.wait(pe)
                    for j in range(5):
                        pe.wait_ge(s_pan[j], 32 if j < 2 else 16)
                        if j >= 3:
                            pe.wait_ge(s_stored, j - 2)
                        for n in range(2):
                            for kt in range(KT):
                                last = nc.tensor.matmul(bank[:, 2 * (j % 3) + n, :], panel[j][:, kt],
                                                        hT[:, kt, n * HALF:(n + 1) * HALF],
                                                        start=kt == 0, stop=kt == KT - 1)
                        last.then_inc(s_ready, 1)
                    pe.wait_ge(s_pad, 3)
                    pe.wait_ge(s_stored, 5)
                    for g in range(4):
                        for j in range(4):
                            n = 4 * g + j
                            last = nc.tensor.transpose(bank[:, 4 + g, j * P:(j + 1) * P],
                                                       vT[:, n * CH:n * CH + P], c("ident"))
                        last.then_inc(s_vt, 1)

                @block.scalar
                def _(act):
                    nrm.act(act)
                    dst = [kd[:, 0, CH:], kd[:, 1, CH:], vT[:, CH:], raw[:, 0, 1:], raw[:, 1, 1:]]
                    for j in range(5):
                        act.wait_ge(s_ready, j + 1)
                        b = 2 * (j % 3)
                        nc.scalar.activation(dst[j], bank[:, b:b + 2, :].rearrange("p a b -> p (a b)"),
                                             ACT.Copy).then_inc(s_stored, 1)
                    act.wait_ge(s_mix, 2)
                    nc.scalar.activation(uT[0:CH, :], uT[0:CH, :], ACT.Tanh).then_inc(s_u, 1)
                    act.wait_ge(s_mix, 4)
                    nc.scalar.activation(ugT[:], ugT[:], ACT.Tanh, scale=0.5).then_inc(s_u, 1)

                @block.vector
                def _(dve):
                    nrm.dve(dve)
                    dve.wait_ge(s_pad, 3)
                    for j, dst in enumerate([uT, ugT]):
                        dve.wait_ge(s_stored, 4 + j)
                        nc.vector.tensor_sub(diff[:], raw[:, j, 0:T], raw[:, j, 1:T + 1]).then_inc(s_mix, 1)
                        dve.wait_ge(s_mix, 2 * j + 1)
                        nc.vector.scalar_tensor_tensor(out=dst[:], in0=diff[:], scalar=par_u[:, j:j + 1],
                                                       in1=raw[:, j, 1:T + 1], op0=ALU.mult,
                                                       op1=ALU.add).then_inc(s_mix, 1)
                        dve.wait_ge(s_mix, 2 * j + 2)
                    for g in range(4):
                        dve.wait_ge(s_vt, g + 1)
                        nc.vector.tensor_copy(v_win[:, 4 * g:4 * g + 4, :].rearrange("p a b -> p (a b)"),
                                              bank[:, 4 + g, :]).then_inc(s_vw, 1)
                    dve.wait_ge(s_vw, 4)
                    dve.wait_ge(s_u, 2)
                    nc.vector.tensor_scalar(ugT[:], ugT[:], 0.5, 0.5, ALU.mult, ALU.add).then_inc(s_u, 1)
                    dve.wait_ge(s_u, 3)

        shared()

        def mixer():
            a = Region(xT_at)
            lo_end = after_x
            panel = [a(KT, P) for _ in range(4)]
            qT, gaT, gbT = a(T), a(T), a(T)
            b_bd = a(NC, P)
            assert a.at <= lo_end
            a2 = Region(shared_end)
            k_bd, a_bd, v_bd = a2(NC, P), a2(NC, P), a2(NC, P)
            b_tok, k_tok, v_tok = a2(NC, P), a2(NC, P), a2(NC, P)
            lak_bd, nm_bd, x_bd, xt_bd, z_bd = a2(NC, P), a2(NC, P), a2(NC, P), a2(NC, P), a2(NC, P)
            zraw = a2(3, T + 1)
            lora = a2(3, P)
            ar = a2(NC, 2, CH)
            rm, km, vm, kp, g_out = a2(HALF), a2(HALF), a2(HALF), a2(HALF), a2(HALF)
            ld, cum, pin, pinv, pex = a2(HALF), a2(HALF), a2(HALF), a2(HALF), a2(HALF)
            kk, av, t1, t2 = a2(HALF), a2(HALF), a2(HALF), a2(HALF)
            b_st, v_st, mb, mk, n_st = a2(NC, CH), a2(NC, CH), a2(NC, CH), a2(NC, CH), a2(NC, CH)
            oa = a2(HALF)
            mrg = [a2(HALF) for _ in range(2)]
            alibi = a2(P)
            mx, es, den = a2(NC), a2(NC), a2(NC)
            pp, half_w0 = a2(NPAR), a2(2)
            s_st, s_tmp, p1, sa_st = a2(CH), a2(CH), a2(CH), a2(CH)
            sa_bd = a2(P)
            s_bd = [a2(P) for _ in range(2)]

            def by_chunk(t):
                return t.rearrange("p (a b) -> p a b", a=NC)

            xt_st, x_st, z_st = by_chunk(kk), by_chunk(av), by_chunk(pex)
            q_bd, o_bd, prob, prob_t = z_bd, xt_bd, ar[:].rearrange("p a b c -> p a (b c)"), b_tok

            sems = {}

            def S(name):
                if name not in sems:
                    sems[name] = sem(name)
                return sems[name]

            def pv(name):
                i = PAR.index(name)
                return pp[:, i:i + 1]

            def bd(t, e):
                return t[e * CH:(e + 1) * CH, :, e * CH:(e + 1) * CH]

            def bd1(t, e):
                return t[e * CH:(e + 1) * CH, e * CH:(e + 1) * CH]

            def hs(t, e):
                return t[e * CH:(e + 1) * CH]

            def over_chunks(m):
                return m.unsqueeze(1).broadcast_to([m.shape[0], NC, m.shape[1]])

            def flat(t):
                return t.rearrange("p a b -> p (a b)")

            def two(bk, n=P):
                return bank[:, bk:bk + 2, :].rearrange("p a (c b) -> p (a c) b", b=P)

            def one(bk):
                return bank[:, bk, :].rearrange("p (c b) -> p c b", b=CH)

            PROJ = ["k", "r", "v", "q", "ga", "gb"]
            s_slot = [sem(f"mix_panel_loaded{j}") for j in range(4)]
            s_lora = sem("lora_panels_loaded")
            s_zero = sem("mix_zeroed")
            s_mw = [sem(f"merged_written{h}") for h in range(2)]
            DVE_STEPS = 153

            with nc.Block() as block:
                @block.sync
                def _(sp):
                    def load(j, p):
                        sp.dma_start(panel[j % 4][:],
                                     w_in[:, :, COLS[PROJ[j]]:COLS[PROJ[j]] + D][:, :, ds(p * P, P)]).then_inc(s_slot[j % 4], 16)

                    def load_lora(p):
                        sp.dma_start(lora[0:CH, 0, :], d["w2"][:, ds(p * P, P)]).then_inc(s_lora, 16)
                        sp.dma_start(lora[CH:P, 1, :], d["a2"][:, ds(p * P, P)]).then_inc(s_lora, 16)
                        sp.dma_start(lora[:, 2, :], d["g2"][:, ds(p * P, P)]).then_inc(s_lora, 16)

                    def write_merged(p):
                        for h in range(2):
                            sp.wait_ge(S("merged_ready"), p * 2 + (h + 1))
                            sp.dma_start(m_spill[:, h * HALF:][:, ds(p * T, HALF)], mrg[h][:]).then_inc(s_mw[h], 16)

                    def second_use(p):
                        for j in (4, 5):
                            sp.wait_ge(S("proj_ready"), p * 6 + (j - 3))
                            load(j, p)

                    sp.wait_ge(s_zero, 1)
                    for j in range(4):
                        load(j, 0)
                    load_lora(0)
                    with sp.Fori(0, PAIRS - 1) as p:
                        following = sp.snap(p + 1)
                        second_use(p)
                        for j, used in ((3, 4), (2, 3), (0, 5), (1, 6)):
                            sp.wait_ge(S("proj_ready"), p * 6 + used)
                            load(j, following)
                        sp.wait_ge(S("lora_ready"), p * 2 + 2)
                        load_lora(following)
                        write_merged(p)
                    second_use(PAIRS - 1)
                    write_merged(PAIRS - 1)
                    for h in range(2):
                        sp.wait_ge(s_mw[h], 16 * PAIRS + 16)

                @block.gpsimd
                def _(pool):
                    nc.gpsimd.memset(lora[:], 0.0).then_inc(s_zero, 1)
                    nc.gpsimd.memset(zraw[:, :, 0:1], 0.0).then_inc(s_zero, 1)
                    for t in (b_bd, k_bd, a_bd, v_bd, lak_bd, nm_bd, x_bd, xt_bd, z_bd, sa_bd, s_bd[0], s_bd[1]):
                        nc.gpsimd.memset(t[:], 0.0).then_inc(s_zero, 1)
                    with pool.Fori(0, PAIRS) as p:
                        for h in range(2):
                            for n, m in enumerate(LEVELS):
                                if n == 0:
                                    pool.wait_ge(S("n_stored"), p * 2 + (h + 1))
                                else:
                                    pool.wait_ge(S("z_ready"), p * 10 + (h * 5 + n))
                                for e in range(2):
                                    last = nc.gpsimd.tensor_tensor(bd(nm_bd, e), hs(n_st, e),
                                                                   over_chunks(hs(c(f"join{m}"), e)), ALU.mult)
                                last.then_inc(S("nm_ready"), 1)

                @block.tensor
                def _(pe):
                    def per_chunk(out, lhs, rhs):
                        for n in range(NC):
                            last = nc.tensor.matmul(out[:, n, :], lhs[:, n, :], rhs(n), start=True, stop=True)
                        return last

                    pe.wait_ge(s_zero, 14)
                    with pe.Fori(0, PAIRS) as p:
                        g = p // 4
                        for j in range(6):
                            uses = 2 if j % 4 < 2 else 1
                            pe.wait_ge(s_slot[j % 4], (p * uses + (j // 4 + 1)) * 16)
                            pe.wait_ge(S("proj_stored"), p * 6 + (j + 1))
                            for n in range(2):
                                for kt in range(KT):
                                    last = nc.tensor.matmul(bank[:, 2 * (j % 2) + n, :], panel[j % 4][:, kt],
                                                            hT[:, kt, n * HALF:(n + 1) * HALF],
                                                            start=kt == 0, stop=kt == KT - 1)
                            last.then_inc(S("proj_ready"), 1)
                        for h in range(2):
                            tok = slice(h * HALF, (h + 1) * HALF)

                            def wait(name, k=1, j=1):
                                pe.wait_ge(S(name), p * (2 * k) + (h * k + j))

                            wait("q_bd_ready")
                            for n in range(NC):
                                w0 = (h * NC + n) * CH
                                last = nc.tensor.matmul(two(4)[:, n, :], q_bd[:, n, :],
                                                        flat(kd)[:, ds(g * (CH + T) + w0, P)], start=True, stop=True)
                            last.then_inc(S("att_scores_ready"), 1)
                            wait("att_exp_done")
                            for n in range(NC):
                                last = nc.tensor.transpose(two(6)[:, n, :], prob[:, n, :], c("ident"))
                            last.then_inc(S("probs_transposed"), 1)
                            wait("prob_t_stored")
                            for n in range(NC):
                                last = nc.tensor.matmul(one(4)[:, n, :], prob_t[:, n, :],
                                                        flat(v_win)[:, ds(g * CH + (h * NC + n) * P, CH)],
                                                        start=True, stop=True)
                            last.then_inc(S("att_out_ready"), 1)
                            wait("o_bd_ready")
                            per_chunk(one(5), o_bd, lambda n: c("stack_ident")).then_inc(S("att_outT_ready"), 1)

                            wait("kk_squared")
                            nc.tensor.matmul(bank[:, 6, :], c("bd_ones"), t1[:], start=True,
                                             stop=True).then_inc(S("kk_summed"), 1)
                            if h == 0:
                                pe.wait_ge(s_lora, (p + 1) * 48)
                            wait("oa_stored")
                            for n, src in enumerate((uT, uT, ugT)):
                                last = nc.tensor.matmul(bank[:, (7, 4, 5)[n], :], lora[:, n, :], src[:, tok],
                                                        start=True, stop=True)
                            last.then_inc(S("lora_ready"), 1)

                            wait("bd_ready")
                            for out_bank, src, name, before in ((4, b_bd, "b_tok_ready", None),
                                                                (6, k_bd, "k_tok_ready", None),
                                                                (4, v_bd, "v_tok_ready", "b_tok_stored")):
                                if before:
                                    wait(before)
                                for n in range(NC):
                                    last = nc.tensor.transpose(two(out_bank)[:, n, :], src[:, n, :], c("ident"))
                                last.then_inc(S(name), 1)
                            wait("k_tok_stored")
                            per_chunk(one(6), v_bd, lambda n: c("stack_ident")).then_inc(S("v_st_ready"), 1)
                            per_chunk(one(7), a_bd, lambda n: b_st[:, n, :]).then_inc(S("n_ready"), 1)
                            wait("v_tok_stored")
                            per_chunk(two(4), b_bd, lambda n: flat(ar[:, n])).then_inc(S("b_scores_ready"), 1)
                            wait("b_scores_stored")
                            per_chunk(two(4), k_bd, lambda n: flat(ar[:, n])).then_inc(S("k_scores_ready"), 1)

                            wait("k_scores_stored")
                            wait("v_st_stored")
                            for n in range(5):
                                wait("nm_ready", 5, n + 1)
                                wait("x_ready", 5, n + 1)
                                per_chunk(one(4), nm_bd, lambda i: xt_st[:, i, :]).then_inc(S("z_ready"), 1)
                                wait("z_stored", 5, n + 1)
                                per_chunk(one(5), x_bd, lambda i: z_st[:, i, :]).then_inc(S("xt_grown"), 1)
                                if n < 4:
                                    per_chunk(one(6), z_bd, lambda i: x_st[:, i, :]).then_inc(S("x_grown"), 1)

                            wait("xt_bd_ready")
                            for n in range(NC):
                                mm = nc.tensor.matmul
                                pe.wait_ge(S("state_ready"), p * 17 + (h * NC + n + 1))
                                mm(bank[:, 4, 0:CH], a_bd[:, n, :], s_st[:], start=True, stop=False)
                                mm(bank[:, 4, 0:CH], lak_bd[:, n, :], v_st[:, n, :], start=False,
                                   stop=True).then_inc(S("p1_ready"), 1)
                                wait("p1_stored", NC, n + 1)
                                mm(bank[:, 5, 0:CH], xt_bd[:, n, :], p1[:], start=True,
                                   stop=True).then_inc(S("sa_ready"), 1)
                                wait("sa_stored", NC, n + 1)
                                mm(bank[:, 6, 0:CH], b_tok[:, n, :], sa_st[:], start=True, stop=False)
                                mm(bank[:, 6, 0:CH], k_tok[:, n, :], v_st[:, n, :], start=False,
                                   stop=True).then_inc(S("state_sum_ready"), 1)
                                pe.wait_ge(S("s_bd_ready"), p * 17 + (h * NC + n + 1))
                                wait("sa_bd_stored", NC, n + 1)
                                mm(one(7)[:, n, :], sa_bd[:], mb[:, n, :], start=True, stop=False)
                                mm(one(7)[:, n, :], v_tok[:, n, :], mk[:, n, :], start=False, stop=False)
                                mm(one(7)[:, n, :], s_bd[n % 2][:], ar[:, n, 1, :], start=False,
                                   stop=True).then_inc(S("y_ready"), 1)

                            wait("y_stored")
                            nc.tensor.matmul(bank[:, 4, :], c("bd_ones"), ld[:], start=True,
                                             stop=True).then_inc(S("mean_ready"), 1)
                            wait("rk_ready")
                            nc.tensor.matmul(bank[:, 6, :], c("bd_ones"), t2[:], start=True,
                                             stop=True).then_inc(S("bonus_ready"), 1)
                            wait("yc_squared")
                            nc.tensor.matmul(bank[:, 5, :], c("bd_ones"), t1[:], start=True,
                                             stop=True).then_inc(S("var_ready"), 1)

                @block.scalar
                def _(act):
                    A = nc.scalar.activation
                    act.wait_ge(s_zero, 14)
                    with act.Fori(0, PAIRS) as p:
                        act.wait_ge(S("pair_done"), p + 1)
                        for j in range(6):
                            act.wait_ge(S("proj_ready"), p * 6 + (j + 1))
                            src = flat(bank[:, 2 * (j % 2):2 * (j % 2) + 2, :])
                            if j < 3:
                                i = A(zraw[:, j, 1:T + 1], src, ACT.Copy)
                            elif j == 3:
                                i = A(qT[:], src, ACT.Copy)
                            else:
                                i = A((gaT, gbT)[j - 4][:], src, ACT.Tanh, scale=0.5)
                            i.then_inc(S("proj_stored"), 1)
                        for h in range(2):
                            def wait(name, k=1, j=1):
                                act.wait_ge(S(name), p * (2 * k) + (h * k + j))

                            wait("att_shifted")
                            A(flat(prob), flat(prob), ACT.Exp).then_inc(S("att_exp_done"), 1)
                            A(es[:], mx[:], ACT.Exp, bias=pv("sink"), scale=-1.0).then_inc(S("sink_exp_done"), 1)
                            wait("probs_transposed")
                            A(flat(prob_t), flat(bank[:, 6:8, :]), ACT.Copy).then_inc(S("prob_t_stored"), 1)
                            wait("att_outT_ready")
                            A(oa[:], bank[:, 5, :], ACT.Copy).then_inc(S("oa_stored"), 1)

                            wait("lora_ready")
                            A(ld[:], bank[:, 7, :], ACT.Tanh, bias=half_w0[:, 0:1], scale=0.5)
                            A(av[:], bank[:, 4, :], ACT.Tanh, bias=half_w0[:, 1:2], scale=0.5)
                            A(g_out[:], bank[:, 5, :], ACT.Copy).then_inc(S("lora_stored"), 1)
                            wait("kk_summed")
                            A(flat(b_st), bank[:, 6, :], ACT.Sqrt).then_inc(S("kk_rooted"), 1)
                            wait("cum_ready")
                            A(pin[:], cum[:], ACT.Exp)
                            A(pinv[:], cum[:], ACT.Exp, scale=-1.0)
                            wait("cum_before_ready")
                            A(pex[:], t1[:], ACT.Exp).then_inc(S("exp_done"), 1)

                            wait("b_tok_ready")
                            A(flat(b_tok), flat(bank[:, 4:6, :]), ACT.Copy).then_inc(S("b_tok_stored"), 1)
                            wait("k_tok_ready")
                            A(flat(k_tok), flat(bank[:, 6:8, :]), ACT.Copy).then_inc(S("k_tok_stored"), 1)
                            wait("v_tok_ready")
                            A(flat(v_tok), flat(bank[:, 4:6, :]), ACT.Copy).then_inc(S("v_tok_stored"), 1)
                            wait("v_st_ready")
                            A(flat(v_st), bank[:, 6, :], ACT.Copy).then_inc(S("v_st_stored"), 1)

                            for n in range(NC):
                                wait("sa_stored", NC, n + 1)
                                if n > 0 or h > 0:
                                    wait("y_ready", NC, n)
                                for e in range(2):
                                    last = A(bd1(sa_bd, e), hs(sa_st, e), ACT.Copy)
                                last.then_inc(S("sa_bd_stored"), 1)
                                wait("state_added", NC, n + 1)
                                for e in range(2):
                                    last = A(bd1(s_bd[(n + 1) % 2], e), hs(s_tmp, e), ACT.Copy,
                                             scale=hs(pin, e)[:, n * CH + CH - 1:n * CH + CH])
                                last.then_inc(S("s_bd_ready"), 1)

                            wait("y_ready", NC, NC)
                            A(ld[:], bank[:, 7, :], ACT.Copy).then_inc(S("y_stored"), 1)
                            wait("var_ready")
                            A(pex[:], bank[:, 5, :], ACT.Sqrt, bias=eps[:, 1:2],
                              scale=1.0 / CH).then_inc(S("var_rooted"), 1)

                @block.vector
                def _(dve):
                    V = nc.vector
                    dve.sem_inc(S("proj_stored"), 2)
                    dve.sem_inc(S("pair_done"), 1)
                    for h in range(2):
                        dve.sem_inc(s_mw[h], 16)
                    dve.wait_ge(s_zero, 14)
                    with dve.Fori(0, PAIRS) as p:
                        step = [0]

                        def link(ins):
                            step[0] += 1
                            ins.then_inc(S("dve_step"), 1)
                            dve.wait_ge(S("dve_step"), p * DVE_STEPS + step[0])

                        link(V.tensor_copy(pp[:], par[:, :, ds(p, 1)].rearrange("p a b -> p (a b)")))
                        link(V.tensor_scalar(half_w0[:, 0:1], pv("w0"), 0.5, None, ALU.mult))
                        link(V.tensor_scalar(half_w0[:, 1:2], pv("a0"), 0.5, None, ALU.mult))
                        link(V.tensor_scalar(alibi[:], c("dist"), c("neg_slope")[:, ds(p, 1)], None, ALU.mult))
                        V.memset(s_st[:], 0.0).then_inc(S("state_ready"), 1)
                        for e in range(2):
                            last = V.memset(bd1(s_bd[0], e), 0.0)
                        last.then_inc(S("s_bd_ready"), 1)

                        for h in range(2):
                            def wait(name, k=1, j=1):
                                dve.wait_ge(S(name), p * (2 * k) + (h * k + j))

                            def both(f, name=None):
                                for e in range(2):
                                    last = f(e)
                                    if e == 0 or name is None:
                                        link(last)
                                    else:
                                        last.then_inc(S(name), 1)

                            tok = slice(h * HALF, (h + 1) * HALF)
                            if h == 0:
                                dve.wait_ge(S("proj_stored"), p * 6 + 8)
                            both(lambda e: V.tensor_copy(bd(q_bd, e), by_chunk(qT[:, tok])[e * CH:(e + 1) * CH]),
                                 "q_bd_ready")
                            wait("att_scores_ready")
                            link(V.scalar_tensor_tensor(out=prob, in0=two(4), scalar=0.125,
                                                        in1=over_chunks(alibi), op0=ALU.mult, op1=ALU.add))
                            if h == 0:
                                link(V.memset(prob[:, 0, 0:CH], -1e30))
                            link(V.tensor_reduce(mx[:], prob, AX.X, ALU.max))
                            link(V.tensor_scalar(mx[:], mx[:], pv("sink"), None, ALU.max))
                            V.tensor_tensor(prob, prob, mx.unsqueeze(2).broadcast_to([P, NC, P]),
                                            ALU.subtract).then_inc(S("att_shifted"), 1)
                            wait("att_exp_done")
                            link(V.tensor_reduce(den[:], prob, AX.X, ALU.add))
                            wait("sink_exp_done")
                            link(V.tensor_add(den[:], den[:], es[:]))
                            link(V.reciprocal(den[:], den[:]))
                            wait("att_out_ready")
                            both(lambda e: V.tensor_tensor(bd(o_bd, e), one(4)[e * CH:(e + 1) * CH],
                                                           hs(den, e).unsqueeze(2).broadcast_to([CH, NC, CH]),
                                                           ALU.mult), "o_bd_ready")

                            for j, (dst, name) in enumerate(((km, "mu_k"), (rm, "mu_r"), (vm, "mu_v"))):
                                cur = zraw[:, j, 1 + h * HALF:1 + (h + 1) * HALF]
                                prev = zraw[:, j, h * HALF:(h + 1) * HALF]
                                link(V.tensor_sub(t2[:], prev, cur))
                                link(V.scalar_tensor_tensor(out=dst[:], in0=t2[:], scalar=pv(name), in1=cur,
                                                            op0=ALU.mult, op1=ALU.add))
                                if j == 0:
                                    link(V.tensor_scalar(kk[:], km[:], pv("k_k"), None, ALU.mult))
                                    V.tensor_mul(t1[:], kk[:], kk[:]).then_inc(S("kk_squared"), 1)
                            wait("lora_stored")
                            link(V.tensor_scalar(ld[:], ld[:], C_DECAY, C_DECAY, ALU.mult, ALU.add))
                            V.tensor_tensor_scan(cum[:], c("keep"), ld[:], 0.0, ALU.mult,
                                                 ALU.add).then_inc(S("cum_ready"), 1)
                            wait("cum_ready")
                            wait("kk_rooted")
                            V.tensor_sub(t1[:], cum[:], ld[:]).then_inc(S("cum_before_ready"), 1)
                            link(V.tensor_scalar(av[:], av[:], 0.5, 0.5, ALU.mult, ALU.add))
                            link(V.tensor_scalar(t2[:], flat(b_st), 1e-12, None, ALU.max))
                            link(V.reciprocal(t2[:], t2[:]))
                            link(V.tensor_mul(kk[:], kk[:], t2[:]))
                            link(V.tensor_scalar(t2[:], av[:], 1.0, pv("k_a"), ALU.subtract, ALU.mult))
                            link(V.scalar_tensor_tensor(out=kp[:], in0=t2[:], scalar=1.0, in1=km[:], op0=ALU.add,
                                                        op1=ALU.mult))
                            link(V.tensor_mul(t2[:], kk[:], av[:]))
                            wait("exp_done")
                            link(V.tensor_mul(flat(b_st), t2[:], pinv[:]))
                            both(lambda e: V.tensor_copy(bd(b_bd, e), hs(b_st, e)))
                            both(lambda e: V.tensor_mul(bd(k_bd, e), hs(by_chunk(kp), e), hs(by_chunk(pinv), e)))
                            link(V.scalar_tensor_tensor(out=ar[:, :, 0, :], in0=by_chunk(kk), scalar=-1.0,
                                                        in1=by_chunk(pex), op0=ALU.mult, op1=ALU.mult))
                            link(V.tensor_mul(ar[:, :, 1, :], by_chunk(rm), by_chunk(pin)))
                            both(lambda e: V.tensor_copy(bd(a_bd, e), hs(ar, e)[:, :, 0, :]))
                            both(lambda e: V.tensor_copy(bd(v_bd, e), hs(by_chunk(vm), e)), "bd_ready")

                            ident8 = over_chunks(c("stack_ident"))
                            wait("n_ready")
                            link(V.tensor_tensor(n_st, one(7), over_chunks(c("col_before_row")), ALU.mult))
                            link(V.tensor_tensor(x_st, n_st, over_chunks(c("join1")), ALU.mult))
                            V.tensor_tensor(x_st, x_st, ident8, ALU.add).then_inc(S("n_stored"), 1)
                            wait("n_stored")
                            both(lambda e: V.tensor_copy(bd(x_bd, e), hs(x_st, e)))
                            wait("b_scores_ready")
                            link(V.tensor_tensor(xt_st, two(4)[:, :, 0:CH], over_chunks(c("join1T")), ALU.mult))
                            link(V.tensor_tensor(xt_st, xt_st, ident8, ALU.add))
                            V.tensor_tensor(mb, two(4)[:, :, CH:P], over_chunks(c("row_upto_col")),
                                            ALU.mult).then_inc(S("b_scores_stored"), 1)
                            wait("b_scores_stored")
                            wait("k_scores_ready")
                            both(lambda e: V.tensor_tensor(bd(lak_bd, e), hs(two(4), e)[:, :, 0:CH],
                                                           over_chunks(hs(c("row_before_col"), e)), ALU.mult))
                            V.tensor_tensor(mk, two(4)[:, :, CH:P], over_chunks(c("row_upto_col")),
                                            ALU.mult).then_inc(S("k_scores_stored"), 1)
                            wait("k_scores_stored")
                            dve.sem_inc(S("x_ready"), 1)
                            for n in range(5):
                                wait("z_ready", 5, n + 1)
                                link(V.tensor_copy(z_st, one(4)))
                                both(lambda e: V.tensor_copy(bd(z_bd, e), hs(z_st, e)), "z_stored")
                                wait("xt_grown", 5, n + 1)
                                if n == 4:
                                    both(lambda e: V.tensor_tensor(bd(xt_bd, e), hs(one(5), e), hs(xt_st, e),
                                                                   ALU.add), "xt_bd_ready")
                                    break
                                link(V.tensor_tensor(xt_st, one(5), xt_st, ALU.add))
                                wait("x_grown", 4, n + 1)
                                link(V.tensor_tensor(x_st, one(6), x_st, ALU.add))
                                both(lambda e: V.tensor_copy(bd(x_bd, e), hs(x_st, e)), "x_ready")

                            V.scalar_tensor_tensor(out=t2[:], in0=rm[:], scalar=pv("r_k"), in1=kp[:], op0=ALU.mult,
                                                   op1=ALU.mult).then_inc(S("rk_ready"), 1)
                            for n in range(NC):
                                wait("p1_ready", NC, n + 1)
                                V.tensor_copy(p1[:], bank[:, 4, 0:CH]).then_inc(S("p1_stored"), 1)
                                wait("sa_ready", NC, n + 1)
                                if n > 0 or h > 0:
                                    wait("sa_bd_stored", NC, n)
                                V.tensor_copy(sa_st[:], bank[:, 5, 0:CH]).then_inc(S("sa_stored"), 1)
                                wait("state_sum_ready", NC, n + 1)
                                if n > 0 or h > 0:
                                    dve.wait_ge(S("s_bd_ready"), p * 17 + (h * NC + n + 1))
                                V.tensor_tensor(s_tmp[:], bank[:, 6, 0:CH], s_st[:],
                                                ALU.add).then_inc(S("state_added"), 1)
                                wait("state_added", NC, n + 1)
                                V.tensor_scalar(s_st[:], s_tmp[:], pin[:, n * CH + CH - 1:n * CH + CH], None,
                                                ALU.mult).then_inc(S("state_ready"), 1)

                            wait("mean_ready")
                            link(V.scalar_tensor_tensor(out=cum[:], in0=bank[:, 4, :], scalar=-1.0 / CH, in1=ld[:],
                                                        op0=ALU.mult, op1=ALU.add))
                            V.tensor_mul(t1[:], cum[:], cum[:]).then_inc(S("yc_squared"), 1)
                            wait("bonus_ready")
                            link(V.tensor_tensor(vm[:], bank[:, 6, :], vm[:], ALU.mult))
                            wait("var_rooted")
                            link(V.reciprocal(pex[:], pex[:]))
                            link(V.tensor_mul(cum[:], cum[:], pex[:]))
                            link(V.tensor_scalar(cum[:], cum[:], pv("ln_w"), pv("ln_b"), ALU.mult, ALU.add))
                            link(V.tensor_add(cum[:], cum[:], vm[:]))
                            link(V.tensor_mul(cum[:], cum[:], g_out[:]))
                            if h == 0:
                                dve.wait_ge(S("proj_stored"), p * 6 + 8)
                            link(V.scalar_tensor_tensor(out=cum[:], in0=gbT[:, tok], scalar=1.0, in1=cum[:],
                                                        op0=ALU.add, op1=ALU.mult))
                            link(V.scalar_tensor_tensor(out=oa[:], in0=gaT[:, tok], scalar=1.0, in1=oa[:],
                                                        op0=ALU.add, op1=ALU.mult))
                            link(V.tensor_add(cum[:], cum[:], oa[:]))
                            dve.wait_ge(s_mw[h], p * 16 + 16)
                            V.tensor_scalar(mrg[h][:], cum[:], 0.5, None, ALU.mult).then_inc(S("merged_ready"), 1)
                            wait("merged_ready")
                        dve.sem_inc(S("pair_done"), 1)
                        assert step[0] == DVE_STEPS

        mixer()

        def finish():
            r = Region(after_x)
            yT, sq, rms, rows = r(KT, T), r(KT, T), r(T), r(8, D)
            nrm = Norm(xT, yT, sq, rms, "final_norm", T)
            s_tr, s_ev, s_out = sem("out_transposed"), sem("out_rows_ready"), sem("out_written")
            with nc.Block() as block:
                @block.sync
                def _(sp):
                    for t in range(8):
                        sp.wait_ge(s_ev, 2 * t + 2)
                        sp.dma_start(out[t * P:(t + 1) * P, :], rows[:, t, :]).then_inc(s_out, 16)
                    sp.wait_ge(s_out, 128)

                @block.scalar
                def _(act):
                    nrm.act(act)

                @block.tensor
                def _(pe):
                    nrm.pe(pe)
                    nrm.wait(pe)
                    for g in range(16):
                        if g >= 6:
                            pe.wait_ge(s_ev, g - 5)
                        for j in range(4):
                            kt = 4 * (g % 2) + j
                            last = nc.tensor.transpose(bank[:, g % 6, j * P:(j + 1) * P],
                                                       yT[:, kt, (g // 2) * P:(g // 2 + 1) * P], c("ident"))
                        last.then_inc(s_tr, 1)

                @block.vector
                def _(dve):
                    nrm.dve(dve)
                    for g in range(16):
                        dve.wait_ge(s_tr, g + 1)
                        nc.vector.tensor_copy(rows[:, g // 2, (g % 2) * HALF:(g % 2 + 1) * HALF],
                                              bank[:, g % 6, :]).then_inc(s_ev, 1)
        s_re = sem("project_reloaded")
        s_pan = [sem(f"project_panel_loaded{s}") for s in range(4)]
        s_ready, s_free_banks = sem("project_ready"), sem("project_added")

        def project(done, w, srcT, reload):
            r = Region(after_x + KT * T * (1 if reload else 2))
            slot = [r(KT, P) for _ in range(4)]
            wp = panels(w)
            o0, p0 = done * KT, done * 32
            with nc.Block() as block:
                @block.sync
                def _(sp):
                    if reload:
                        sp.dma_start(srcT[:].rearrange("p a b -> p (a b)"), m_spill[:, :]).then_inc(s_re, 16)
                        sp.dma_start(xT[:].rearrange("p a b -> p (a b)"), x_spill[:, :]).then_inc(s_re, 16)
                    for s in range(4):
                        sp.dma_start(slot[s][:], wp[:, :, s * P:(s + 1) * P]).then_inc(s_pan[s], 16)
                    for s in range(4):
                        sp.wait_ge(s_ready, o0 + s + 1)
                        sp.dma_start(slot[s][:], wp[:, :, (4 + s) * P:(5 + s) * P]).then_inc(s_pan[s], 16)

                @block.tensor
                def _(pe):
                    if reload:
                        pe.wait_ge(s_re, 32)
                    for o in range(KT):
                        pe.wait_ge(s_pan[o % 4], p0 + 16 * (o // 4 + 1))
                        if o >= 4:
                            pe.wait_ge(s_free_banks, o0 + o - 3)
                        for n in range(2):
                            for kt in range(KT):
                                last = nc.tensor.matmul(bank[:, 2 * (o % 4) + n, :], slot[o % 4][:, kt],
                                                        srcT[:, kt, n * HALF:(n + 1) * HALF],
                                                        start=kt == 0, stop=kt == KT - 1)
                        last.then_inc(s_ready, 1)

                @block.vector
                def _(dve):
                    if reload:
                        dve.wait_ge(s_re, 32)
                    for o in range(KT):
                        dve.wait_ge(s_ready, o0 + o + 1)
                        nc.vector.tensor_tensor(
                            xT[:, o, :], bank[:, 2 * (o % 4):2 * (o % 4) + 2, :].rearrange("p a b -> p (a b)"),
                            xT[:, o, :], ALU.add).then_inc(s_free_banks, 1)
                    dve.wait_ge(s_free_banks, o0 + KT)

        project(0, d["w_out"], hT, True)

        def cross():
            r = Region(after_x)
            hx, oT = r(KT, T), r(KT, T)
            memT, rms_m = r(KT, NMEM), r(NMEM)
            after = r.at
            r1 = Region(after)
            sq, rms, mem_rows, sq_m = r1(KT, T), r1(T), r1(MT, D), r1(KT, NMEM)
            r2 = Region(after)
            q_w, k_w, v_w = r2(2, KT, P), r2(2, KT, P), r2(KT, NMEM)
            qh, kh, vh = r2(2, T), r2(2, NMEM), r2(MT, 2 * P)
            prob, prob_t = r2(8, NMEM), r2(MT, T)
            mx, den = r2(8), r2(8)
            nx = Norm(xT, hx, sq, rms, "cross_norm", T)
            nm = Norm(memT, memT, sq_m, rms_m, "mem_norm", NMEM)
            s_in, s_tr, s_ev = sem("mem_loaded"), sem("mem_transposed"), sem("mem_stored")

            def flat(t):
                return t.rearrange("p a b -> p (a b)")

            with nc.Block() as block:
                @block.sync
                def _(sp):
                    sp.dma_start(mem_rows[:], d["mem"].rearrange("(t p) c -> p t c", p=P)).then_inc(s_in, 16)

                @block.tensor
                def _(pe):
                    pe.wait_ge(s_in, 16)
                    for g in range(4):
                        for j in range(4):
                            kt = 2 * g + j // 2
                            last = nc.tensor.transpose(bank[:, g, j * P:(j + 1) * P],
                                                       mem_rows[:, j % 2, kt * P:(kt + 1) * P], c("ident"))
                        last.then_inc(s_tr, 1)
                    nx.pe(pe)
                    pe.wait_ge(nx.rooted, nx.p0 + 2)
                    nm.pe(pe)

                @block.scalar
                def _(act):
                    nx.act(act)
                    act.wait_ge(s_ev, 4)
                    nm.act(act)

                @block.vector
                def _(dve):
                    for g in range(4):
                        dve.wait_ge(s_tr, g + 1)
                        nc.vector.tensor_copy(flat(memT[:, 2 * g:2 * g + 2, :]), bank[:, g, :]).then_inc(s_ev, 1)
                    nx.dve(dve)
                    nm.dve(dve)
                    nm.wait(dve)
                    nx.wait(dve)

            s_w = [sem(f"cross_{n}_weights_loaded") for n in "qkv"]
            s_q, s_k, s_v = sem("cross_q_ready"), sem("cross_k_ready"), sem("cross_v_ready")
            s_qs, s_kvs = sem("cross_q_stored"), sem("cross_kv_stored")
            s_sc, s_sh, s_exp, s_norm = sem("cross_scores"), sem("cross_shifted"), sem("cross_exp"), sem("cross_probs")
            s_pt, s_pts, s_o, s_os = (sem("cross_probs_transposed"), sem("cross_probs_t_stored"), sem("cross_out"),
                                      sem("cross_out_stored"))
            s_step = sem("cross_dve_step")
            with nc.Block() as block:
                wq, wkv = panels(d["w_cq"]), panels(d["w_ckv"])

                @block.sync
                def _(sp):
                    def load_q(i):
                        for t in range(2):
                            sp.dma_start(q_w[:, t], wq[:, :, t * P:][:, :, ds(i * NMEM, P)]).then_inc(s_w[0], 16)

                    def load_k(i):
                        for t in range(2):
                            sp.dma_start(k_w[:, t], wkv[:, :, t * P:][:, :, ds(i * NMEM, P)]).then_inc(s_w[1], 16)

                    def load_v(i):
                        sp.dma_start(v_w[:], wkv[:, :, D:][:, :, ds(i * NMEM, NMEM)]).then_inc(s_w[2], 16)

                    load_k(0)
                    load_v(0)
                    load_q(0)
                    with sp.Fori(1, XH) as i:
                        sp.wait_ge(s_k, i)
                        load_k(i)
                        sp.wait_ge(s_v, i)
                        load_v(i)
                        sp.wait_ge(s_q, i * 2)
                        load_q(i)

                @block.tensor
                def _(pe):
                    mm = nc.tensor.matmul
                    with pe.Fori(0, XH) as i:
                        pe.wait_ge(s_os, i * 2 + 2)
                        pe.wait_ge(s_w[1], i * 32 + 32)
                        for t in range(2):
                            for kt in range(KT):
                                last = mm(bank[:, 4 + t, 0:NMEM], k_w[:, t, kt], memT[:, kt, :], start=kt == 0,
                                          stop=kt == KT - 1)
                        last.then_inc(s_k, 1)
                        pe.wait_ge(s_w[2], i * 16 + 16)
                        for t in range(MT):
                            for kt in range(KT):
                                last = mm(bank[:, 6 + t, 0:NMEM], memT[:, kt, t * P:(t + 1) * P], v_w[:, kt, :],
                                          start=kt == 0, stop=kt == KT - 1)
                        last.then_inc(s_v, 1)
                        pe.wait_ge(s_w[0], i * 32 + 32)
                        for t in range(2):
                            for n in range(2):
                                for kt in range(KT):
                                    last = mm(bank[:, 2 * t + n, :], q_w[:, t, kt], hx[:, kt, n * HALF:(n + 1) * HALF],
                                              start=kt == 0, stop=kt == KT - 1)
                            last.then_inc(s_q, 1)
                        pe.wait_ge(s_kvs, i * 2 + 2)
                        pe.wait_ge(s_qs, i * 2 + 2)
                        for t in range(8):
                            for k in range(2):
                                last = mm(bank[:, t // 2, (t % 2) * NMEM:(t % 2 + 1) * NMEM],
                                          qh[:, k, t * P:(t + 1) * P], kh[:, k, :], start=k == 0, stop=k == 1)
                        last.then_inc(s_sc, 1)
                        pe.wait_ge(s_norm, i + 1)
                        for m in range(MT):
                            for t in range(8):
                                last = nc.tensor.transpose(bank[:, 4 + 2 * m + t // 4, (t % 4) * P:(t % 4 + 1) * P],
                                                           prob[:, t, m * P:(m + 1) * P], c("ident"))
                            last.then_inc(s_pt, 1)
                        pe.wait_ge(s_pts, i * 2 + 2)
                        for t in range(2):
                            for n in range(2):
                                for m in range(MT):
                                    last = mm(bank[:, 2 * t + n, :], vh[:, m, t * P:(t + 1) * P],
                                              prob_t[:, m, n * HALF:(n + 1) * HALF], start=m == 0, stop=m == MT - 1)
                            last.then_inc(s_o, 1)

                @block.scalar
                def _(act):
                    A = nc.scalar.activation
                    with act.Fori(0, XH) as i:
                        act.wait_ge(s_k, i + 1)
                        A(kh[:], bank[:, 4:6, 0:NMEM], ACT.Copy).then_inc(s_kvs, 1)
                        act.wait_ge(s_v, i + 1)
                        A(vh[:], bank[:, 6:8, 0:NMEM], ACT.Copy).then_inc(s_kvs, 1)
                        for t in range(2):
                            act.wait_ge(s_q, i * 2 + (t + 1))
                            A(qh[:, t, :], flat(bank[:, 2 * t:2 * t + 2, :]), ACT.Copy).then_inc(s_qs, 1)
                        act.wait_ge(s_sh, i + 1)
                        A(flat(prob), flat(prob), ACT.Exp, scale=1.0 / 16).then_inc(s_exp, 1)
                        for m in range(MT):
                            act.wait_ge(s_pt, i * 2 + (m + 1))
                            A(prob_t[:, m, :], flat(bank[:, 4 + 2 * m:6 + 2 * m, :]), ACT.Copy).then_inc(s_pts, 1)

                @block.vector
                def _(dve):
                    V = nc.vector
                    dve.sem_inc(s_os, 2)
                    with dve.Fori(0, XH) as i:
                        step = [0]

                        def link(ins):
                            step[0] += 1
                            ins.then_inc(s_step, 1)
                            dve.wait_ge(s_step, i * 3 + step[0])

                        dve.wait_ge(s_sc, i + 1)
                        sc = bank[:, 0:4, :].rearrange("p a (b c) -> p (a b) c", c=NMEM)
                        link(V.tensor_reduce(mx[:], sc, AX.X, ALU.max))
                        V.tensor_tensor(prob[:], sc, mx[:].unsqueeze(2).broadcast_to([P, 8, NMEM]),
                                        ALU.subtract).then_inc(s_sh, 1)
                        dve.wait_ge(s_exp, i + 1)
                        link(V.tensor_reduce(den[:], prob[:], AX.X, ALU.add))
                        link(V.reciprocal(den[:], den[:]))
                        V.tensor_tensor(prob[:], prob[:], den[:].unsqueeze(2).broadcast_to([P, 8, NMEM]),
                                        ALU.mult).then_inc(s_norm, 1)
                        for t in range(2):
                            dve.wait_ge(s_o, i * 2 + (t + 1))
                            V.tensor_scalar(flat(oT[:, ds(i * 2 + t, 1), :]), flat(bank[:, 2 * t:2 * t + 2, :]), 1.0,
                                            None, ALU.mult).then_inc(s_os, 1)
                    dve.wait_ge(s_os, 2 * XH + 2)
            project(1, d["w_co"], oT, False)

        cross()
        ffn(1, d["w_gate2"], d["w_up2"], d["w_down2"], "ffn2_norm")

        finish()


def kernel(**inputs):
    import concourse.bacc as _bacc
    from concourse.bass_utils import run_bass_kernel_spmd as _run

    def col(v):
        return np.ascontiguousarray(np.reshape(v, (-1, P)).T)

    g = {k: np.asarray(v) for k, v in inputs.items()}
    mu = g["rwkv_mu"][0]
    vec = {"ffn1_norm": g["ffn1_norm"][0], "mix_norm": g["mix_norm"][0], "cross_norm": g["cross_norm"][0],
           "mem_norm": g["mem_norm"][0], "ffn2_norm": g["ffn2_norm"][0], "final_norm": g["final_norm"],
           "mu_r": mu[0:D], "mu_k": mu[D:2 * D], "mu_v": mu[2 * D:3 * D], "w0": g["rwkv_w0"][0],
           "a0": g["rwkv_a0"][0], "k_k": g["rwkv_k_k"][0], "k_a": g["rwkv_k_a"][0],
           "r_k": np.reshape(g["rwkv_r_k"][0], (-1,)), "ln_w": g["rwkv_ln_w"][0], "ln_b": g["rwkv_ln_b"][0],
           "sink": np.repeat(g["attn_sinks"][0], CH)}
    arrays = {
        "x": g["x"][0], "mem": g["mem"][0], "consts": constants()[0],
        "params": np.concatenate([col(vec[n]) for n in PAR], 1),
        "params_u": col(mu[3 * D:3 * D + 2 * P]),
        "w_gate1": g["ffn1_w_gate"][0], "w_up1": g["ffn1_w_up"][0], "w_down1": g["ffn1_w_down"][0],
        "w_in": g["w_in"][0], "w2": g["rwkv_w2"][0], "a2": g["rwkv_a2"][0], "g2": g["rwkv_g2"][0],
        "w_out": g["w_out"][0], "w_cq": g["w_cq"][0], "w_ckv": g["w_ckv"][0], "w_co": g["w_co"][0],
        "w_gate2": g["ffn2_w_gate"][0], "w_up2": g["ffn2_w_up"][0], "w_down2": g["ffn2_w_down"][0],
    }
    arrays = {k: np.ascontiguousarray(v) for k, v in arrays.items()}
    nc = _bacc.Bacc("TRN2", target_bir_lowering=False, num_devices=1)
    d = {n: nc.dram_tensor(n, v.shape, mybir.dt.from_np(v.dtype), kind="ExternalInput").ap()
         for n, v in arrays.items()}
    out = nc.dram_tensor("out", (T, D), F32, kind="ExternalOutput").ap()
    x_spill = nc.dram_tensor("x_spill", (P, KT * T), F32, kind="Internal").ap()
    m_spill = nc.dram_tensor("m_spill", (P, KT * T), F32, kind="Internal").ap()
    build(nc, d, out, x_spill, m_spill)
    r = _run(nc, [arrays], core_ids=[0])
    return r.results[0]["out"].reshape(1, T, D)
```

```python
import concourse.bass as bass
from concourse import mybir
from contextlib import ExitStack
import numpy as np

F32 = mybir.dt.float32
ACT = mybir.ActivationFunctionType
ALU = mybir.AluOpType
AX = mybir.AxisListType
ds = bass.ds

P = 128
SBUF_WORDS = 53000
D = 1024
KT = D // P
T = 1024
HALF = 512
NF = 2816 // P
CH = 64
NC = HALF // CH
PAIRS = 8
NMEM = 256
MT = NMEM // P
XH = 4
RMS_EPS = 1e-6
GN_EPS = 64e-5
LEVELS = [2, 4, 8, 16, 32]
C_DECAY = -0.5 * float(np.exp(-0.5))

PAR = ["ffn1_norm", "mix_norm", "cross_norm", "mem_norm", "ffn2_norm", "final_norm", "mu_r", "mu_k", "mu_v",
       "w0", "a0", "k_k", "k_a", "r_k", "ln_w", "ln_b", "sink"]
NPAR = len(PAR)
COLS = {"q": 0, "ak": 1024, "av": 1152, "r": 1280, "k": 2304, "v": 3328, "u": 4352, "ug": 4480, "ga": 4608,
        "gb": 5632}


def constants():
    row, col = np.arange(P)[:, None], np.arange(P)[None, :]
    i, j = row % CH, np.arange(CH)[None, :]
    parts = {"ident": row == col, "stack_ident": i == j, "bd_ones": row // CH == col // CH,
             "ones": np.ones((P, P)), "dist": np.abs(i + CH - col),
             "neg_slope": -2.0 ** (-8.0 * (2 * np.arange(PAIRS)[None, :] + row // CH + 1) / 16),
             "row_before_col": i < j, "row_upto_col": i <= j, "col_before_row": j < i,
             "keep": np.ones((P, 1)) * (np.arange(HALF)[None, :] % CH != 0)}

    def joins(m, a, b):
        return (a // (2 * m) == b // (2 * m)) & ((a // m) % 2 == 1) & ((b // m) % 2 == 0)

    parts["join1"] = joins(1, i, j)
    parts["join1T"] = joins(1, j, i)
    for m in LEVELS:
        parts[f"join{m}"] = joins(m, i, j)
    where, at = {}, 0
    for name, a in parts.items():
        where[name] = (at, a.shape[1])
        at += a.shape[1]
    return np.concatenate([np.asarray(a, np.float32) for a in parts.values()], 1), where


def build(nc, d, out, x_spill, m_spill):
    table, where = constants()
    ctx = ExitStack()
    with ctx:
        def sem(name):
            return ctx.enter_context(nc.semaphore(name))

        arena = ctx.enter_context(nc.sbuf_tensor("arena", [P, SBUF_WORDS], F32))
        bank = ctx.enter_context(nc.psum_tensor("bank", [P, 8, 512], F32))

        class Region:

            def __init__(self, at):
                self.at = at

            def __call__(self, *dims):
                n = int(np.prod(dims))
                v = arena[:, self.at:self.at + n]
                self.at += n
                assert self.at <= SBUF_WORDS, self.at
                if len(dims) == 2:
                    v = v.rearrange("p (a b) -> p a b", a=dims[0])
                elif len(dims) == 3:
                    v = v.rearrange("p (a b c) -> p a b c", a=dims[0], b=dims[1])
                return v

        keep = Region(0)
        cst = keep(table.shape[1])
        par = keep(NPAR, KT)
        par_u = keep(2)
        eps = keep(2)
        phase_base = keep.at
        xT_at = phase_base
        xT = keep(KT, T)
        after_x = keep.at

        def c(name):
            at, n = where[name]
            return cst[:, at:at + n]

        def gain(name, kt):
            return par[:, PAR.index(name), kt:kt + 1]

        def panels(w, rows=KT):
            return w.rearrange("(k p) n -> p k n", p=P)

        io = Region(after_x)
        x_rows = io(8, D)
        s_cst, s_xin, s_x_tr, s_x_ev = sem("consts_loaded"), sem("rows_loaded"), sem("x_transposed"), sem("x_stored")
        s_eps = sem("eps_set")
        with nc.Block() as block:
            @block.sync
            def _(sp):
                sp.dma_start(cst[:], d["consts"][:, :]).then_inc(s_cst, 16)
                sp.dma_start(par[:], d["params"].rearrange("p (a b) -> p a b", a=NPAR)).then_inc(s_cst, 16)
                sp.dma_start(par_u[:], d["params_u"][:, :]).then_inc(s_cst, 16)
                sp.dma_start(x_rows[:], d["x"].rearrange("(t p) c -> p t c", p=P)).then_inc(s_xin, 16)

            @block.gpsimd
            def _(pool):
                nc.gpsimd.memset(eps[:, 0:1], RMS_EPS).then_inc(s_eps, 1)
                nc.gpsimd.memset(eps[:, 1:2], GN_EPS).then_inc(s_eps, 1)

            @block.tensor
            def _(pe):
                pe.wait_ge(s_cst, 48)
                pe.wait_ge(s_xin, 16)
                for g in range(16):
                    if g >= 8:
                        pe.wait_ge(s_x_ev, g - 7)
                    for j in range(4):
                        last = nc.tensor.transpose(bank[:, g % 8, j * P:(j + 1) * P],
                                                   x_rows[:, 4 * (g % 2) + j, (g // 2) * P:(g // 2 + 1) * P],
                                                   c("ident"))
                    last.then_inc(s_x_tr, 1)

            @block.vector
            def _(dve):
                for g in range(16):
                    dve.wait_ge(s_x_tr, g + 1)
                    nc.vector.tensor_copy(xT[:, g // 2, (g % 2) * HALF:(g % 2 + 1) * HALF],
                                          bank[:, g % 8, :]).then_inc(s_x_ev, 1)
                dve.wait_ge(s_x_ev, 16)
                dve.wait_ge(s_eps, 2)

        class Norm:

            squared, summed, rooted = sem("norm_squared"), sem("norm_summed"), sem("norm_rooted")
            inverted, done = sem("norm_inverted"), sem("norm_done")
            uses, parts_before = 0, 0

            def __init__(self, src, dst, sq, rms, name, width):
                self.src, self.dst, self.sq, self.rms, self.name, self.width = src, dst, sq, rms, name, width
                self.parts = [(a, min(HALF, width - a)) for a in range(0, width, HALF)]
                self.n0, self.p0 = Norm.uses, Norm.parts_before
                Norm.uses += 1
                Norm.parts_before += len(self.parts)

            def act(self, act):
                for kt in range(KT):
                    nc.scalar.activation(self.sq[:, kt], self.src[:, kt], ACT.Square).then_inc(self.squared, 1)
                for n, (a, w) in enumerate(self.parts):
                    act.wait_ge(self.summed, self.p0 + n + 1)
                    nc.scalar.activation(self.rms[:, a:a + w], bank[:, 6 + n, 0:w], ACT.Sqrt, bias=eps[:, 0:1],
                                         scale=1.0 / D).then_inc(self.rooted, 1)

            def pe(self, pe):
                pe.wait_ge(self.squared, KT * (self.n0 + 1))
                for n, (a, w) in enumerate(self.parts):
                    for kt in range(KT):
                        last = nc.tensor.matmul(bank[:, 6 + n, 0:w], c("ones"), self.sq[:, kt, a:a + w],
                                                start=kt == 0, stop=kt == KT - 1)
                    last.then_inc(self.summed, 1)

            def dve(self, dve):
                for n, (a, w) in enumerate(self.parts):
                    dve.wait_ge(self.rooted, self.p0 + n + 1)
                    nc.vector.reciprocal(self.rms[:, a:a + w], self.rms[:, a:a + w]).then_inc(self.inverted, 1)
                    dve.wait_ge(self.inverted, self.p0 + n + 1)
                    for kt in range(KT):
                        nc.vector.scalar_tensor_tensor(
                            out=self.dst[:, kt, a:a + w], in0=self.src[:, kt, a:a + w], scalar=gain(self.name, kt),
                            in1=self.rms[:, a:a + w], op0=ALU.mult, op1=ALU.mult).then_inc(self.done, 1)

            def wait(self, eng, part=1):
                eng.wait_ge(self.done, KT * (self.p0 + min(part + 1, len(self.parts))))

        s_gw = [sem(f"ffn_gate_loaded{s}") for s in range(2)]
        s_uw = [sem(f"ffn_up_loaded{s}") for s in range(2)]
        s_dw = [sem(f"ffn_down_loaded{s}") for s in range(2)]
        s_gu = sem(f"ffn_gate_up_ready")
        s_silu = sem(f"ffn_silu_done")
        s_free = sem(f"ffn_gate_up_banks_free")
        s_down = sem(f"ffn_down_ready")
        s_dfree = sem(f"ffn_down_banks_free")

        def ffn(done, w_gate, w_up, w_down, norm_name):
            r = Region(after_x)
            hT = r(KT, T)
            aT = r(NF, T)
            gate_w = [r(KT, P) for _ in range(2)]
            up_w = [r(KT, P) for _ in range(2)]
            sq = aT[:, 0:KT, :]
            rms = aT[:, KT, :]
            nrm = Norm(xT, hT, sq, rms, norm_name, T)
            wg, wu, wd = panels(w_gate), panels(w_up), panels(w_down)
            sg = [r(T), r(T)]
            g0, w0, d0, dw0 = done * NF, done * NF // 2 * 16, done * KT, done * KT // 2 * 16
            dreg = Region(after_x)
            down_w = [dreg(NF, P), dreg(NF, P)]
            with nc.Block() as block:
                @block.sync
                def _(sp):
                    for s in range(2):
                        sp.dma_start(gate_w[s][:], wg[:, :, s * P:(s + 1) * P]).then_inc(s_gw[s], 16)
                        sp.dma_start(up_w[s][:], wu[:, :, s * P:(s + 1) * P]).then_inc(s_uw[s], 16)
                    with sp.Fori(1, NF // 2) as i:
                        for s in range(2):
                            sp.wait_ge(s_gu, i * 2 + (g0 + s - 1))
                            sp.dma_start(gate_w[s][:], wg[:, :, ds((i * 2 + s) * P, P)]).then_inc(s_gw[s], 16)
                            sp.dma_start(up_w[s][:], wu[:, :, ds((i * 2 + s) * P, P)]).then_inc(s_uw[s], 16)
                    sp.wait_ge(s_gu, g0 + NF)
                    for s in range(2):
                        sp.dma_start(down_w[s][:], wd[:, :, s * P:(s + 1) * P]).then_inc(s_dw[s], 16)
                    with sp.Fori(1, KT // 2) as i:
                        for s in range(2):
                            sp.wait_ge(s_down, i * 2 + (d0 + s - 1))
                            sp.dma_start(down_w[s][:], wd[:, :, ds((i * 2 + s) * P, P)]).then_inc(s_dw[s], 16)

                @block.tensor
                def _(pe):
                    nrm.pe(pe)
                    nrm.wait(pe)
                    with pe.Fori(0, NF // 2) as i:
                        for s in range(2):
                            pe.wait_ge(s_gw[s], i * 16 + (w0 + 16))
                            pe.wait_ge(s_uw[s], i * 16 + (w0 + 16))
                            pe.wait_ge(s_free, i * 2 + (g0 + s + 1))
                            for b, w in ((0, gate_w[s]), (2, up_w[s])):
                                for n in range(2):
                                    for kt in range(KT):
                                        last = nc.tensor.matmul(bank[:, 4 * s + b + n, :], w[:, kt],
                                                                hT[:, kt, n * HALF:(n + 1) * HALF],
                                                                start=kt == 0, stop=kt == KT - 1)
                            last.then_inc(s_gu, 1)
                    pe.wait_ge(s_free, 2 + g0 + NF)
                    with pe.Fori(0, KT // 2) as i:
                        for s in range(2):
                            pe.wait_ge(s_dw[s], i * 16 + (dw0 + 16))
                            pe.wait_ge(s_dfree, i * 2 + (d0 + s + 1))
                            for n in range(2):
                                for kt in range(NF):
                                    last = nc.tensor.matmul(bank[:, 2 * s + n, :], down_w[s][:, kt],
                                                            aT[:, kt, n * HALF:(n + 1) * HALF],
                                                            start=kt == 0, stop=kt == NF - 1)
                            last.then_inc(s_down, 1)

                @block.scalar
                def _(act):
                    nrm.act(act)
                    with act.Fori(0, NF // 2) as i:
                        for s in range(2):
                            act.wait_ge(s_gu, i * 2 + (g0 + s + 1))
                            act.wait_ge(s_free, i * 2 + (g0 + s + 1))
                            nc.scalar.activation(sg[s][:], bank[:, 4 * s:4 * s + 2, :].rearrange("p a b -> p (a b)"),
                                                 ACT.Silu).then_inc(s_silu, 1)

                @block.vector
                def _(dve):
                    if not done:
                        dve.sem_inc(s_free, 2)
                        dve.sem_inc(s_dfree, 2)
                    nrm.dve(dve)
                    nrm.wait(dve)
                    with dve.Fori(0, NF // 2) as i:
                        for s in range(2):
                            dve.wait_ge(s_silu, i * 2 + (g0 + s + 1))
                            nc.vector.tensor_tensor(aT[:, ds(i * 2 + s, 1), :].rearrange("p a b -> p (a b)"), sg[s][:],
                                                    bank[:, 4 * s + 2:4 * s + 4, :].rearrange("p a b -> p (a b)"),
                                                    ALU.mult).then_inc(s_free, 1)
                    with dve.Fori(0, KT // 2) as i:
                        for s in range(2):
                            dve.wait_ge(s_down, i * 2 + (d0 + s + 1))
                            xs = xT[:, ds(i * 2 + s, 1), :].rearrange("p a b -> p (a b)")
                            nc.vector.scalar_tensor_tensor(
                                out=xs, in0=bank[:, 2 * s:2 * s + 2, :].rearrange("p a b -> p (a b)"), scalar=0.5,
                                in1=xs, op0=ALU.mult, op1=ALU.add).then_inc(s_dfree, 1)
                    dve.wait_ge(s_dfree, 2 + d0 + KT)

        ffn(0, d["w_gate1"], d["w_up1"], d["w_down1"], "ffn1_norm")

        w_in = panels(d["w_in"])
        hT_at = after_x
        r = Region(hT_at)
        hT = r(KT, T)
        kd = r(2, CH + T)
        v_win = r(T // CH, P)
        uT = r(T)
        ugT = r(T)
        shared_end = r.at

        def shared():
            s = Region(shared_end)
            sq, rms = s(KT, T), s(T)
            nrm = Norm(xT, hT, sq, rms, "mix_norm", T)
            w = Region(s.at)
            panel = [w(KT, P) for _ in range(5)]
            vT = w(CH + T)
            raw = w(2, T + 1)
            diff = w(T)
            s_pan = [sem(f"shared_panel_loaded{j}") for j in range(5)]
            s_ready, s_stored = sem("shared_ready"), sem("shared_stored")
            s_pad = sem("pads_zeroed")
            s_vt, s_vw = sem("v_transposed"), sem("v_windows_stored")
            s_mix, s_u = sem("low_rank_shift"), sem("low_rank_inputs_done")
            s_spill = sem("x_spilled")
            with nc.Block() as block:
                @block.sync
                def _(sp):
                    for j, name in enumerate(["ak", "ak", "av", "u", "ug"]):
                        if name == "ak":
                            for e in range(2):
                                at = COLS[name] + j * CH
                                sp.dma_start(panel[j][:, :, e * CH:(e + 1) * CH],
                                             w_in[:, :, at:at + CH]).then_inc(s_pan[j], 16)
                        else:
                            sp.dma_start(panel[j][:], w_in[:, :, COLS[name]:COLS[name] + P]).then_inc(s_pan[j], 16)
                    sp.dma_start(x_spill[:, :], xT[:].rearrange("p a b -> p (a b)")).then_inc(s_spill, 16)
                    sp.wait_ge(s_spill, 16)

                @block.gpsimd
                def _(pool):
                    nc.gpsimd.memset(kd[:, :, 0:CH], 0.0).then_inc(s_pad, 1)
                    nc.gpsimd.memset(vT[:, 0:CH], 0.0).then_inc(s_pad, 1)
                    nc.gpsimd.memset(raw[:, :, 0:1], 0.0).then_inc(s_pad, 1)

                @block.tensor
                def _(pe):
                    nrm.pe(pe)
                    nrm.wait(pe)
                    for j in range(5):
                        pe.wait_ge(s_pan[j], 32 if j < 2 else 16)
                        if j >= 3:
                            pe.wait_ge(s_stored, j - 2)
                        for n in range(2):
                            for kt in range(KT):
                                last = nc.tensor.matmul(bank[:, 2 * (j % 3) + n, :], panel[j][:, kt],
                                                        hT[:, kt, n * HALF:(n + 1) * HALF],
                                                        start=kt == 0, stop=kt == KT - 1)
                        last.then_inc(s_ready, 1)
                    pe.wait_ge(s_pad, 3)
                    pe.wait_ge(s_stored, 5)
                    for g in range(4):
                        for j in range(4):
                            n = 4 * g + j
                            last = nc.tensor.transpose(bank[:, 4 + g, j * P:(j + 1) * P],
                                                       vT[:, n * CH:n * CH + P], c("ident"))
                        last.then_inc(s_vt, 1)

                @block.scalar
                def _(act):
                    nrm.act(act)
                    dst = [kd[:, 0, CH:], kd[:, 1, CH:], vT[:, CH:], raw[:, 0, 1:], raw[:, 1, 1:]]
                    for j in range(5):
                        act.wait_ge(s_ready, j + 1)
                        b = 2 * (j % 3)
                        nc.scalar.activation(dst[j], bank[:, b:b + 2, :].rearrange("p a b -> p (a b)"),
                                             ACT.Copy).then_inc(s_stored, 1)
                    act.wait_ge(s_mix, 2)
                    nc.scalar.activation(uT[0:CH, :], uT[0:CH, :], ACT.Tanh).then_inc(s_u, 1)
                    act.wait_ge(s_mix, 4)
                    nc.scalar.activation(ugT[:], ugT[:], ACT.Tanh, scale=0.5).then_inc(s_u, 1)

                @block.vector
                def _(dve):
                    nrm.dve(dve)
                    dve.wait_ge(s_pad, 3)
                    for j, dst in enumerate([uT, ugT]):
                        dve.wait_ge(s_stored, 4 + j)
                        nc.vector.tensor_sub(diff[:], raw[:, j, 0:T], raw[:, j, 1:T + 1]).then_inc(s_mix, 1)
                        dve.wait_ge(s_mix, 2 * j + 1)
                        nc.vector.scalar_tensor_tensor(out=dst[:], in0=diff[:], scalar=par_u[:, j:j + 1],
                                                       in1=raw[:, j, 1:T + 1], op0=ALU.mult,
                                                       op1=ALU.add).then_inc(s_mix, 1)
                        dve.wait_ge(s_mix, 2 * j + 2)
                    for g in range(4):
                        dve.wait_ge(s_vt, g + 1)
                        nc.vector.tensor_copy(v_win[:, 4 * g:4 * g + 4, :].rearrange("p a b -> p (a b)"),
                                              bank[:, 4 + g, :]).then_inc(s_vw, 1)
                    dve.wait_ge(s_vw, 4)
                    dve.wait_ge(s_u, 2)
                    nc.vector.tensor_scalar(ugT[:], ugT[:], 0.5, 0.5, ALU.mult, ALU.add).then_inc(s_u, 1)
                    dve.wait_ge(s_u, 3)

        shared()

        def mixer():
            a = Region(xT_at)
            panel = [a(KT, P) for _ in range(3)]
            q_bd, gaT, gbT, b_bd = a(2 * NC, P), a(T), a(T), a(NC, P)
            assert a.at <= after_x
            a2 = Region(shared_end)
            k_bd, a_bd, v_bd = a2(NC, P), a2(NC, P), a2(NC, P)
            b_tok, k_tok, v_tok = a2(NC, P), a2(NC, P), a2(NC, P)
            lak_bd, nm_bd, x_bd, xt_bd, z_bd = a2(NC, P), a2(NC, P), a2(NC, P), a2(NC, P), a2(NC, P)
            zraw = a2(3, T + 1)
            lora = a2(3, P)
            ar = a2(NC, 2, CH)
            rm, km, vm, kp, g_out = a2(HALF), a2(HALF), a2(HALF), a2(HALF), a2(HALF)
            ld, cum, pin, pinv, pex = a2(HALF), a2(HALF), a2(HALF), a2(HALF), a2(HALF)
            kk, av, t1, t2 = a2(HALF), a2(HALF), a2(HALF), a2(HALF)
            b_st, v_st, mb, mk, n_st = a2(NC, CH), a2(NC, CH), a2(NC, CH), a2(NC, CH), a2(NC, CH)
            oa = a2(HALF)
            mrg = [a2(HALF) for _ in range(2)]
            alibi = a2(P)
            mx, es, den = a2(NC), a2(NC), a2(NC)
            root_in, root = a2(4, 2), a2(4, 2)
            minus_half = a2(4, 2)
            pp, half = a2(NPAR), a2(3)
            s_st, s_tmp, p1, sa_st = a2(CH), a2(CH), a2(CH), a2(CH)
            sa_bd = a2(P)
            s_bd = [a2(P) for _ in range(2)]

            def by_chunk(t):
                return t.rearrange("p (a b) -> p a b", a=NC)

            def flat(t):
                return t.rearrange("p a b -> p (a b)")

            xt_st, x_st, z_st = by_chunk(kk), by_chunk(av), by_chunk(pex)
            o_bd, prob, prob_t = xt_bd, k_tok, b_tok
            diff = [flat(mb), flat(mk), flat(n_st)]
            spread = flat(v_st).rearrange("p (a b c) -> p a b c", a=4, b=2)

            sems = {}

            def S(name):
                if name not in sems:
                    sems[name] = sem(name)
                return sems[name]

            def pv(name):
                i = PAR.index(name)
                return pp[:, i:i + 1]

            def hs(t, e):
                return t[e * CH:(e + 1) * CH]

            def bd(t, e, chunks=slice(0, NC)):
                return t[e * CH:(e + 1) * CH, chunks, e * CH:(e + 1) * CH]

            def bd1(t, e):
                return t[e * CH:(e + 1) * CH, e * CH:(e + 1) * CH]

            def over_chunks(m, n=NC):
                return m.unsqueeze(1).broadcast_to([m.shape[0], n, m.shape[1]])

            def two(bk):
                return bank[:, bk:bk + 2, :].rearrange("p a (c b) -> p (a c) b", b=P)

            def one(bk):
                return bank[:, bk, :].rearrange("p (c b) -> p c b", b=CH)

            PROJ = ["k", "r", "v", "q", "ga", "gb"]
            UNITS = 2 * len(PROJ)
            s_slot = [sem(f"mix_panel_loaded{j}") for j in range(3)]
            s_lora = sem("lora_panels_loaded")
            s_zero = sem("mix_zeroed")
            s_mw = [sem(f"merged_written{h}") for h in range(2)]
            DVE_STEPS = 60
            GROUPS = [slice(0, NC // 2), slice(NC // 2, NC)]

            FILL = [{"scores": 1, "sums": 2, "scale": 1, "probs": 1, "values": 1, "back": 1, "tokens": 1,
                     "triangles": 1, "level": 1, "chunk": 1, "mean": 5, "var": 5, "end": 0},
                    {"scores": 2, "sums": 4, "scale": 3, "probs": 3, "values": 3, "back": 3, "tokens": 3,
                     "triangles": 3, "level": 3, "chunk": 2, "mean": 3, "var": 3, "end": 3}]
            FIRST_UNIT = [8, UNITS]

            class Filling:

                def __init__(self, h, last):
                    self.h, self.at, self.idle = h, 0, h == 1 and last

                def take(self, point):
                    n = 0 if self.idle else FILL[self.h][point]
                    got = range(self.at, self.at + n)
                    self.at += n
                    return [(FIRST_UNIT[self.h] + m // KT, m % KT) for m in got]

                def full(self):
                    return self.idle or self.at == (32, 64)[self.h]

            with nc.Block() as block:
                @block.sync
                def _(sp):
                    def load(j, col):
                        sp.dma_start(panel[j % 3][:],
                                     w_in[:, :, COLS[PROJ[j]]:COLS[PROJ[j]] + D][:, :, ds(col, P)]).then_inc(
                                         s_slot[j % 3], 16)

                    def load_lora(col):
                        sp.dma_start(lora[0:CH, 0, :], d["w2"][:, ds(col, P)]).then_inc(s_lora, 16)
                        sp.dma_start(lora[CH:P, 1, :], d["a2"][:, ds(col, P)]).then_inc(s_lora, 16)
                        sp.dma_start(lora[:, 2, :], d["g2"][:, ds(col, P)]).then_inc(s_lora, 16)

                    def write_merged(p, h):
                        sp.wait_ge(S("merged_ready"), p * 2 + (h + 1))
                        sp.dma_start(m_spill[:, h * HALF:][:, ds(p * T, HALF)], mrg[h][:]).then_inc(s_mw[h], 16)

                    def load_after(j, col, used):
                        sp.wait_ge(S("proj_ready"), used)
                        load(j, col)

                    sp.wait_ge(s_zero, 1)
                    for j in range(3):
                        load(j, 0)
                    load_lora(0)
                    load_after(3, 0, 2)
                    with sp.Fori(0, PAIRS - 1) as p:
                        load_after(4, p * P, p * UNITS + 4)
                        load_after(5, p * P, p * UNITS + 6)
                        load_after(0, (p + 1) * P, p * UNITS + 8)
                        load_after(1, (p + 1) * P, p * UNITS + 10)
                        write_merged(p, 0)
                        load_after(2, (p + 1) * P, p * UNITS + 12)
                        load_after(3, p * P + P, p * UNITS + 14)
                        sp.wait_ge(S("lora_ready"), p * 2 + 2)
                        load_lora(p * P + P)
                        write_merged(p, 1)
                    load_after(4, (PAIRS - 1) * P, (PAIRS - 1) * UNITS + 4)
                    load_after(5, (PAIRS - 1) * P, (PAIRS - 1) * UNITS + 6)
                    for h in range(2):
                        write_merged(PAIRS - 1, h)
                    for h in range(2):
                        sp.wait_ge(s_mw[h], 16 * PAIRS + 16)

                @block.gpsimd
                def _(pool):
                    G = nc.gpsimd
                    G.memset(lora[:], 0.0).then_inc(s_zero, 1)
                    G.memset(zraw[:, :, 0:1], 0.0).then_inc(s_zero, 1)
                    G.memset(minus_half[:], -0.5).then_inc(s_zero, 1)
                    for t in (q_bd, b_bd, k_bd, a_bd, v_bd, lak_bd, nm_bd, x_bd, xt_bd, z_bd, sa_bd, s_bd[0],
                              s_bd[1]):
                        G.memset(t[:], 0.0).then_inc(s_zero, 1)
                    pool.wait_ge(s_zero, 16)
                    with pool.Fori(0, PAIRS) as p:
                        for h in range(2):
                            def wait(name, k=1, j=1):
                                pool.wait_ge(S(name), p * (2 * k) + (h * k + j))

                            for j in range(3):
                                if h == 0:
                                    pool.wait_ge(S("proj_stored"), p * UNITS + (2 + 2 * j + 2))
                                if h == 1 and j == 0:
                                    pool.wait_ge(S("y_stored"), p * 2 + 1)
                                if h == 0 and j == 0:
                                    pool.wait_ge(S("pair_done"), p + 1)
                                G.tensor_tensor(diff[j], zraw[:, j, h * HALF:(h + 1) * HALF],
                                                zraw[:, j, 1 + h * HALF:1 + (h + 1) * HALF],
                                                ALU.subtract).then_inc(S("diff_ready"), 1)
                            wait("kk_sums_stored")
                            G.tensor_tensor(root[:], root_in[:], minus_half[:], ALU.pow).then_inc(S("kk_rooted"), 1)
                            wait("cum_ready")
                            G.tensor_tensor(t1[:], cum[:], ld[:], ALU.subtract).then_inc(S("cum_before_ready"), 1)
                            for n, m in enumerate(LEVELS):
                                if n == 0:
                                    wait("n_stored")
                                else:
                                    wait("z_ready", 10, 2 * n)
                                for e in range(2):
                                    last = G.tensor_tensor(bd(nm_bd, e), hs(n_st, e),
                                                           over_chunks(hs(c(f"join{m}"), e)), ALU.mult)
                                last.then_inc(S("nm_ready"), 1)
                            wait("var_stored")
                            G.tensor_tensor(root[:], root_in[:], minus_half[:], ALU.pow).then_inc(S("var_rooted"), 1)

                @block.tensor
                def _(pe):
                    mm = nc.tensor.matmul

                    def per_chunk(out, lhs, rhs, chunks=range(NC)):
                        for i, n in enumerate(chunks):
                            last = mm(out[:, i, :], lhs[:, n, :], rhs(n), start=True, stop=True)
                        return last

                    def big(p, unit, kt):
                        j, n = unit % UNITS // 2, unit % 2
                        if kt == 0:
                            if n == 0:
                                pe.wait_ge(s_slot[j % 3], p * 32 + (unit // UNITS * 32 + j // 3 * 16 + 16))
                            pe.wait_ge(S("proj_stored"), p * UNITS + (unit + 1))
                        last = mm(bank[:, n, :], panel[j % 3][:, kt], hT[:, kt, n * HALF:(n + 1) * HALF],
                                  start=kt == 0, stop=kt == KT - 1)
                        if kt == KT - 1:
                            last.then_inc(S("proj_ready"), 1)

                    def body(p, last_pair):
                        g = p // 4
                        for h in range(2):
                            tok = slice(h * HALF, (h + 1) * HALF)
                            filling = Filling(h, last_pair)

                            def wait(name, k=1, j=1):
                                pe.wait_ge(S(name), p * (2 * k) + (h * k + j))

                            def fill(point):
                                for unit, kt in filling.take(point):
                                    big(p, unit, kt)

                            if h == 0:
                                pe.wait_ge(S("proj_stored"), p * UNITS + 10)
                            for n in range(NC):
                                w0 = (h * NC + n) * CH
                                last = mm(two(2)[:, n, :], q_bd[:, h * NC + n, :],
                                          flat(kd)[:, ds(g * (CH + T) + w0, P)], start=True, stop=True)
                            last.then_inc(S("att_scores_ready"), 1)
                            fill("scores")
                            wait("kk_squared")
                            for n in range(4):
                                last = mm(bank[:, 4, 2 * n:2 * n + 2], t1[:, n * P:(n + 1) * P],
                                          c("bd_ones")[:, ::CH], start=True, stop=True)
                            last.then_inc(S("kk_summed"), 1)
                            if h == 0:
                                pe.wait_ge(s_lora, p * 48 + 48)
                            for n, src in enumerate((uT, uT, ugT)):
                                last = mm(bank[:, 5 + n, :], lora[:, n, :], src[:, tok], start=True, stop=True)
                            last.then_inc(S("lora_ready"), 1)
                            fill("sums")
                            wait("kk_spread")
                            for n in range(4):
                                last = nc.tensor.transpose(bank[:, 4, n * P:(n + 1) * P],
                                                           spread[:, n].rearrange("p a b -> p (a b)"), c("ident"))
                            last.then_inc(S("kk_scale_ready"), 1)
                            fill("scale")
                            wait("att_exp_done")
                            for n in range(NC):
                                last = nc.tensor.transpose(two(2)[:, n, :], prob[:, n, :], c("ident"))
                            last.then_inc(S("probs_transposed"), 1)
                            fill("probs")
                            wait("prob_t_stored")
                            for n in range(NC):
                                last = mm(one(5)[:, n, :], prob_t[:, n, :],
                                          flat(v_win)[:, ds(g * CH + (h * NC + n) * P, CH)], start=True, stop=True)
                            last.then_inc(S("att_out_ready"), 1)
                            fill("values")
                            wait("o_bd_ready")
                            per_chunk(one(6), o_bd, lambda n: c("stack_ident")).then_inc(S("att_outT_ready"), 1)
                            fill("back")

                            wait("b_bd_ready")
                            for n in range(NC):
                                last = nc.tensor.transpose(two(2)[:, n, :], b_bd[:, n, :], c("ident"))
                            last.then_inc(S("b_tok_ready"), 1)
                            wait("k_bd_ready")
                            for n in range(NC):
                                last = nc.tensor.transpose(two(4)[:, n, :], k_bd[:, n, :], c("ident"))
                            last.then_inc(S("k_tok_ready"), 1)
                            wait("v_bd_ready")
                            wait("oa_stored")
                            for n in range(NC):
                                last = nc.tensor.transpose(two(6)[:, n, :], v_bd[:, n, :], c("ident"))
                            last.then_inc(S("v_tok_ready"), 1)
                            fill("tokens")
                            wait("a_bd_ready")
                            wait("b_tok_stored")
                            per_chunk(one(2), a_bd, lambda n: b_st[:, n, :]).then_inc(S("n_ready"), 1)
                            wait("k_tok_stored")
                            wait("ar_ready")
                            per_chunk(two(4), b_bd, lambda n: flat(ar[:, n])).then_inc(S("b_scores_ready"), 1)
                            wait("v_tok_stored")
                            per_chunk(two(6), k_bd, lambda n: flat(ar[:, n])).then_inc(S("k_scores_ready"), 1)
                            per_chunk(one(3), v_bd, lambda n: c("stack_ident")).then_inc(S("v_st_ready"), 1)
                            fill("triangles")

                            wait("k_scores_stored")
                            wait("v_st_stored")
                            for n in range(5):
                                wait("nm_ready", 5, n + 1)
                                for q in range(2):
                                    if n == 0:
                                        wait("x0_ready")
                                    else:
                                        wait("xt_stored", 8, 2 * (n - 1) + q + 1)
                                    per_chunk(one(2 + q), nm_bd, lambda i: xt_st[:, i, :],
                                              range(4 * q, 4 * q + 4)).then_inc(S("z_ready"), 1)
                                fill("level")
                                for q in range(2):
                                    wait("z_stored", 10, 2 * n + q + 1)
                                    if n > 0:
                                        wait("x_bd_stored", 8, 2 * (n - 1) + q + 1)
                                        wait("x_bd_lower_stored", 8, 2 * (n - 1) + q + 1)
                                    per_chunk(one(4 + q), x_bd, lambda i: z_st[:, i, :],
                                              range(4 * q, 4 * q + 4)).then_inc(S("xt_grown"), 1)
                                    if n < 4:
                                        wait("z_bd_stored", 8, 2 * n + q + 1)
                                        wait("z_bd_lower_stored", 8, 2 * n + q + 1)
                                        per_chunk(one(6 + q), z_bd, lambda i: x_st[:, i, :],
                                                  range(4 * q, 4 * q + 4)).then_inc(S("x_grown"), 1)
                            wait("rk_ready")
                            mm(bank[:, 7, :], c("bd_ones"), t2[:], start=True, stop=True).then_inc(S("bonus_ready"), 1)

                            def outputs(n):
                                pe.wait_ge(S("s_bd_ready"), p * 17 + (h * NC + n + 1))
                                wait("sa_bd_stored", NC, n + 1)
                                mm(one(6)[:, n, :], sa_bd[:], mb[:, n, :], start=True, stop=False)
                                mm(one(6)[:, n, :], v_tok[:, n, :], mk[:, n, :], start=False, stop=False)
                                mm(one(6)[:, n, :], s_bd[n % 2][:], ar[:, n, 1, :], start=False,
                                   stop=True).then_inc(S("y_ready"), 1)

                            wait("xt_bd_ready", 2, 2)
                            for n in range(NC):
                                pe.wait_ge(S("state_ready"), p * 17 + (h * NC + n + 1))
                                mm(bank[:, 2, 0:CH], a_bd[:, n, :], s_st[:], start=True, stop=False)
                                mm(bank[:, 2, 0:CH], lak_bd[:, n, :], v_st[:, n, :], start=False,
                                   stop=True).then_inc(S("p1_ready"), 1)
                                if n > 0:
                                    outputs(n - 1)
                                wait("p1_stored", NC, n + 1)
                                mm(bank[:, 3, 0:CH], xt_bd[:, n, :], p1[:], start=True,
                                   stop=True).then_inc(S("sa_ready"), 1)
                                fill("chunk")
                                wait("sa_stored", NC, n + 1)
                                mm(bank[:, 4, 0:CH], b_tok[:, n, :], sa_st[:], start=True, stop=False)
                                mm(bank[:, 4, 0:CH], k_tok[:, n, :], v_st[:, n, :], start=False,
                                   stop=True).then_inc(S("state_sum_ready"), 1)
                            outputs(NC - 1)

                            wait("y_stored")
                            mm(bank[:, 2, :], c("bd_ones"), ld[:], start=True, stop=True).then_inc(S("mean_ready"), 1)
                            fill("mean")
                            wait("yc_squared")
                            for n in range(4):
                                last = mm(bank[:, 4, 2 * n:2 * n + 2], t1[:, n * P:(n + 1) * P],
                                          c("bd_ones")[:, ::CH], start=True, stop=True)
                            last.then_inc(S("var_ready"), 1)
                            fill("var")
                            wait("var_spread")
                            for n in range(4):
                                last = nc.tensor.transpose(bank[:, 5, n * P:(n + 1) * P],
                                                           spread[:, n].rearrange("p a b -> p (a b)"), c("ident"))
                            last.then_inc(S("var_scale_ready"), 1)
                            fill("end")
                            assert filling.full()

                    pe.wait_ge(s_zero, 16)
                    for unit in range(8):
                        for kt in range(KT):
                            big(0, unit, kt)
                    with pe.Fori(0, PAIRS - 1) as p:
                        body(p, False)
                    body(PAIRS - 1, True)

                @block.scalar
                def _(act):
                    A = nc.scalar.activation

                    def store(p, unit):
                        j, n = unit % UNITS // 2, unit % 2
                        src = bank[:, n, :]
                        tok = slice(n * HALF, (n + 1) * HALF)
                        act.wait_ge(S("proj_ready"), p * UNITS + (unit + 1))
                        if j < 3:
                            if unit == UNITS:
                                act.wait_ge(S("zraw_used"), p * 2 + 2)
                            i = A(zraw[:, j, 1 + n * HALF:1 + (n + 1) * HALF], src, ACT.Copy)
                        elif j == 3:
                            if unit > UNITS and n == 0:
                                act.wait_ge(S("att_scores_ready"), p * 2 + 2)
                            for e in range(2):
                                i = A(bd(q_bd, e, slice(n * NC, (n + 1) * NC)), hs(one(n), e), ACT.Copy)
                        else:
                            if n == 0:
                                act.wait_ge(S("pair_done"), p + 1)
                            i = A((gaT, gbT)[j - 4][:, tok], src, ACT.Tanh, scale=0.5)
                        i.then_inc(S("proj_stored"), 1)

                    def body(p, last_pair):
                        for h in range(2):
                            filling = Filling(h, last_pair)

                            def wait(name, k=1, j=1):
                                act.wait_ge(S(name), p * (2 * k) + (h * k + j))

                            def stores(point):
                                for unit, kt in filling.take(point):
                                    if kt == KT - 1:
                                        store(p, unit)

                            stores("scores")
                            wait("km_ready")
                            A(t1[:], km[:], ACT.Square, scale=pv("k_k")).then_inc(S("kk_squared"), 1)
                            A(kk[:], km[:], ACT.Copy, scale=pv("k_k")).then_inc(S("kk_unscaled"), 1)
                            wait("lora_ready")
                            A(ld[:], bank[:, 5, :], ACT.Tanh, bias=half[:, 0:1],
                              scale=0.5).then_inc(S("decay_tanh"), 1)
                            A(av[:], bank[:, 6, :], ACT.Tanh, bias=half[:, 1:2], scale=0.5)
                            A(g_out[:], bank[:, 7, :], ACT.Copy, scale=0.5).then_inc(S("lora_stored"), 1)
                            wait("decay_tanh")
                            A(ld[:], ld[:], ACT.Copy, bias=C_DECAY, scale=C_DECAY).then_inc(S("ld_ready"), 1)
                            wait("vm_ready")
                            for e in range(2):
                                last = A(bd(v_bd, e), hs(by_chunk(vm), e), ACT.Copy)
                            last.then_inc(S("v_bd_ready"), 1)
                            stores("sums")
                            wait("att_shifted")
                            A(flat(prob), flat(prob), ACT.Exp)
                            A(es[:], mx[:], ACT.Exp, bias=pv("sink"), scale=-1.0).then_inc(S("att_exp_done"), 1)
                            wait("cum_ready")
                            A(pin[:], cum[:], ACT.Exp)
                            A(pinv[:], cum[:], ACT.Exp, scale=-1.0).then_inc(S("inverse_decay_ready"), 1)
                            wait("cum_before_ready")
                            A(pex[:], t1[:], ACT.Exp).then_inc(S("exp_done"), 1)
                            stores("scale")
                            wait("probs_transposed")
                            A(flat(prob_t), flat(bank[:, 2:4, :]), ACT.Copy).then_inc(S("prob_t_stored"), 1)
                            stores("probs")
                            stores("values")
                            wait("att_outT_ready")
                            A(oa[:], bank[:, 6, :], ACT.Copy, scale=0.5).then_inc(S("oa_stored"), 1)
                            stores("back")
                            wait("b_tok_ready")
                            A(flat(b_tok), flat(bank[:, 2:4, :]), ACT.Copy).then_inc(S("b_tok_stored"), 1)
                            wait("a_st_ready")
                            for e in range(2):
                                last = A(bd(a_bd, e), hs(ar, e)[:, :, 0, :], ACT.Copy)
                            last.then_inc(S("a_bd_ready"), 1)
                            wait("v_tok_ready")
                            A(flat(v_tok), flat(bank[:, 6:8, :]), ACT.Copy).then_inc(S("v_tok_stored"), 1)
                            stores("tokens")
                            wait("v_st_ready")
                            A(flat(v_st), bank[:, 3, :], ACT.Copy).then_inc(S("v_st_stored"), 1)
                            stores("triangles")
                            for n in range(5):
                                if n < 4:
                                    for q in range(2):
                                        wait("z_stored", 10, 2 * n + q + 1)
                                        A(bd(z_bd, 1, GROUPS[q]), hs(z_st, 1)[:, GROUPS[q]],
                                          ACT.Copy).then_inc(S("z_bd_lower_stored"), 1)
                                stores("level")
                                if n < 4:
                                    for q in range(2):
                                        wait("x_st_stored", 8, 2 * n + q + 1)
                                        A(bd(x_bd, 1, GROUPS[q]), hs(x_st, 1)[:, GROUPS[q]],
                                          ACT.Copy).then_inc(S("x_bd_lower_stored"), 1)

                            for n in range(NC):
                                wait("sa_stored", NC, n + 1)
                                if n > 0 or h > 0:
                                    wait("y_ready", NC, n)
                                for e in range(2):
                                    last = A(bd1(sa_bd, e), hs(sa_st, e), ACT.Copy)
                                last.then_inc(S("sa_bd_stored"), 1)
                                stores("chunk")
                                wait("state_added", NC, n + 1)
                                for e in range(2):
                                    last = A(bd1(s_bd[(n + 1) % 2], e), hs(s_tmp, e), ACT.Copy,
                                             scale=hs(pin, e)[:, n * CH + CH - 1:n * CH + CH])
                                last.then_inc(S("s_bd_ready"), 1)

                            wait("y_ready", NC, NC)
                            A(ld[:], bank[:, 6, :], ACT.Copy).then_inc(S("y_stored"), 1)
                            stores("mean")
                            wait("yc_ready")
                            A(t1[:], cum[:], ACT.Square).then_inc(S("yc_squared"), 1)
                            stores("var")
                            wait("y_normed")
                            A(cum[:], cum[:], ACT.Identity, bias=pv("ln_b"), scale=pv("ln_w")).then_inc(
                                S("y_affine"), 1)
                            stores("end")

                    act.wait_ge(s_zero, 16)
                    for unit in range(8):
                        store(0, unit)
                    with act.Fori(0, PAIRS - 1) as p:
                        body(p, False)
                    body(PAIRS - 1, True)

                @block.vector
                def _(dve):
                    V = nc.vector
                    dve.sem_inc(S("proj_stored"), 2)
                    dve.sem_inc(S("pair_done"), 1)
                    for h in range(2):
                        dve.sem_inc(s_mw[h], 16)
                    dve.wait_ge(s_zero, 16)
                    with dve.Fori(0, PAIRS) as p:
                        step = [0]

                        def link(ins):
                            step[0] += 1
                            ins.then_inc(S("dve_step"), 1)
                            dve.wait_ge(S("dve_step"), p * DVE_STEPS + step[0])

                        link(V.tensor_copy(pp[:], par[:, :, ds(p, 1)].rearrange("p a b -> p (a b)")))
                        for i, name in enumerate(("w0", "a0", "k_a")):
                            link(V.tensor_scalar(half[:, i:i + 1], pv(name), 0.5, None, ALU.mult))
                        link(V.tensor_scalar(alibi[:], c("dist"), c("neg_slope")[:, ds(p, 1)], None, ALU.mult))
                        V.memset(s_st[:], 0.0).then_inc(S("state_ready"), 1)
                        for e in range(2):
                            last = V.memset(bd1(s_bd[0], e), 0.0)
                        last.then_inc(S("s_bd_ready"), 1)

                        for h in range(2):
                            def wait(name, k=1, j=1):
                                dve.wait_ge(S(name), p * (2 * k) + (h * k + j))

                            def both(f, name=None):
                                for e in range(2):
                                    last = f(e)
                                    if e == 0 or name is None:
                                        link(last)
                                    else:
                                        last.then_inc(S(name), 1)

                            tok = slice(h * HALF, (h + 1) * HALF)
                            for j, (dst, mu, name) in enumerate(((km, "mu_k", "km_ready"), (rm, "mu_r", None),
                                                                 (vm, "mu_v", "vm_ready"))):
                                wait("diff_ready", 3, j + 1)
                                mixed = V.scalar_tensor_tensor(out=dst[:], in0=diff[j], scalar=pv(mu),
                                                               in1=zraw[:, j, 1 + h * HALF:1 + (h + 1) * HALF],
                                                               op0=ALU.mult, op1=ALU.add)
                                if name:
                                    mixed.then_inc(S(name), 1)
                            dve.wait_ge(S("vm_ready"), p * 2 + (h + 1))
                            dve.sem_inc(S("zraw_used"), 1)

                            wait("att_scores_ready")
                            link(V.scalar_tensor_tensor(out=prob[:], in0=two(2), scalar=0.125,
                                                        in1=over_chunks(alibi), op0=ALU.mult, op1=ALU.add))
                            if h == 0:
                                link(V.memset(prob[:, 0, 0:CH], -1e30))
                            link(V.tensor_reduce(mx[:], prob[:], AX.X, ALU.max))
                            link(V.tensor_scalar(mx[:], mx[:], pv("sink"), None, ALU.max))
                            V.tensor_tensor(prob[:], prob[:], mx.unsqueeze(2).broadcast_to([P, NC, P]),
                                            ALU.subtract).then_inc(S("att_shifted"), 1)

                            wait("kk_summed")
                            V.tensor_scalar(root_in[:], bank[:, 4, 0:8].rearrange("p (a b) -> p a b", a=4), 1e-24,
                                            None, ALU.max).then_inc(S("kk_sums_stored"), 1)
                            wait("ld_ready")
                            V.tensor_tensor_scan(cum[:], c("keep"), ld[:], 0.0, ALU.mult,
                                                 ALU.add).then_inc(S("cum_ready"), 1)
                            wait("kk_rooted")
                            V.tensor_copy(spread, root[:].unsqueeze(3).broadcast_to([P, 4, 2, CH])).then_inc(
                                S("kk_spread"), 1)
                            wait("lora_stored")
                            link(V.tensor_scalar(t2[:], av[:], 1.0, half[:, 2:3], ALU.subtract, ALU.mult))
                            link(V.scalar_tensor_tensor(out=kp[:], in0=t2[:], scalar=1.0, in1=km[:], op0=ALU.add,
                                                        op1=ALU.mult))
                            wait("kk_unscaled")
                            wait("kk_scale_ready")
                            link(V.tensor_tensor(kk[:], bank[:, 4, :], kk[:], ALU.mult))
                            link(V.scalar_tensor_tensor(out=t2[:], in0=av[:], scalar=1.0, in1=kk[:], op0=ALU.add,
                                                        op1=ALU.mult))
                            wait("inverse_decay_ready")
                            link(V.scalar_tensor_tensor(out=flat(b_st), in0=t2[:], scalar=0.5, in1=pinv[:],
                                                        op0=ALU.mult, op1=ALU.mult))
                            both(lambda e: V.tensor_copy(bd(b_bd, e), hs(b_st, e)), "b_bd_ready")
                            wait("att_exp_done")
                            link(V.tensor_reduce(den[:], prob[:], AX.X, ALU.add))
                            link(V.tensor_add(den[:], den[:], es[:]))
                            link(V.reciprocal(den[:], den[:]))
                            wait("exp_done")
                            V.scalar_tensor_tensor(out=ar[:, :, 0, :], in0=by_chunk(kk), scalar=-1.0,
                                                   in1=by_chunk(pex), op0=ALU.mult,
                                                   op1=ALU.mult).then_inc(S("a_st_ready"), 1)
                            V.tensor_mul(ar[:, :, 1, :], by_chunk(rm), by_chunk(pin)).then_inc(S("ar_ready"), 1)
                            wait("att_out_ready")
                            both(lambda e: V.tensor_tensor(bd(o_bd, e), one(5)[e * CH:(e + 1) * CH],
                                                           hs(den, e).unsqueeze(2).broadcast_to([CH, NC, CH]),
                                                           ALU.mult), "o_bd_ready")
                            both(lambda e: V.tensor_mul(bd(k_bd, e), hs(by_chunk(kp), e), hs(by_chunk(pinv), e)),
                                 "k_bd_ready")
                            wait("k_tok_ready")
                            V.tensor_copy(flat(k_tok), flat(bank[:, 4:6, :])).then_inc(S("k_tok_stored"), 1)

                            ident8 = over_chunks(c("stack_ident"))
                            wait("n_ready")
                            V.tensor_tensor(n_st, one(2), over_chunks(c("col_before_row")),
                                            ALU.mult).then_inc(S("n_stored"), 1)
                            wait("n_stored")
                            link(V.tensor_tensor(x_st, n_st, over_chunks(c("join1")), ALU.mult))
                            link(V.tensor_tensor(x_st, x_st, ident8, ALU.add))
                            both(lambda e: V.tensor_copy(bd(x_bd, e), hs(x_st, e)))
                            wait("b_scores_ready")
                            link(V.tensor_tensor(xt_st, two(4)[:, :, 0:CH], over_chunks(c("join1T")), ALU.mult))
                            link(V.tensor_tensor(xt_st, xt_st, ident8, ALU.add))
                            V.tensor_tensor(mb, two(4)[:, :, CH:P], over_chunks(c("row_upto_col")),
                                            ALU.mult).then_inc(S("x0_ready"), 1)
                            wait("k_scores_ready")
                            both(lambda e: V.tensor_tensor(bd(lak_bd, e), hs(two(6), e)[:, :, 0:CH],
                                                           over_chunks(hs(c("row_before_col"), e)), ALU.mult))
                            V.tensor_tensor(mk, two(6)[:, :, CH:P], over_chunks(c("row_upto_col")),
                                            ALU.mult).then_inc(S("k_scores_stored"), 1)
                            V.scalar_tensor_tensor(out=t2[:], in0=rm[:], scalar=pv("r_k"), in1=kp[:], op0=ALU.mult,
                                                   op1=ALU.mult).then_inc(S("rk_ready"), 1)
                            for n in range(5):
                                for q, sl in enumerate(GROUPS):
                                    wait("z_ready", 10, 2 * n + q + 1)
                                    V.tensor_copy(z_st[:, sl], one(2 + q)[:, 0:NC // 2]).then_inc(S("z_stored"), 1)
                                    if n < 4:
                                        wait("z_stored", 10, 2 * n + q + 1)
                                        V.tensor_copy(bd(z_bd, 0, sl), hs(z_st, 0)[:, sl]).then_inc(
                                            S("z_bd_stored"), 1)
                                for q, sl in enumerate(GROUPS):
                                    wait("xt_grown", 10, 2 * n + q + 1)
                                    if n == 4:
                                        for e in range(2):
                                            last = V.tensor_tensor(bd(xt_bd, e, sl), hs(one(4 + q), e)[:, 0:NC // 2],
                                                                   hs(xt_st, e)[:, sl], ALU.add)
                                        last.then_inc(S("xt_bd_ready"), 1)
                                        continue
                                    V.tensor_tensor(xt_st[:, sl], one(4 + q)[:, 0:NC // 2], xt_st[:, sl],
                                                    ALU.add).then_inc(S("xt_stored"), 1)
                                    wait("x_grown", 8, 2 * n + q + 1)
                                    V.tensor_tensor(x_st[:, sl], one(6 + q)[:, 0:NC // 2], x_st[:, sl],
                                                    ALU.add).then_inc(S("x_st_stored"), 1)
                                    wait("x_st_stored", 8, 2 * n + q + 1)
                                    V.tensor_copy(bd(x_bd, 0, sl), hs(x_st, 0)[:, sl]).then_inc(S("x_bd_stored"), 1)
                            wait("bonus_ready")
                            link(V.tensor_tensor(vm[:], bank[:, 7, :], vm[:], ALU.mult))

                            for n in range(NC):
                                wait("p1_ready", NC, n + 1)
                                V.tensor_copy(p1[:], bank[:, 2, 0:CH]).then_inc(S("p1_stored"), 1)
                                wait("sa_ready", NC, n + 1)
                                if n > 0 or h > 0:
                                    wait("sa_bd_stored", NC, n)
                                V.tensor_copy(sa_st[:], bank[:, 3, 0:CH]).then_inc(S("sa_stored"), 1)
                                wait("state_sum_ready", NC, n + 1)
                                if n > 0 or h > 0:
                                    dve.wait_ge(S("s_bd_ready"), p * 17 + (h * NC + n + 1))
                                V.tensor_tensor(s_tmp[:], bank[:, 4, 0:CH], s_st[:],
                                                ALU.add).then_inc(S("state_added"), 1)
                                wait("state_added", NC, n + 1)
                                V.tensor_scalar(s_st[:], s_tmp[:], pin[:, n * CH + CH - 1:n * CH + CH], None,
                                                ALU.mult).then_inc(S("state_ready"), 1)

                            wait("mean_ready")
                            V.scalar_tensor_tensor(out=cum[:], in0=bank[:, 2, :], scalar=-1.0 / CH, in1=ld[:],
                                                   op0=ALU.mult, op1=ALU.add).then_inc(S("yc_ready"), 1)
                            wait("var_ready")
                            V.tensor_scalar(root_in[:], bank[:, 4, 0:8].rearrange("p (a b) -> p a b", a=4),
                                            1.0 / CH, GN_EPS, ALU.mult, ALU.add).then_inc(S("var_stored"), 1)
                            wait("var_rooted")
                            V.tensor_copy(spread, root[:].unsqueeze(3).broadcast_to([P, 4, 2, CH])).then_inc(
                                S("var_spread"), 1)
                            wait("var_scale_ready")
                            V.tensor_tensor(cum[:], bank[:, 5, :], cum[:], ALU.mult).then_inc(S("y_normed"), 1)
                            if h == 0:
                                dve.wait_ge(S("proj_stored"), p * UNITS + 14)
                            wait("oa_stored")
                            link(V.scalar_tensor_tensor(out=oa[:], in0=gaT[:, tok], scalar=1.0, in1=oa[:],
                                                        op0=ALU.add, op1=ALU.mult))
                            link(V.scalar_tensor_tensor(out=g_out[:], in0=gbT[:, tok], scalar=1.0, in1=g_out[:],
                                                        op0=ALU.add, op1=ALU.mult))
                            wait("y_affine")
                            link(V.tensor_add(cum[:], cum[:], vm[:]))
                            link(V.tensor_mul(cum[:], cum[:], g_out[:]))
                            dve.wait_ge(s_mw[h], p * 16 + 16)
                            V.tensor_add(mrg[h][:], cum[:], oa[:]).then_inc(S("merged_ready"), 1)
                            wait("merged_ready")
                        dve.sem_inc(S("pair_done"), 1)
                        assert step[0] == DVE_STEPS, f"DVE_STEPS {step[0]}"

        mixer()

        def finish():
            r = Region(after_x)
            yT, sq, rms, rows = r(KT, T), r(KT, T), r(T), r(8, D)
            nrm = Norm(xT, yT, sq, rms, "final_norm", T)
            s_tr, s_ev, s_out = s_x_tr, s_x_ev, sem("out_written")
            with nc.Block() as block:
                @block.sync
                def _(sp):
                    for t in range(8):
                        sp.wait_ge(s_ev, 16 + 2 * t + 2)
                        sp.dma_start(out[t * P:(t + 1) * P, :], rows[:, t, :]).then_inc(s_out, 16)
                    sp.wait_ge(s_out, 128)

                @block.scalar
                def _(act):
                    nrm.act(act)

                @block.tensor
                def _(pe):
                    nrm.pe(pe)
                    nrm.wait(pe)
                    for g in range(16):
                        if g >= 6:
                            pe.wait_ge(s_ev, 16 + g - 5)
                        for j in range(4):
                            kt = 4 * (g % 2) + j
                            last = nc.tensor.transpose(bank[:, g % 6, j * P:(j + 1) * P],
                                                       yT[:, kt, (g // 2) * P:(g // 2 + 1) * P], c("ident"))
                        last.then_inc(s_tr, 1)

                @block.vector
                def _(dve):
                    nrm.dve(dve)
                    for g in range(16):
                        dve.wait_ge(s_tr, 16 + g + 1)
                        nc.vector.tensor_copy(rows[:, g // 2, (g % 2) * HALF:(g % 2 + 1) * HALF],
                                              bank[:, g % 6, :]).then_inc(s_ev, 1)
        s_re = sem("project_reloaded")
        s_pan = [sem(f"project_panel_loaded{s}") for s in range(4)]
        s_ready, s_free_banks = sem("project_ready"), sem("project_added")

        def project(done, w, srcT, reload):
            r = Region(after_x + KT * T * (1 if reload else 2))
            slot = [r(KT, P) for _ in range(4)]
            wp = panels(w)
            o0, p0 = done * KT, done * 32
            with nc.Block() as block:
                @block.sync
                def _(sp):
                    if reload:
                        sp.dma_start(srcT[:].rearrange("p a b -> p (a b)"), m_spill[:, :]).then_inc(s_re, 16)
                        sp.dma_start(xT[:].rearrange("p a b -> p (a b)"), x_spill[:, :]).then_inc(s_re, 16)
                    for s in range(4):
                        sp.dma_start(slot[s][:], wp[:, :, s * P:(s + 1) * P]).then_inc(s_pan[s], 16)
                    for s in range(4):
                        sp.wait_ge(s_ready, o0 + s + 1)
                        sp.dma_start(slot[s][:], wp[:, :, (4 + s) * P:(5 + s) * P]).then_inc(s_pan[s], 16)

                @block.tensor
                def _(pe):
                    if reload:
                        pe.wait_ge(s_re, 32)
                    for o in range(KT):
                        pe.wait_ge(s_pan[o % 4], p0 + 16 * (o // 4 + 1))
                        if o >= 4:
                            pe.wait_ge(s_free_banks, o0 + o - 3)
                        for n in range(2):
                            for kt in range(KT):
                                last = nc.tensor.matmul(bank[:, 2 * (o % 4) + n, :], slot[o % 4][:, kt],
                                                        srcT[:, kt, n * HALF:(n + 1) * HALF],
                                                        start=kt == 0, stop=kt == KT - 1)
                        last.then_inc(s_ready, 1)

                @block.vector
                def _(dve):
                    if reload:
                        dve.wait_ge(s_re, 32)
                    for o in range(KT):
                        dve.wait_ge(s_ready, o0 + o + 1)
                        nc.vector.tensor_tensor(
                            xT[:, o, :], bank[:, 2 * (o % 4):2 * (o % 4) + 2, :].rearrange("p a b -> p (a b)"),
                            xT[:, o, :], ALU.add).then_inc(s_free_banks, 1)
                    dve.wait_ge(s_free_banks, o0 + KT)

        project(0, d["w_out"], hT, True)

        def cross():
            r = Region(after_x)
            hx, oT = r(KT, T), r(KT, T)
            memT, rms_m = r(KT, NMEM), r(NMEM)
            after = r.at
            r1 = Region(after)
            sq, rms, mem_rows, sq_m = r1(KT, T), r1(T), r1(MT, D), r1(KT, NMEM)
            r2 = Region(after)
            q_w, k_w, v_w = r2(2, KT, P), r2(2, KT, P), r2(KT, NMEM)
            qh, kh, vh = r2(2, T), r2(2, NMEM), r2(MT, 2 * P)
            prob, prob_t = r2(8, NMEM), r2(MT, T)
            mx, den = r2(8), r2(8)
            nx = Norm(xT, hx, sq, rms, "cross_norm", T)
            nm = Norm(memT, memT, sq_m, rms_m, "mem_norm", NMEM)
            s_in, s_tr, s_ev = sem("mem_loaded"), sem("mem_transposed"), sem("mem_stored")

            def flat(t):
                return t.rearrange("p a b -> p (a b)")

            with nc.Block() as block:
                @block.sync
                def _(sp):
                    sp.dma_start(mem_rows[:], d["mem"].rearrange("(t p) c -> p t c", p=P)).then_inc(s_in, 16)

                @block.tensor
                def _(pe):
                    pe.wait_ge(s_in, 16)
                    for g in range(4):
                        for j in range(4):
                            kt = 2 * g + j // 2
                            last = nc.tensor.transpose(bank[:, g, j * P:(j + 1) * P],
                                                       mem_rows[:, j % 2, kt * P:(kt + 1) * P], c("ident"))
                        last.then_inc(s_tr, 1)
                    nx.pe(pe)
                    pe.wait_ge(nx.rooted, nx.p0 + 2)
                    nm.pe(pe)

                @block.scalar
                def _(act):
                    nx.act(act)
                    act.wait_ge(s_ev, 4)
                    nm.act(act)

                @block.vector
                def _(dve):
                    for g in range(4):
                        dve.wait_ge(s_tr, g + 1)
                        nc.vector.tensor_copy(flat(memT[:, 2 * g:2 * g + 2, :]), bank[:, g, :]).then_inc(s_ev, 1)
                    nx.dve(dve)
                    nm.dve(dve)
                    nm.wait(dve)
                    nx.wait(dve)

            s_w = [sem(f"cross_{n}_weights_loaded") for n in "qkv"]
            s_q, s_k, s_v = sem("cross_q_ready"), sem("cross_k_ready"), sem("cross_v_ready")
            s_qs, s_kvs = sem("cross_q_stored"), sem("cross_kv_stored")
            s_sc, s_sh, s_exp, s_norm = sem("cross_scores"), sem("cross_shifted"), sem("cross_exp"), sem("cross_probs")
            s_pt, s_pts, s_o, s_os = (sem("cross_probs_transposed"), sem("cross_probs_t_stored"), sem("cross_out"),
                                      sem("cross_out_stored"))
            s_step = sem("cross_dve_step")
            with nc.Block() as block:
                wq, wkv = panels(d["w_cq"]), panels(d["w_ckv"])

                @block.sync
                def _(sp):
                    def load_q(i):
                        for t in range(2):
                            sp.dma_start(q_w[:, t], wq[:, :, t * P:][:, :, ds(i * NMEM, P)]).then_inc(s_w[0], 16)

                    def load_k(i):
                        for t in range(2):
                            sp.dma_start(k_w[:, t], wkv[:, :, t * P:][:, :, ds(i * NMEM, P)]).then_inc(s_w[1], 16)

                    def load_v(i):
                        sp.dma_start(v_w[:], wkv[:, :, D:][:, :, ds(i * NMEM, NMEM)]).then_inc(s_w[2], 16)

                    load_k(0)
                    load_v(0)
                    load_q(0)
                    with sp.Fori(1, XH) as i:
                        sp.wait_ge(s_k, i)
                        load_k(i)
                        sp.wait_ge(s_v, i)
                        load_v(i)
                        sp.wait_ge(s_q, i * 2)
                        load_q(i)

                @block.tensor
                def _(pe):
                    mm = nc.tensor.matmul
                    with pe.Fori(0, XH) as i:
                        pe.wait_ge(s_os, i * 2 + 2)
                        pe.wait_ge(s_w[1], i * 32 + 32)
                        for t in range(2):
                            for kt in range(KT):
                                last = mm(bank[:, 4 + t, 0:NMEM], k_w[:, t, kt], memT[:, kt, :], start=kt == 0,
                                          stop=kt == KT - 1)
                        last.then_inc(s_k, 1)
                        pe.wait_ge(s_w[2], i * 16 + 16)
                        for t in range(MT):
                            for kt in range(KT):
                                last = mm(bank[:, 6 + t, 0:NMEM], memT[:, kt, t * P:(t + 1) * P], v_w[:, kt, :],
                                          start=kt == 0, stop=kt == KT - 1)
                        last.then_inc(s_v, 1)
                        pe.wait_ge(s_w[0], i * 32 + 32)
                        for t in range(2):
                            for n in range(2):
                                for kt in range(KT):
                                    last = mm(bank[:, 2 * t + n, :], q_w[:, t, kt], hx[:, kt, n * HALF:(n + 1) * HALF],
                                              start=kt == 0, stop=kt == KT - 1)
                            last.then_inc(s_q, 1)
                        pe.wait_ge(s_kvs, i * 2 + 2)
                        pe.wait_ge(s_qs, i * 2 + 2)
                        for t in range(8):
                            for k in range(2):
                                last = mm(bank[:, t // 2, (t % 2) * NMEM:(t % 2 + 1) * NMEM],
                                          qh[:, k, t * P:(t + 1) * P], kh[:, k, :], start=k == 0, stop=k == 1)
                        last.then_inc(s_sc, 1)
                        pe.wait_ge(s_norm, i + 1)
                        for m in range(MT):
                            for t in range(8):
                                last = nc.tensor.transpose(bank[:, 4 + 2 * m + t // 4, (t % 4) * P:(t % 4 + 1) * P],
                                                           prob[:, t, m * P:(m + 1) * P], c("ident"))
                            last.then_inc(s_pt, 1)
                        pe.wait_ge(s_pts, i * 2 + 2)
                        for t in range(2):
                            for n in range(2):
                                for m in range(MT):
                                    last = mm(bank[:, 2 * t + n, :], vh[:, m, t * P:(t + 1) * P],
                                              prob_t[:, m, n * HALF:(n + 1) * HALF], start=m == 0, stop=m == MT - 1)
                            last.then_inc(s_o, 1)

                @block.scalar
                def _(act):
                    A = nc.scalar.activation
                    with act.Fori(0, XH) as i:
                        act.wait_ge(s_k, i + 1)
                        A(kh[:], bank[:, 4:6, 0:NMEM], ACT.Copy).then_inc(s_kvs, 1)
                        act.wait_ge(s_v, i + 1)
                        A(vh[:], bank[:, 6:8, 0:NMEM], ACT.Copy).then_inc(s_kvs, 1)
                        for t in range(2):
                            act.wait_ge(s_q, i * 2 + (t + 1))
                            A(qh[:, t, :], flat(bank[:, 2 * t:2 * t + 2, :]), ACT.Copy).then_inc(s_qs, 1)
                        act.wait_ge(s_sh, i + 1)
                        A(flat(prob), flat(prob), ACT.Exp, scale=1.0 / 16).then_inc(s_exp, 1)
                        for m in range(MT):
                            act.wait_ge(s_pt, i * 2 + (m + 1))
                            A(prob_t[:, m, :], flat(bank[:, 4 + 2 * m:6 + 2 * m, :]), ACT.Copy).then_inc(s_pts, 1)

                @block.vector
                def _(dve):
                    V = nc.vector
                    dve.sem_inc(s_os, 2)
                    with dve.Fori(0, XH) as i:
                        step = [0]

                        def link(ins):
                            step[0] += 1
                            ins.then_inc(s_step, 1)
                            dve.wait_ge(s_step, i * 3 + step[0])

                        dve.wait_ge(s_sc, i + 1)
                        sc = bank[:, 0:4, :].rearrange("p a (b c) -> p (a b) c", c=NMEM)
                        link(V.tensor_reduce(mx[:], sc, AX.X, ALU.max))
                        V.tensor_tensor(prob[:], sc, mx[:].unsqueeze(2).broadcast_to([P, 8, NMEM]),
                                        ALU.subtract).then_inc(s_sh, 1)
                        dve.wait_ge(s_exp, i + 1)
                        link(V.tensor_reduce(den[:], prob[:], AX.X, ALU.add))
                        link(V.reciprocal(den[:], den[:]))
                        V.tensor_tensor(prob[:], prob[:], den[:].unsqueeze(2).broadcast_to([P, 8, NMEM]),
                                        ALU.mult).then_inc(s_norm, 1)
                        for t in range(2):
                            dve.wait_ge(s_o, i * 2 + (t + 1))
                            V.tensor_scalar(flat(oT[:, ds(i * 2 + t, 1), :]), flat(bank[:, 2 * t:2 * t + 2, :]), 1.0,
                                            None, ALU.mult).then_inc(s_os, 1)
                    dve.wait_ge(s_os, 2 * XH + 2)
            project(1, d["w_co"], oT, False)

        cross()
        ffn(1, d["w_gate2"], d["w_up2"], d["w_down2"], "ffn2_norm")

        finish()


def kernel(**inputs):
    import concourse.bacc as _bacc
    from concourse.bass_utils import run_bass_kernel_spmd as _run

    def col(v):
        return np.ascontiguousarray(np.reshape(v, (-1, P)).T)

    g = {k: np.asarray(v) for k, v in inputs.items()}
    mu = g["rwkv_mu"][0]
    vec = {"ffn1_norm": g["ffn1_norm"][0], "mix_norm": g["mix_norm"][0], "cross_norm": g["cross_norm"][0],
           "mem_norm": g["mem_norm"][0], "ffn2_norm": g["ffn2_norm"][0], "final_norm": g["final_norm"],
           "mu_r": mu[0:D], "mu_k": mu[D:2 * D], "mu_v": mu[2 * D:3 * D], "w0": g["rwkv_w0"][0],
           "a0": g["rwkv_a0"][0], "k_k": g["rwkv_k_k"][0], "k_a": g["rwkv_k_a"][0],
           "r_k": np.reshape(g["rwkv_r_k"][0], (-1,)), "ln_w": g["rwkv_ln_w"][0], "ln_b": g["rwkv_ln_b"][0],
           "sink": np.repeat(g["attn_sinks"][0], CH)}
    arrays = {
        "x": g["x"][0], "mem": g["mem"][0], "consts": constants()[0],
        "params": np.concatenate([col(vec[n]) for n in PAR], 1),
        "params_u": col(mu[3 * D:3 * D + 2 * P]),
        "w_gate1": g["ffn1_w_gate"][0], "w_up1": g["ffn1_w_up"][0], "w_down1": g["ffn1_w_down"][0],
        "w_in": g["w_in"][0], "w2": g["rwkv_w2"][0], "a2": g["rwkv_a2"][0], "g2": g["rwkv_g2"][0],
        "w_out": g["w_out"][0], "w_cq": g["w_cq"][0], "w_ckv": g["w_ckv"][0], "w_co": g["w_co"][0],
        "w_gate2": g["ffn2_w_gate"][0], "w_up2": g["ffn2_w_up"][0], "w_down2": g["ffn2_w_down"][0],
    }
    arrays = {k: np.ascontiguousarray(v) for k, v in arrays.items()}
    nc = _bacc.Bacc("TRN2", target_bir_lowering=False, num_devices=1)
    d = {n: nc.dram_tensor(n, v.shape, mybir.dt.from_np(v.dtype), kind="ExternalInput").ap()
         for n, v in arrays.items()}
    out = nc.dram_tensor("out", (T, D), F32, kind="ExternalOutput").ap()
    x_spill = nc.dram_tensor("x_spill", (P, KT * T), F32, kind="Internal").ap()
    m_spill = nc.dram_tensor("m_spill", (P, KT * T), F32, kind="Internal").ap()
    build(nc, d, out, x_spill, m_spill)
    r = _run(nc, [arrays], core_ids=[0])
    return r.results[0]["out"].reshape(1, T, D)
```

```python
import concourse.bass as bass
from concourse import mybir
from contextlib import ExitStack
import numpy as np

F32 = mybir.dt.float32
F32R = mybir.dt.float32r
ACT = mybir.ActivationFunctionType
ALU = mybir.AluOpType
AX = mybir.AxisListType
ds = bass.ds

P = 128
SBUF_WORDS = 53000
BASE_WORDS = 10114
D = 1024
KT = D // P
T = 1024
HALF = 512
NF = 2816 // P
CH = 64
NC = HALF // CH
PAIRS = 8
NMEM = 256
MT = NMEM // P
XH = 4
RMS_EPS = 1e-6
GN_EPS = 64e-5
LEVELS = [2, 4, 8, 16, 32]
C_DECAY = -0.5 * float(np.exp(-0.5))

PAR = ["ffn1_norm", "mix_norm", "cross_norm", "mem_norm", "ffn2_norm", "final_norm", "mu_r", "mu_k", "mu_v",
       "w0", "a0", "k_k", "k_a", "r_k", "ln_w", "ln_b", "sink"]
NPAR = len(PAR)
COLS = {"q": 0, "ak": 1024, "av": 1152, "r": 1280, "k": 2304, "v": 3328, "u": 4352, "ug": 4480, "ga": 4608,
        "gb": 5632}


def constants():
    row, col = np.arange(P)[:, None], np.arange(P)[None, :]
    i, j = row % CH, np.arange(CH)[None, :]
    parts = {"ident": row == col, "stack_ident": i == j, "bd_ones": row // CH == col // CH,
             "ones": np.ones((P, P)), "dist": np.abs(i + CH - col),
             "neg_slope": -2.0 ** (-8.0 * (2 * np.arange(PAIRS)[None, :] + row // CH + 1) / 16),
             "row_before_col": i < j, "row_upto_col": i <= j, "col_before_row": j < i,
             "keep": np.ones((P, 1)) * (np.arange(HALF)[None, :] % CH != 0)}

    def joins(m, a, b):
        return (a // (2 * m) == b // (2 * m)) & ((a // m) % 2 == 1) & ((b // m) % 2 == 0)

    parts["join1"] = joins(1, i, j)
    parts["join1T"] = joins(1, j, i)
    for m in LEVELS:
        parts[f"join{m}"] = joins(m, i, j)
    where, at = {}, 0
    for name, a in parts.items():
        where[name] = (at, a.shape[1])
        at += a.shape[1]
    return np.concatenate([np.asarray(a, np.float32) for a in parts.values()], 1), where


def build(nc, d, out, x_spill, m_spill):
    table, where = constants()
    ctx = ExitStack()
    with ctx:
        def sem(name):
            return ctx.enter_context(nc.semaphore(name))

        BASE = BASE_WORDS
        arena = ctx.enter_context(nc.sbuf_tensor("arena", [P, BASE], F32))
        opened = []
        work = [None]
        bank = ctx.enter_context(nc.psum_tensor("bank", [P, 8, 512], F32))

        class Region:

            def __init__(self, at):
                self.at = at

            def __call__(self, *dims):
                n = int(np.prod(dims))
                if self.at < BASE:
                    v = arena[:, self.at:self.at + n]
                else:
                    v = work[0][:, self.at - BASE:self.at - BASE + n]
                self.at += n
                assert self.at <= SBUF_WORDS, self.at
                if len(dims) == 2:
                    v = v.rearrange("p (a b) -> p a b", a=dims[0])
                elif len(dims) == 3:
                    v = v.rearrange("p (a b c) -> p a b c", a=dims[0], b=dims[1])
                return v

        keep = Region(0)
        cst = keep(table.shape[1])
        par = keep(NPAR, KT)
        par_u = keep(2)
        minus_half_c = keep(16)
        sums_in, sums_root = keep(8, 2), keep(8, 2)
        phase_base = keep.at
        xT_at = phase_base
        xT = keep(KT, T)
        after_x = keep.at
        assert after_x == BASE, after_x

        def open_work(scope):
            work[0] = scope.enter_context(nc.sbuf_tensor(f"work{len(opened)}", [P, SBUF_WORDS - BASE], F32))
            opened.append(1)

        def c(name):
            at, n = where[name]
            return cst[:, at:at + n]

        def gain(name, kt):
            return par[:, PAR.index(name), kt:kt + 1]

        def panels(w, rows=KT):
            return w.rearrange("(k p) n -> p k n", p=P)

        scope = ExitStack()
        open_work(scope)
        x_rows = Region(after_x)(8, D)
        s_cst, s_xin, s_x_tr, s_x_ev = sem("consts_loaded"), sem("rows_loaded"), sem("x_transposed"), sem("x_stored")
        s_eps = sem("eps_set")
        with nc.Block() as block:
            @block.sync
            def _(sp):
                sp.dma_start(cst[:], d["consts"][:, :]).then_inc(s_cst, 16)
                sp.dma_start(par[:], d["params"].rearrange("p (a b) -> p a b", a=NPAR)).then_inc(s_cst, 16)
                sp.dma_start(par_u[:], d["params_u"][:, :]).then_inc(s_cst, 16)
                sp.dma_start(x_rows[:], d["x"].rearrange("(t p) c -> p t c", p=P)).then_inc(s_xin, 16)

            @block.gpsimd
            def _(pool):
                nc.gpsimd.memset(minus_half_c[:], -0.5).then_inc(s_eps, 1)

            @block.tensor
            def _(pe):
                pe.wait_ge(s_cst, 48)
                pe.wait_ge(s_xin, 16)
                for g in range(16):
                    if g >= 8:
                        pe.wait_ge(s_x_ev, g - 7)
                    for j in range(4):
                        last = nc.tensor.transpose(bank[:, g % 8, j * P:(j + 1) * P],
                                                   x_rows[:, 4 * (g % 2) + j, (g // 2) * P:(g // 2 + 1) * P],
                                                   c("ident"))
                    last.then_inc(s_x_tr, 1)

            @block.vector
            def _(dve):
                for g in range(16):
                    dve.wait_ge(s_x_tr, g + 1)
                    nc.vector.tensor_copy(xT[:, g // 2, (g % 2) * HALF:(g % 2 + 1) * HALF],
                                          bank[:, g % 8, :]).then_inc(s_x_ev, 1)
                dve.wait_ge(s_x_ev, 16)
                dve.wait_ge(s_eps, 1)

        scope.close()

        class Norm:
            squared, added, summed = sem("norm_squared"), sem("norm_added"), sem("norm_summed")
            averaged, rooted, spread_s = sem("norm_averaged"), sem("norm_rooted"), sem("norm_spread")
            scale, done, high = sem("norm_scale_ready"), sem("norm_done"), sem("norm_high")
            low = [sem("norm_low_even"), sem("norm_low_odd")]
            uses, splits = 0, 0

            def __init__(self, src, scratch, name, width, dst=None, parts=None):
                self.src, self.dst, self.parts, self.name, self.width = src, dst, parts, name, width
                self.sq = [scratch(width), scratch(width)]
                self.acc = scratch(width)
                self.blocks = width // P
                self.n0, self.s0 = Norm.uses, Norm.splits
                Norm.uses += 1
                Norm.splits += parts is not None

            def square(self, act, kt):
                if kt >= 2:
                    act.wait_ge(self.added, 7 * self.n0 + max(1, kt - 2))
                nc.scalar.activation(self.sq[kt % 2], self.src[:, kt], ACT.Square).then_inc(self.squared, 1)

            def add_square(self, dve, j):
                dve.wait_ge(self.squared, KT * self.n0 + j + 1)
                if j > 1:
                    dve.wait_ge(self.added, 7 * self.n0 + j - 1)
                nc.vector.tensor_add(self.acc, self.sq[0] if j == 1 else self.acc,
                                     self.sq[j % 2]).then_inc(self.added, 1)

            def act(self, act, between=None, after_square=None, squared_before=False):
                for kt in range(0 if not squared_before else KT, KT):
                    self.square(act, kt)
                    if after_square:
                        after_square(kt)
                if between:
                    between()
                if self.parts:
                    for kt in range(KT):
                        act.wait_ge(self.done, KT * self.n0 + kt + 1)
                        nc.scalar.activation(self.parts[0][:, kt], self.sq[kt % 2], ACT.Copy).then_inc(self.high, 1)

            def pool(self, pool):
                pool.wait_ge(self.averaged, self.n0 + 1)
                nb = self.blocks
                half = minus_half_c.rearrange("p (a b) -> p a b", b=2)
                nc.gpsimd.tensor_tensor(sums_root[:, 0:nb, 0:1], sums_in[:, 0:nb, 0:1], half[:, 0:nb, 0:1],
                                        ALU.pow).then_inc(self.rooted, 1)
                if self.parts:
                    for kt in range(0, KT, 2):
                        self.subtract_low(pool, nc.gpsimd, kt)

            def subtract_low(self, eng, ops, kt):
                eng.wait_ge(self.high, KT * self.s0 + kt + 1)
                ops.tensor_tensor(self.parts[1][:, kt], self.sq[kt % 2], self.parts[0][:, kt].bitcast(F32),
                                  ALU.subtract).then_inc(self.low[kt % 2], 1)

            def pe(self, pe):
                pe.wait_ge(self.added, 7 * self.n0 + 7)
                for n in range(self.blocks):
                    last = nc.tensor.matmul(bank[:, 6, 2 * n:2 * n + 2], self.acc[:, n * P:(n + 1) * P],
                                            c("ones")[:, 0:2], start=True, stop=True)
                last.then_inc(self.summed, 1)
                pe.wait_ge(self.spread_s, self.n0 + 1)
                for n in range(self.blocks):
                    last = nc.tensor.transpose(bank[:, 6 + n // 4, n % 4 * P:(n % 4 + 1) * P],
                                               self.acc[:, n * P:(n + 1) * P], c("ident"))
                last.then_inc(self.scale, 1)

            def dve(self, dve, squared_before=False):
                V, nb = nc.vector, self.blocks
                for j in range(1 if not squared_before else KT, KT):
                    self.add_square(dve, j)
                dve.wait_ge(self.summed, self.n0 + 1)
                V.tensor_scalar(sums_in[:, 0:nb], bank[:, 6, 0:2 * nb].rearrange("p (a b) -> p a b", b=2), 1.0 / D,
                                RMS_EPS, ALU.mult, ALU.add).then_inc(self.averaged, 1)
                dve.wait_ge(self.rooted, self.n0 + 1)
                V.tensor_copy(self.acc.rearrange("p (a b) -> p a b", b=P),
                              sums_root[:, 0:nb, 0:1].broadcast_to([P, nb, P])).then_inc(self.spread_s, 1)
                dve.wait_ge(self.scale, self.n0 + 1)
                factor = bank[:, 6:8, :].rearrange("p a b -> p (a b)")[:, 0:self.width]
                for kt in range(KT):
                    if self.parts and kt >= 2:
                        self.wait(dve, kt - 2)
                    V.scalar_tensor_tensor(out=self.sq[kt % 2] if self.parts else self.dst[:, kt],
                                           in0=self.src[:, kt], scalar=gain(self.name, kt), in1=factor,
                                           op0=ALU.mult, op1=ALU.mult).then_inc(self.done, 1)
                    if self.parts and kt % 2 == 0 and kt > 0:
                        self.subtract_low(dve, V, kt - 1)
                if self.parts:
                    self.subtract_low(dve, V, KT - 1)

            def wait(self, eng, kt=KT - 1):
                if self.parts:
                    eng.wait_ge(self.low[kt % 2], KT // 2 * self.s0 + kt // 2 + 1)
                else:
                    eng.wait_ge(self.done, KT * self.n0 + kt + 1)

        s_raw = [sem(f"ffn_weights_loaded{s}") for s in range(3)]
        s_high, s_low = sem("weights_high"), sem("weights_low")
        s_gu, s_silu, s_mult = sem("gate_up_ready"), sem("silu_done"), sem("gate_times_up")
        s_ah, s_al = sem("act_high"), sem("act_low")
        s_down, s_added = sem("down_ready"), sem("down_added")

        def ffn(done, w_gate, w_up, w_down, norm_name):
            GROUPS = NF // 2
            scope = ExitStack()
            open_ffn = Region(after_x)
            n_f32 = 3 * T + 2 * T + 3 * T
            work[0] = scope.enter_context(nc.sbuf_tensor(f"ffn_work{done}", [P, n_f32], F32))
            raw = [open_ffn(KT, P) for _ in range(3)]
            sg = open_ffn(2, T)

            def two_parts(name, *dims):
                return [scope.enter_context(nc.sbuf_tensor(f"{name}_{part}{done}", [P, *dims], F32R))
                        for part in ("high", "low")]

            h = two_parts("h", KT, T)
            w = two_parts("w", 6, KT, P)
            a = two_parts("a", 2, T)
            nrm = Norm(xT, open_ffn, norm_name, T, parts=h)
            wg, wu = panels(w_gate), panels(w_up)
            raw0, sp0, u0, d0 = done * GROUPS * 32, done * GROUPS * 6, done * GROUPS * 4, done * GROUPS * 16

            def flat(t):
                return t.rearrange("p a b -> p (a b)")

            def load(sp, g, i):
                dst = raw[i % 3]
                if i < 4:
                    src = (wg, wu)[i % 2][:, :, i // 2 * P:][:, :, ds(g * (2 * P), P)]
                else:
                    dst, src = flat(dst), w_down[(i - 4) * P:, :][ds(g * (2 * P), P), :]
                sp.dma_start(dst, src).then_inc(s_raw[i % 3], 16)

            with nc.Block() as block:
                @block.sync
                def _(sp):
                    for i in range(6):
                        if i >= 3:
                            sp.wait_ge(s_low, sp0 + i - 2)
                        load(sp, 0, i)
                    with sp.Fori(1, GROUPS) as g:
                        for i in range(6):
                            sp.wait_ge(s_low, g * 6 + (sp0 + i - 2))
                            load(sp, g, i)

                @block.gpsimd
                def _(pool):
                    if not done:
                        pool.sem_inc(s_gu, 4)
                        pool.sem_inc(s_down, 16)
                        pool.sem_inc(s_mult, 2)
                        pool.sem_inc(s_al, 4)
                        pool.sem_inc(s_added, 4)

                    def subtract_low(g, i):
                        pool.wait_ge(s_high, g * 6 + (sp0 + i + 1))
                        nc.gpsimd.tensor_tensor(w[1][:, i], raw[i % 3], w[0][:, i].bitcast(F32),
                                                ALU.subtract).then_inc(s_low, 1)

                    for i in range(3):
                        subtract_low(0, i)
                    nrm.pool(pool)
                    for i in range(3, 6):
                        subtract_low(0, i)
                    with pool.Fori(1, GROUPS) as g:
                        for i in range(6):
                            subtract_low(g, i)

                @block.tensor
                def _(pe):
                    mm = nc.tensor.matmul
                    nrm.pe(pe)
                    with pe.Fori(0, GROUPS) as g:
                        for f in range(2):
                            for n in range(2):
                                u = 2 * f + n
                                if n == 0:
                                    pe.wait_ge(s_low, g * 6 + (sp0 + 2 * f + 2))
                                pe.wait_ge(s_mult, g * 4 + (u0 + u + 1))
                                tok = slice(n * HALF, (n + 1) * HALF)
                                for b in range(2):
                                    for kt in range(KT):
                                        if u == 0 and b == 0:
                                            nrm.wait(pe, kt)
                                        for wp, hp in ((0, 0), (0, 1), (1, 0)):
                                            last = mm(bank[:, 2 * n + b, :], w[wp][:, 2 * f + b, kt],
                                                      h[hp][:, kt, tok], start=kt + wp + hp == 0,
                                                      stop=kt == KT - 1 and wp == 1)
                                last.then_inc(s_gu, 1)
                        for v in range(16):
                            n, o = v // 8, v % 8
                            tok = slice(n * HALF, (n + 1) * HALF)
                            if v == 0:
                                pe.wait_ge(s_low, g * 6 + (sp0 + 6))
                            if o == 0:
                                pe.wait_ge(s_al, g * 4 + (u0 + 4 + 3 + n))
                            pe.wait_ge(s_added, g * 16 + (d0 + v + 1))
                            for k in range(2):
                                for wp, ap in ((0, 0), (0, 1), (1, 0)):
                                    last = mm(bank[:, 4 + v % 4, :], w[wp][:, 4 + k, o], a[ap][:, k, tok],
                                              start=k + wp + ap == 0, stop=k == 1 and wp == 1)
                            last.then_inc(s_down, 1)

                @block.scalar
                def _(act):
                    A = nc.scalar.activation

                    def round_high(g, i):
                        act.wait_ge(s_raw[i % 3], g * 32 + (raw0 + i // 3 * 16 + 16))
                        if i < 4:
                            act.wait_ge(s_gu, g * 4 + (u0 + 2 + i // 2 * 2))
                        else:
                            act.wait_ge(s_down, g * 16 + (d0 + 16))
                        A(w[0][:, i], raw[i % 3], ACT.Copy).then_inc(s_high, 1)

                    def activate(g, f):
                        for n in range(2):
                            u = 2 * f + n
                            part = sg[:, f, n * HALF:(n + 1) * HALF]
                            act.wait_ge(s_gu, g * 4 + (u0 + 4 + u + 1))
                            act.wait_ge(s_al, g * 4 + (u0 + u + 1))
                            A(part, bank[:, 2 * n, :], ACT.Silu).then_inc(s_silu, 1)
                            act.wait_ge(s_mult, g * 4 + (u0 + 2 + u + 1))
                            act.wait_ge(s_down, g * 16 + (d0 + 16))
                            A(a[0][:, f, n * HALF:(n + 1) * HALF], part, ACT.Copy).then_inc(s_ah, 1)

                    def group(g, last):
                        for f in range(2):
                            activate(g, f)
                            if not last:
                                round_high(g + 1, 2 * f)
                                round_high(g + 1, 2 * f + 1)
                        if not last:
                            round_high(g + 1, 4)
                            round_high(g + 1, 5)

                    def first_panels(kt):
                        if 3 <= kt < 6:
                            round_high(0, kt - 3)

                    def other_panels():
                        for i in range(3, 6):
                            round_high(0, i)

                    nrm.act(act, other_panels, first_panels)
                    with act.Fori(0, GROUPS - 1) as g:
                        group(g, False)
                    group(GROUPS - 1, True)

                @block.vector
                def _(dve):
                    V = nc.vector
                    nrm.dve(dve)
                    with dve.Fori(0, GROUPS) as g:
                        for u in range(4):
                            f, n = u // 2, u % 2
                            tok = slice(n * HALF, (n + 1) * HALF)
                            dve.wait_ge(s_silu, g * 4 + (u0 + u + 1))
                            V.tensor_tensor(sg[:, f, tok], sg[:, f, tok], bank[:, 2 * n + 1, :],
                                            ALU.mult).then_inc(s_mult, 1)
                            dve.wait_ge(s_ah, g * 4 + (u0 + u + 1))
                            V.tensor_tensor(a[1][:, f, tok], sg[:, f, tok], a[0][:, f, tok].bitcast(F32),
                                            ALU.subtract).then_inc(s_al, 1)
                        for v in range(16):
                            n, o = v // 8, v % 8
                            xs = xT[:, o, n * HALF:(n + 1) * HALF]
                            dve.wait_ge(s_down, g * 16 + (d0 + 16 + v + 1))
                            V.scalar_tensor_tensor(out=xs, in0=bank[:, 4 + v % 4, :], scalar=0.5, in1=xs,
                                                   op0=ALU.mult, op1=ALU.add).then_inc(s_added, 1)
                    dve.wait_ge(s_added, d0 + 4 + GROUPS * 16)
            scope.close()

        ffn(0, d["w_gate1"], d["w_up1"], d["w_down1"], "ffn1_norm")

        scope = ExitStack()
        open_work(scope)
        w_in = panels(d["w_in"])
        hT_at = after_x
        r = Region(hT_at)
        hT = r(KT, T)
        kd = r(2, CH + T)
        v_win = r(T // CH, P)
        uT = r(T)
        ugT = r(T)
        shared_end = r.at

        def shared():
            s = Region(shared_end)
            nrm = Norm(xT, s, "mix_norm", T, dst=hT)
            w = Region(s.at)
            panel = [w(KT, P) for _ in range(5)]
            vT = w(CH + T)
            raw = w(2, T + 1)
            diff = w(T)
            s_pan = [sem(f"shared_panel_loaded{j}") for j in range(5)]
            s_ready, s_stored = sem("shared_ready"), sem("shared_stored")
            s_pad = sem("pads_zeroed")
            s_vt, s_vw = sem("v_transposed"), sem("v_windows_stored")
            s_mix, s_u = sem("low_rank_shift"), sem("low_rank_inputs_done")
            s_spill = sem("x_spilled")
            with nc.Block() as block:
                @block.sync
                def _(sp):
                    for j, name in enumerate(["ak", "ak", "av", "u", "ug"]):
                        if name == "ak":
                            for e in range(2):
                                at = COLS[name] + j * CH
                                sp.dma_start(panel[j][:, :, e * CH:(e + 1) * CH],
                                             w_in[:, :, at:at + CH]).then_inc(s_pan[j], 16)
                        else:
                            sp.dma_start(panel[j][:], w_in[:, :, COLS[name]:COLS[name] + P]).then_inc(s_pan[j], 16)
                    sp.dma_start(x_spill[:, :], xT[:].rearrange("p a b -> p (a b)")).then_inc(s_spill, 16)
                    sp.wait_ge(s_spill, 16)

                @block.gpsimd
                def _(pool):
                    nc.gpsimd.memset(kd[:, :, 0:CH], 0.0).then_inc(s_pad, 1)
                    nc.gpsimd.memset(vT[:, 0:CH], 0.0).then_inc(s_pad, 1)
                    nc.gpsimd.memset(raw[:, :, 0:1], 0.0).then_inc(s_pad, 1)
                    nrm.pool(pool)

                @block.tensor
                def _(pe):
                    nrm.pe(pe)
                    for j in range(5):
                        pe.wait_ge(s_pan[j], 32 if j < 2 else 16)
                        if j >= 3:
                            pe.wait_ge(s_stored, j - 2)
                        for kt in range(KT):
                            if j == 0:
                                nrm.wait(pe, kt)
                            for n in range(2):
                                last = nc.tensor.matmul(bank[:, 2 * (j % 3) + n, :], panel[j][:, kt],
                                                        hT[:, kt, n * HALF:(n + 1) * HALF],
                                                        start=kt == 0, stop=kt == KT - 1)
                        last.then_inc(s_ready, 1)
                    pe.wait_ge(s_pad, 3)
                    pe.wait_ge(s_stored, 5)
                    for g in range(4):
                        for j in range(4):
                            n = 4 * g + j
                            last = nc.tensor.transpose(bank[:, 4 + g, j * P:(j + 1) * P],
                                                       vT[:, n * CH:n * CH + P], c("ident"))
                        last.then_inc(s_vt, 1)

                @block.scalar
                def _(act):
                    nrm.act(act)
                    dst = [kd[:, 0, CH:], kd[:, 1, CH:], vT[:, CH:], raw[:, 0, 1:], raw[:, 1, 1:]]
                    for j in range(5):
                        act.wait_ge(s_ready, j + 1)
                        b = 2 * (j % 3)
                        nc.scalar.activation(dst[j], bank[:, b:b + 2, :].rearrange("p a b -> p (a b)"),
                                             ACT.Copy).then_inc(s_stored, 1)
                    act.wait_ge(s_mix, 2)
                    nc.scalar.activation(uT[0:CH, :], uT[0:CH, :], ACT.Tanh).then_inc(s_u, 1)
                    act.wait_ge(s_mix, 4)
                    nc.scalar.activation(ugT[:], ugT[:], ACT.Tanh, scale=0.5).then_inc(s_u, 1)

                @block.vector
                def _(dve):
                    nrm.dve(dve)
                    dve.wait_ge(s_pad, 3)
                    for j, dst in enumerate([uT, ugT]):
                        dve.wait_ge(s_stored, 4 + j)
                        nc.vector.tensor_sub(diff[:], raw[:, j, 0:T], raw[:, j, 1:T + 1]).then_inc(s_mix, 1)
                        dve.wait_ge(s_mix, 2 * j + 1)
                        nc.vector.scalar_tensor_tensor(out=dst[:], in0=diff[:], scalar=par_u[:, j:j + 1],
                                                       in1=raw[:, j, 1:T + 1], op0=ALU.mult,
                                                       op1=ALU.add).then_inc(s_mix, 1)
                        dve.wait_ge(s_mix, 2 * j + 2)
                    for g in range(4):
                        dve.wait_ge(s_vt, g + 1)
                        nc.vector.tensor_copy(v_win[:, 4 * g:4 * g + 4, :].rearrange("p a b -> p (a b)"),
                                              bank[:, 4 + g, :]).then_inc(s_vw, 1)
                    dve.wait_ge(s_vw, 4)
                    dve.wait_ge(s_u, 2)
                    nc.vector.tensor_scalar(ugT[:], ugT[:], 0.5, 0.5, ALU.mult, ALU.add).then_inc(s_u, 1)
                    dve.wait_ge(s_u, 3)

        shared()

        def mixer():
            own = ExitStack()
            a = Region(xT_at)
            panel = [a(KT, P) for _ in range(3)]
            q_bd, gaT, gbT, b_bd = a(2 * NC, P), a(T), a(T), a(NC, P)
            assert a.at <= after_x
            a2 = Region(shared_end)
            k_bd, a_bd, v_bd = a2(NC, P), a2(NC, P), a2(NC, P)
            b_tok, k_tok, v_tok = a2(NC, P), a2(NC, P), a2(NC, P)
            lak_bd, nm_bd, x_bd, xt_bd = a2(NC, P), a2(NC, P), a2(NC, P), a2(NC, P)
            zraw = a2(3, T + 1)
            lora = a2(3, P)
            ar = a2(NC, 2, CH)
            rm, km, vm, kp, g_out = a2(HALF), a2(HALF), a2(HALF), a2(HALF), a2(HALF)
            ld, cum, pin, pinv, pex = a2(HALF), a2(HALF), a2(HALF), a2(HALF), a2(HALF)
            kk, av, t1, t2 = a2(HALF), a2(HALF), a2(HALF), a2(HALF)
            b_st, v_st, mb, mk, n_st = a2(NC, CH), a2(NC, CH), a2(NC, CH), a2(NC, CH), a2(NC, CH)
            oa = a2(HALF)
            mrg = [a2(HALF) for _ in range(2)]
            alibi = a2(P)
            mx, es, den = a2(NC), a2(NC), a2(NC)
            root_in, root = a2(4, 2), a2(4, 2)
            minus_half = a2(4, 2)
            pp, half = a2(NPAR), a2(3)
            s_st, s_tmp, p1, sa_st = a2(CH), a2(CH), a2(CH), a2(CH)
            sa_bd = a2(P)
            s_bd = [a2(P) for _ in range(2)]

            def by_chunk(t):
                return t.rearrange("p (a b) -> p a b", a=NC)

            def flat(t):
                return t.rearrange("p a b -> p (a b)")

            xt_st, x_st, z_st = by_chunk(kk), by_chunk(av), by_chunk(pex)
            o_bd, prob, prob_t = xt_bd, k_tok, b_tok
            diff = [flat(mb), flat(mk), flat(n_st)]
            spread = flat(v_st).rearrange("p (a b c) -> p a b c", a=4, b=2)

            sems = {}

            def S(name):
                if name not in sems:
                    sems[name] = own.enter_context(nc.semaphore(name))
                return sems[name]

            def pv(name):
                i = PAR.index(name)
                return pp[:, i:i + 1]

            def hs(t, e):
                return t[e * CH:(e + 1) * CH]

            def bd(t, e, chunks=slice(0, NC)):
                return t[e * CH:(e + 1) * CH, chunks, e * CH:(e + 1) * CH]

            def bd1(t, e):
                return t[e * CH:(e + 1) * CH, e * CH:(e + 1) * CH]

            def over_chunks(m, n=NC):
                return m.unsqueeze(1).broadcast_to([m.shape[0], n, m.shape[1]])

            def two(bk):
                return bank[:, bk:bk + 2, :].rearrange("p a (c b) -> p (a c) b", b=P)

            def one(bk):
                return bank[:, bk, :].rearrange("p (c b) -> p c b", b=CH)

            PROJ = ["k", "r", "v", "q", "ga", "gb"]
            UNITS = 2 * len(PROJ)

            def job(unit):
                u = unit % UNITS
                return (u // 2, u % 2) if u < 8 else (4 + u % 2, (u - 8) // 2)

            s_slot = [sem(f"mix_panel_loaded{j}") for j in range(3)]
            s_lora = sem("lora_panels_loaded")
            s_zero = sem("mix_zeroed")
            s_mw = [sem(f"merged_written{h}") for h in range(2)]
            DVE_STEPS = 60
            GROUPS = [slice(0, NC // 2), slice(NC // 2, NC)]

            FILL = [{"scores": 1, "sums": 4, "scale": 2, "probs": 2, "values": 3, "back": 1, "tokens": 1,
                     "triangles": 5, "level": 1, "chunk": 1, "state": 1, "mean": 4, "var": 4, "end": 0},
                    {"scores": 0, "sums": 3, "scale": 2, "probs": 2, "values": 2, "back": 1, "tokens": 1,
                     "triangles": 5, "level": 2, "chunk": 1, "state": 1, "mean": 3, "var": 3, "end": 0}]
            LAST_FILL = {"sums": 2, "triangles": 1, "level": 1, "chunk": 1}
            PRE_UNITS = 2
            FIRST_UNIT = [8, UNITS + PRE_UNITS]

            class Filling:

                def __init__(self, h, last):
                    self.at, self.fill = 0, LAST_FILL if last else FILL[h]
                    self.first = 8 + 2 * h if last else FIRST_UNIT[h]
                    self.size = 2 * KT if last else KT * (FIRST_UNIT[1] - 8 if h == 0 else UNITS + 8 - FIRST_UNIT[1])

                def take(self, point):
                    n = self.fill.get(point, 0)
                    got = range(self.at, self.at + n)
                    self.at += n
                    return [(self.first + m // KT, m % KT) for m in got]

                def full(self):
                    return self.at == self.size

            with nc.Block() as block:
                @block.sync
                def _(sp):
                    def load(j, col):
                        sp.dma_start(panel[j % 3][:],
                                     w_in[:, :, COLS[PROJ[j]]:COLS[PROJ[j]] + D][:, :, ds(col, P)]).then_inc(
                                         s_slot[j % 3], 16)

                    def load_lora(col):
                        sp.dma_start(lora[0:CH, 0, :], d["w2"][:, ds(col, P)]).then_inc(s_lora, 16)
                        sp.dma_start(lora[CH:P, 1, :], d["a2"][:, ds(col, P)]).then_inc(s_lora, 16)
                        sp.dma_start(lora[:, 2, :], d["g2"][:, ds(col, P)]).then_inc(s_lora, 16)

                    def write_merged(p, h):
                        sp.wait_ge(S("merged_ready"), p * 2 + (h + 1))
                        sp.dma_start(m_spill[:, h * HALF:][:, ds(p * T, HALF)], mrg[h][:]).then_inc(s_mw[h], 16)

                    def load_after(j, col, used):
                        sp.wait_ge(S("proj_ready"), used)
                        load(j, col)

                    sp.wait_ge(s_zero, 1)
                    for j in range(3):
                        load(j, 0)
                    load_lora(0)
                    load_after(3, 0, 2)
                    load_after(4, 0, 4)
                    load_after(5, 0, 6)
                    with sp.Fori(0, PAIRS - 1) as p:
                        load_after(0, (p + 1) * P, p * UNITS + 8)
                        load_after(1, (p + 1) * P, p * UNITS + 11)
                        load_after(2, (p + 1) * P, p * UNITS + 12)
                        write_merged(p, 0)
                        load_after(3, p * P + P, p * UNITS + 14)
                        sp.wait_ge(S("lora_ready"), p * 2 + 2)
                        load_lora(p * P + P)
                        load_after(4, p * P + P, p * UNITS + (UNITS + 4))
                        load_after(5, p * P + P, p * UNITS + (UNITS + 6))
                        write_merged(p, 1)
                    for h in range(2):
                        write_merged(PAIRS - 1, h)
                    for h in range(2):
                        sp.wait_ge(s_mw[h], 16 * PAIRS + 16)

                @block.gpsimd
                def _(pool):
                    G = nc.gpsimd
                    G.memset(lora[:], 0.0).then_inc(s_zero, 1)
                    G.memset(zraw[:, :, 0:1], 0.0).then_inc(s_zero, 1)
                    G.memset(minus_half[:], -0.5).then_inc(s_zero, 1)
                    for t in (q_bd, b_bd, sa_bd, s_bd[0], s_bd[1]):
                        G.memset(t[:], 0.0).then_inc(s_zero, 1)
                    pool.wait_ge(s_zero, 15)
                    with pool.Fori(0, PAIRS) as p:
                        for h in range(2):
                            def wait(name, k=1, j=1):
                                pool.wait_ge(S(name), p * (2 * k) + (h * k + j))

                            for j in range(3):
                                if h == 0:
                                    pool.wait_ge(S("proj_stored"), p * UNITS + (2 + 2 * j + 2))
                                if h == 1 and j == 0:
                                    pool.wait_ge(S("y_stored"), p * 2 + 1)
                                if h == 0 and j == 0:
                                    pool.wait_ge(S("pair_done"), p + 1)
                                G.tensor_tensor(diff[j], zraw[:, j, h * HALF:(h + 1) * HALF],
                                                zraw[:, j, 1 + h * HALF:1 + (h + 1) * HALF],
                                                ALU.subtract).then_inc(S("diff_ready"), 1)
                            wait("kk_sums_stored")
                            G.tensor_tensor(root[:], root_in[:], minus_half[:], ALU.pow).then_inc(S("kk_rooted"), 1)
                            wait("cum_ready")
                            G.tensor_tensor(t1[:], cum[:], ld[:], ALU.subtract).then_inc(S("cum_before_ready"), 1)
                            for n, m in enumerate(LEVELS):
                                if n == 0:
                                    wait("n_stored")
                                else:
                                    wait("z_ready", 10, 2 * n)
                                for e in range(2):
                                    last = G.tensor_tensor(bd(nm_bd, e), hs(n_st, e),
                                                           over_chunks(hs(c(f"join{m}"), e)), ALU.mult)
                                last.then_inc(S("nm_ready"), 1)
                            wait("var_stored")
                            G.tensor_tensor(root[:], root_in[:], minus_half[:], ALU.pow).then_inc(S("var_rooted"), 1)

                @block.tensor
                def _(pe):
                    mm = nc.tensor.matmul

                    def per_chunk(out, lhs, rhs, chunks=range(NC)):
                        for i, n in enumerate(chunks):
                            last = mm(out[:, i, :], lhs[:, n, :], rhs(n), start=True, stop=True)
                        return last

                    def big(p, unit, kt):
                        j, n = job(unit)
                        if kt == 0:
                            if n == 0:
                                pe.wait_ge(s_slot[j % 3], p * 32 + (unit // UNITS * 32 + j // 3 * 16 + 16))
                            pe.wait_ge(S("proj_stored"), p * UNITS + (unit + 1))
                        last = mm(bank[:, unit % 2, :], panel[j % 3][:, kt], hT[:, kt, n * HALF:(n + 1) * HALF],
                                  start=kt == 0, stop=kt == KT - 1)
                        if kt == KT - 1:
                            last.then_inc(S("proj_ready"), 1)

                    def body(p, last_pair):
                        g = p // 4
                        for h in range(2):
                            tok = slice(h * HALF, (h + 1) * HALF)
                            filling = Filling(h, last_pair)

                            def wait(name, k=1, j=1):
                                pe.wait_ge(S(name), p * (2 * k) + (h * k + j))

                            def fill(point):
                                for unit, kt in filling.take(point):
                                    big(p, unit, kt)

                            if h == 0:
                                pe.wait_ge(S("proj_stored"), p * UNITS + 10)
                            for n in range(NC):
                                w0 = (h * NC + n) * CH
                                last = mm(two(2)[:, n, :], q_bd[:, h * NC + n, :],
                                          flat(kd)[:, ds(g * (CH + T) + w0, P)], start=True, stop=True)
                            last.then_inc(S("att_scores_ready"), 1)
                            fill("scores")
                            wait("km_ready")
                            if h == 0:
                                pe.wait_ge(s_lora, p * 48 + 48)
                            for n, src in enumerate((uT, uT, ugT)):
                                last = mm(bank[:, 5 + n, :], lora[:, n, :], src[:, tok], start=True, stop=True)
                            last.then_inc(S("lora_ready"), 1)
                            wait("kk_squared")
                            for n in range(4):
                                last = mm(bank[:, 4, 2 * n:2 * n + 2], t1[:, n * P:(n + 1) * P],
                                          c("bd_ones")[:, ::CH], start=True, stop=True)
                            last.then_inc(S("kk_summed"), 1)
                            fill("sums")
                            wait("kk_spread")
                            for n in range(4):
                                last = nc.tensor.transpose(bank[:, 4, n * P:(n + 1) * P],
                                                           spread[:, n].rearrange("p a b -> p (a b)"), c("ident"))
                            last.then_inc(S("kk_scale_ready"), 1)
                            fill("scale")
                            wait("att_exp_done")
                            for n in range(NC):
                                last = nc.tensor.transpose(two(2)[:, n, :], prob[:, n, :], c("ident"))
                            last.then_inc(S("probs_transposed"), 1)
                            fill("probs")
                            wait("prob_t_stored")
                            for n in range(NC):
                                last = mm(one(5)[:, n, :], prob_t[:, n, :],
                                          flat(v_win)[:, ds(g * CH + (h * NC + n) * P, CH)], start=True, stop=True)
                            last.then_inc(S("att_out_ready"), 1)
                            fill("values")
                            wait("o_bd_ready")
                            for n in range(NC):
                                last = nc.tensor.transpose(two(6)[:, n, :], o_bd[:, n, :], c("ident"))
                            last.then_inc(S("att_outT_ready"), 1)
                            fill("back")

                            wait("b_bd_ready")
                            for n in range(NC):
                                last = nc.tensor.transpose(two(2)[:, n, :], b_bd[:, n, :], c("ident"))
                            last.then_inc(S("b_tok_ready"), 1)
                            wait("k_bd_ready")
                            for n in range(NC):
                                last = nc.tensor.transpose(two(4)[:, n, :], k_bd[:, n, :], c("ident"))
                            last.then_inc(S("k_tok_ready"), 1)
                            wait("v_bd_ready")
                            wait("oa_stored")
                            for n in range(NC):
                                last = nc.tensor.transpose(two(6)[:, n, :], v_bd[:, n, :], c("ident"))
                            last.then_inc(S("v_tok_ready"), 1)
                            fill("tokens")
                            wait("a_bd_ready")
                            wait("b_tok_stored")
                            per_chunk(one(2), a_bd, lambda n: b_st[:, n, :]).then_inc(S("n_ready"), 1)
                            wait("k_tok_stored")
                            wait("ar_ready")
                            per_chunk(two(4), b_bd, lambda n: flat(ar[:, n])).then_inc(S("b_scores_ready"), 1)
                            wait("v_tok_stored")
                            per_chunk(two(6), k_bd, lambda n: flat(ar[:, n])).then_inc(S("k_scores_ready"), 1)
                            fill("triangles")

                            wait("k_scores_stored")
                            for n in range(5):
                                wait("nm_ready", 5, n + 1)
                                for q in range(2):
                                    if n == 0:
                                        wait("x0_ready")
                                    else:
                                        wait("xt_stored", 8, 2 * (n - 1) + q + 1)
                                    per_chunk(one(2 + q), nm_bd, lambda i: xt_st[:, i, :],
                                              range(4 * q, 4 * q + 4)).then_inc(S("z_ready"), 1)
                                if n > 0:
                                    for q in range(2):
                                        wait("xt_bd_upper_stored", 8, 2 * (n - 1) + q + 1)
                                        wait("xt_bd_lower_stored", 8, 2 * (n - 1) + q + 1)
                                        for i in range(4):
                                            last = nc.tensor.transpose(bank[:, 6 + q, i * P:(i + 1) * P],
                                                                       xt_bd[:, 4 * q + i, :], c("ident"))
                                        last.then_inc(S("xt_transposed"), 1)
                                fill("level")
                                for q in range(2):
                                    wait("z_stored", 10, 2 * n + q + 1)
                                    if n > 0:
                                        wait("x_bd_stored", 8, 2 * (n - 1) + q + 1)
                                    per_chunk(one(4 + q), x_bd, lambda i: z_st[:, i, :],
                                              range(4 * q, 4 * q + 4)).then_inc(S("xt_grown"), 1)
                            wait("rk_ready")
                            mm(bank[:, 7, :], c("bd_ones"), t2[:], start=True, stop=True).then_inc(S("bonus_ready"), 1)

                            def outputs(n):
                                pe.wait_ge(S("s_bd_ready"), p * 17 + (h * NC + n + 1))
                                wait("sa_bd_stored", NC, n + 1)
                                mm(one(6)[:, n, :], sa_bd[:], mb[:, n, :], start=True, stop=False)
                                mm(one(6)[:, n, :], v_tok[:, n, :], mk[:, n, :], start=False, stop=False)
                                mm(one(6)[:, n, :], s_bd[n % 2][:], ar[:, n, 1, :], start=False,
                                   stop=True).then_inc(S("y_ready"), 1)

                            wait("xt_bd_ready", 2, 2)
                            for n in range(NC):
                                pe.wait_ge(S("state_ready"), p * 17 + (h * NC + n + 1))
                                mm(bank[:, 2, 0:CH], a_bd[:, n, :], s_st[:], start=True, stop=False)
                                mm(bank[:, 2, 0:CH], lak_bd[:, n, :], v_st[:, n, :], start=False,
                                   stop=True).then_inc(S("p1_ready"), 1)
                                if n > 0:
                                    outputs(n - 1)
                                wait("p1_stored", NC, n + 1)
                                mm(bank[:, 3, 0:CH], xt_bd[:, n, :], p1[:], start=True,
                                   stop=True).then_inc(S("sa_ready"), 1)
                                fill("chunk")
                                wait("sa_stored", NC, n + 1)
                                mm(bank[:, 4, 0:CH], b_tok[:, n, :], sa_st[:], start=True, stop=False)
                                mm(bank[:, 4, 0:CH], k_tok[:, n, :], v_st[:, n, :], start=False,
                                   stop=True).then_inc(S("state_sum_ready"), 1)
                                fill("state")
                            outputs(NC - 1)

                            wait("y_stored")
                            mm(bank[:, 2, :], c("bd_ones"), ld[:], start=True, stop=True).then_inc(S("mean_ready"), 1)
                            fill("mean")
                            wait("yc_squared")
                            for n in range(4):
                                last = mm(bank[:, 4, 2 * n:2 * n + 2], t1[:, n * P:(n + 1) * P],
                                          c("bd_ones")[:, ::CH], start=True, stop=True)
                            last.then_inc(S("var_ready"), 1)
                            fill("var")
                            wait("var_spread")
                            for n in range(4):
                                last = nc.tensor.transpose(bank[:, 5, n * P:(n + 1) * P],
                                                           spread[:, n].rearrange("p a b -> p (a b)"), c("ident"))
                            last.then_inc(S("var_scale_ready"), 1)
                            fill("end")
                            assert filling.full()

                    for unit in range(8):
                        for kt in range(KT):
                            big(0, unit, kt)
                    pe.wait_ge(s_zero, 15)
                    with pe.Fori(0, PAIRS - 1) as p:
                        body(p, False)
                    body(PAIRS - 1, True)

                @block.scalar
                def _(act):
                    A = nc.scalar.activation

                    def store(p, unit):
                        j, n = job(unit)
                        src = bank[:, unit % 2, :]
                        tok = slice(n * HALF, (n + 1) * HALF)
                        act.wait_ge(S("proj_ready"), p * UNITS + (unit + 1))
                        if j < 3:
                            if unit == UNITS:
                                act.wait_ge(S("zraw_used"), p * 2 + 2)
                            i = A(zraw[:, j, 1 + n * HALF:1 + (n + 1) * HALF], src, ACT.Copy)
                        elif j == 3:
                            if unit > UNITS and n == 0:
                                act.wait_ge(S("att_scores_ready"), p * 2 + 2)
                            for e in range(2):
                                i = A(bd(q_bd, e, slice(n * NC, (n + 1) * NC)), hs(one(n), e), ACT.Copy)
                        else:
                            if n == 0:
                                act.wait_ge(S("pair_done"), p + 1)
                            i = A((gaT, gbT)[j - 4][:, tok], src, ACT.Tanh, scale=0.5)
                        i.then_inc(S("proj_stored"), 1)

                    def body(p, last_pair):
                        for h in range(2):
                            filling = Filling(h, last_pair)

                            def wait(name, k=1, j=1):
                                act.wait_ge(S(name), p * (2 * k) + (h * k + j))

                            def stores(point):
                                for unit, kt in filling.take(point):
                                    if kt == KT - 1 and (h == 1 or unit < UNITS):
                                        store(p, unit)

                            stores("scores")
                            wait("km_ready")
                            A(t1[:], km[:], ACT.Square, scale=pv("k_k")).then_inc(S("kk_squared"), 1)
                            A(kk[:], km[:], ACT.Copy, scale=pv("k_k")).then_inc(S("kk_unscaled"), 1)
                            if h == 1 and not last_pair:
                                for unit in range(UNITS, FIRST_UNIT[1]):
                                    store(p, unit)
                            wait("lora_ready")
                            A(ld[:], bank[:, 5, :], ACT.Tanh, bias=half[:, 0:1],
                              scale=0.5).then_inc(S("decay_tanh"), 1)
                            A(av[:], bank[:, 6, :], ACT.Tanh, bias=half[:, 1:2], scale=0.5)
                            A(g_out[:], bank[:, 7, :], ACT.Copy, scale=0.5).then_inc(S("lora_stored"), 1)
                            wait("decay_tanh")
                            A(ld[:], ld[:], ACT.Copy, bias=C_DECAY, scale=C_DECAY).then_inc(S("ld_ready"), 1)
                            wait("vm_ready")
                            for e in range(2):
                                last = A(bd(v_bd, e), hs(by_chunk(vm), e), ACT.Copy)
                            last.then_inc(S("v_bd_ready"), 1)
                            stores("sums")
                            wait("att_shifted")
                            A(flat(prob), flat(prob), ACT.Exp)
                            A(es[:], mx[:], ACT.Exp, bias=pv("sink"), scale=-1.0).then_inc(S("att_exp_done"), 1)
                            wait("cum_ready")
                            A(pin[:], cum[:], ACT.Exp)
                            A(pinv[:], cum[:], ACT.Exp, scale=-1.0).then_inc(S("inverse_decay_ready"), 1)
                            wait("cum_before_ready")
                            A(pex[:], t1[:], ACT.Exp).then_inc(S("exp_done"), 1)
                            stores("scale")
                            wait("probs_transposed")
                            A(flat(prob_t), flat(bank[:, 2:4, :]), ACT.Copy).then_inc(S("prob_t_stored"), 1)
                            stores("probs")
                            stores("values")
                            wait("att_outT_ready")
                            for e in range(2):
                                last = A(hs(by_chunk(oa), e), bd(two(6), e), ACT.Copy, scale=0.5)
                            last.then_inc(S("oa_stored"), 1)
                            stores("back")
                            wait("b_tok_ready")
                            A(flat(b_tok), flat(bank[:, 2:4, :]), ACT.Copy).then_inc(S("b_tok_stored"), 1)
                            wait("a_st_ready")
                            for e in range(2):
                                last = A(bd(a_bd, e), hs(ar, e)[:, :, 0, :], ACT.Copy)
                            last.then_inc(S("a_bd_ready"), 1)
                            wait("v_tok_ready")
                            for e in range(2):
                                A(hs(v_st, e), bd(two(6), e), ACT.Copy)
                            A(flat(v_tok), flat(bank[:, 6:8, :]), ACT.Copy).then_inc(S("v_tok_stored"), 1)
                            stores("tokens")
                            stores("triangles")
                            for n in range(5):
                                if n > 0:
                                    for q in range(2):
                                        wait("xt_transposed", 8, 2 * (n - 1) + q + 1)
                                        A(flat(x_bd[:, GROUPS[q]]), bank[:, 6 + q, :],
                                          ACT.Copy).then_inc(S("x_bd_stored"), 1)
                                stores("level")
                                if n < 4:
                                    for q in range(2):
                                        wait("xt_stored", 8, 2 * n + q + 1)
                                        A(bd(xt_bd, 1, GROUPS[q]), hs(xt_st, 1)[:, GROUPS[q]],
                                          ACT.Copy).then_inc(S("xt_bd_lower_stored"), 1)

                            for n in range(NC):
                                wait("sa_stored", NC, n + 1)
                                if n > 0 or h > 0:
                                    wait("y_ready", NC, n)
                                for e in range(2):
                                    last = A(bd1(sa_bd, e), hs(sa_st, e), ACT.Copy)
                                last.then_inc(S("sa_bd_stored"), 1)
                                stores("chunk")
                                wait("state_added", NC, n + 1)
                                for e in range(2):
                                    last = A(bd1(s_bd[(n + 1) % 2], e), hs(s_tmp, e), ACT.Copy,
                                             scale=hs(pin, e)[:, n * CH + CH - 1:n * CH + CH])
                                last.then_inc(S("s_bd_ready"), 1)
                                stores("state")

                            wait("y_ready", NC, NC)
                            A(ld[:], bank[:, 6, :], ACT.Copy).then_inc(S("y_stored"), 1)
                            stores("mean")
                            wait("yc_ready")
                            A(t1[:], cum[:], ACT.Square).then_inc(S("yc_squared"), 1)
                            stores("var")
                            wait("y_normed")
                            A(cum[:], cum[:], ACT.Identity, bias=pv("ln_b"), scale=pv("ln_w")).then_inc(
                                S("y_affine"), 1)
                            stores("end")

                    act.wait_ge(s_zero, 15)
                    for unit in range(8):
                        store(0, unit)
                    with act.Fori(0, PAIRS - 1) as p:
                        body(p, False)
                    body(PAIRS - 1, True)

                @block.vector
                def _(dve):
                    V = nc.vector
                    dve.sem_inc(S("proj_stored"), 2)
                    dve.sem_inc(S("pair_done"), 1)
                    for h in range(2):
                        dve.sem_inc(s_mw[h], 16)
                    dve.wait_ge(s_zero, 1)
                    for t in (k_bd, a_bd, v_bd, lak_bd, nm_bd, x_bd, xt_bd):
                        V.memset(t[:], 0.0).then_inc(s_zero, 1)
                    dve.wait_ge(s_zero, 15)
                    with dve.Fori(0, PAIRS) as p:
                        step = [0]

                        def link(ins):
                            step[0] += 1
                            ins.then_inc(S("dve_step"), 1)
                            dve.wait_ge(S("dve_step"), p * DVE_STEPS + step[0])

                        link(V.tensor_copy(pp[:], par[:, :, ds(p, 1)].rearrange("p a b -> p (a b)")))
                        for i, name in enumerate(("w0", "a0", "k_a")):
                            link(V.tensor_scalar(half[:, i:i + 1], pv(name), 0.5, None, ALU.mult))
                        link(V.tensor_scalar(alibi[:], c("dist"), c("neg_slope")[:, ds(p, 1)], None, ALU.mult))
                        V.memset(s_st[:], 0.0).then_inc(S("state_ready"), 1)
                        for e in range(2):
                            last = V.memset(bd1(s_bd[0], e), 0.0)
                        last.then_inc(S("s_bd_ready"), 1)

                        for h in range(2):
                            def wait(name, k=1, j=1):
                                dve.wait_ge(S(name), p * (2 * k) + (h * k + j))

                            def both(f, name=None):
                                for e in range(2):
                                    last = f(e)
                                    if e == 0 or name is None:
                                        link(last)
                                    else:
                                        last.then_inc(S(name), 1)

                            tok = slice(h * HALF, (h + 1) * HALF)
                            for j, (dst, mu, name) in enumerate(((km, "mu_k", "km_ready"), (rm, "mu_r", None),
                                                                 (vm, "mu_v", "vm_ready"))):
                                wait("diff_ready", 3, j + 1)
                                mixed = V.scalar_tensor_tensor(out=dst[:], in0=diff[j], scalar=pv(mu),
                                                               in1=zraw[:, j, 1 + h * HALF:1 + (h + 1) * HALF],
                                                               op0=ALU.mult, op1=ALU.add)
                                if name:
                                    mixed.then_inc(S(name), 1)
                            dve.wait_ge(S("vm_ready"), p * 2 + (h + 1))
                            dve.sem_inc(S("zraw_used"), 1)

                            wait("att_scores_ready")
                            link(V.scalar_tensor_tensor(out=prob[:], in0=two(2), scalar=0.125,
                                                        in1=over_chunks(alibi), op0=ALU.mult, op1=ALU.add))
                            if h == 0:
                                link(V.memset(prob[:, 0, 0:CH], -1e30))
                            link(V.tensor_reduce(mx[:], prob[:], AX.X, ALU.max))
                            link(V.tensor_scalar(mx[:], mx[:], pv("sink"), None, ALU.max))
                            V.tensor_tensor(prob[:], prob[:], mx.unsqueeze(2).broadcast_to([P, NC, P]),
                                            ALU.subtract).then_inc(S("att_shifted"), 1)

                            wait("kk_summed")
                            V.tensor_scalar(root_in[:], bank[:, 4, 0:8].rearrange("p (a b) -> p a b", a=4), 1e-24,
                                            None, ALU.max).then_inc(S("kk_sums_stored"), 1)
                            wait("ld_ready")
                            V.tensor_tensor_scan(cum[:], c("keep"), ld[:], 0.0, ALU.mult,
                                                 ALU.add).then_inc(S("cum_ready"), 1)
                            wait("kk_rooted")
                            V.tensor_copy(spread, root[:].unsqueeze(3).broadcast_to([P, 4, 2, CH])).then_inc(
                                S("kk_spread"), 1)
                            wait("lora_stored")
                            link(V.tensor_scalar(t2[:], av[:], 1.0, half[:, 2:3], ALU.subtract, ALU.mult))
                            link(V.scalar_tensor_tensor(out=kp[:], in0=t2[:], scalar=1.0, in1=km[:], op0=ALU.add,
                                                        op1=ALU.mult))
                            wait("kk_unscaled")
                            wait("kk_scale_ready")
                            link(V.tensor_tensor(kk[:], bank[:, 4, :], kk[:], ALU.mult))
                            link(V.scalar_tensor_tensor(out=t2[:], in0=av[:], scalar=1.0, in1=kk[:], op0=ALU.add,
                                                        op1=ALU.mult))
                            wait("inverse_decay_ready")
                            link(V.scalar_tensor_tensor(out=flat(b_st), in0=t2[:], scalar=0.5, in1=pinv[:],
                                                        op0=ALU.mult, op1=ALU.mult))
                            both(lambda e: V.tensor_copy(bd(b_bd, e), hs(b_st, e)), "b_bd_ready")
                            wait("att_exp_done")
                            link(V.tensor_reduce(den[:], prob[:], AX.X, ALU.add))
                            link(V.tensor_add(den[:], den[:], es[:]))
                            link(V.reciprocal(den[:], den[:]))
                            wait("exp_done")
                            V.scalar_tensor_tensor(out=ar[:, :, 0, :], in0=by_chunk(kk), scalar=-1.0,
                                                   in1=by_chunk(pex), op0=ALU.mult,
                                                   op1=ALU.mult).then_inc(S("a_st_ready"), 1)
                            V.tensor_mul(ar[:, :, 1, :], by_chunk(rm), by_chunk(pin)).then_inc(S("ar_ready"), 1)
                            wait("att_out_ready")
                            both(lambda e: V.tensor_tensor(bd(o_bd, e), one(5)[e * CH:(e + 1) * CH],
                                                           hs(den, e).unsqueeze(2).broadcast_to([CH, NC, CH]),
                                                           ALU.mult), "o_bd_ready")
                            both(lambda e: V.tensor_mul(bd(k_bd, e), hs(by_chunk(kp), e), hs(by_chunk(pinv), e)),
                                 "k_bd_ready")
                            wait("k_tok_ready")
                            V.tensor_copy(flat(k_tok), flat(bank[:, 4:6, :])).then_inc(S("k_tok_stored"), 1)

                            ident8 = over_chunks(c("stack_ident"))
                            wait("n_ready")
                            V.tensor_tensor(n_st, one(2), over_chunks(c("col_before_row")),
                                            ALU.mult).then_inc(S("n_stored"), 1)
                            wait("n_stored")
                            link(V.tensor_tensor(x_st, n_st, over_chunks(c("join1")), ALU.mult))
                            link(V.tensor_tensor(x_st, x_st, ident8, ALU.add))
                            both(lambda e: V.tensor_copy(bd(x_bd, e), hs(x_st, e)))
                            wait("b_scores_ready")
                            link(V.tensor_tensor(xt_st, two(4)[:, :, 0:CH], over_chunks(c("join1T")), ALU.mult))
                            link(V.tensor_tensor(xt_st, xt_st, ident8, ALU.add))
                            V.tensor_tensor(mb, two(4)[:, :, CH:P], over_chunks(c("row_upto_col")),
                                            ALU.mult).then_inc(S("x0_ready"), 1)
                            wait("k_scores_ready")
                            both(lambda e: V.tensor_tensor(bd(lak_bd, e), hs(two(6), e)[:, :, 0:CH],
                                                           over_chunks(hs(c("row_before_col"), e)), ALU.mult))
                            V.tensor_tensor(mk, two(6)[:, :, CH:P], over_chunks(c("row_upto_col")),
                                            ALU.mult).then_inc(S("k_scores_stored"), 1)
                            V.scalar_tensor_tensor(out=t2[:], in0=rm[:], scalar=pv("r_k"), in1=kp[:], op0=ALU.mult,
                                                   op1=ALU.mult).then_inc(S("rk_ready"), 1)
                            for n in range(5):
                                for q, sl in enumerate(GROUPS):
                                    wait("z_ready", 10, 2 * n + q + 1)
                                    V.tensor_copy(z_st[:, sl], one(2 + q)[:, 0:NC // 2]).then_inc(S("z_stored"), 1)
                                for q, sl in enumerate(GROUPS):
                                    wait("xt_grown", 10, 2 * n + q + 1)
                                    if n == 4:
                                        for e in range(2):
                                            last = V.tensor_tensor(bd(xt_bd, e, sl), hs(one(4 + q), e)[:, 0:NC // 2],
                                                                   hs(xt_st, e)[:, sl], ALU.add)
                                        last.then_inc(S("xt_bd_ready"), 1)
                                        continue
                                    V.tensor_tensor(xt_st[:, sl], one(4 + q)[:, 0:NC // 2], xt_st[:, sl],
                                                    ALU.add).then_inc(S("xt_stored"), 1)
                                    wait("xt_stored", 8, 2 * n + q + 1)
                                    V.tensor_copy(bd(xt_bd, 0, sl), hs(xt_st, 0)[:, sl]).then_inc(
                                        S("xt_bd_upper_stored"), 1)
                            wait("bonus_ready")
                            link(V.tensor_tensor(vm[:], bank[:, 7, :], vm[:], ALU.mult))

                            for n in range(NC):
                                wait("p1_ready", NC, n + 1)
                                V.tensor_copy(p1[:], bank[:, 2, 0:CH]).then_inc(S("p1_stored"), 1)
                                wait("sa_ready", NC, n + 1)
                                if n > 0 or h > 0:
                                    wait("sa_bd_stored", NC, n)
                                V.tensor_copy(sa_st[:], bank[:, 3, 0:CH]).then_inc(S("sa_stored"), 1)
                                wait("state_sum_ready", NC, n + 1)
                                if n > 0 or h > 0:
                                    dve.wait_ge(S("s_bd_ready"), p * 17 + (h * NC + n + 1))
                                V.tensor_tensor(s_tmp[:], bank[:, 4, 0:CH], s_st[:],
                                                ALU.add).then_inc(S("state_added"), 1)
                                wait("state_added", NC, n + 1)
                                V.tensor_scalar(s_st[:], s_tmp[:], pin[:, n * CH + CH - 1:n * CH + CH], None,
                                                ALU.mult).then_inc(S("state_ready"), 1)

                            wait("mean_ready")
                            V.scalar_tensor_tensor(out=cum[:], in0=bank[:, 2, :], scalar=-1.0 / CH, in1=ld[:],
                                                   op0=ALU.mult, op1=ALU.add).then_inc(S("yc_ready"), 1)
                            wait("var_ready")
                            V.tensor_scalar(root_in[:], bank[:, 4, 0:8].rearrange("p (a b) -> p a b", a=4),
                                            1.0 / CH, GN_EPS, ALU.mult, ALU.add).then_inc(S("var_stored"), 1)
                            wait("var_rooted")
                            V.tensor_copy(spread, root[:].unsqueeze(3).broadcast_to([P, 4, 2, CH])).then_inc(
                                S("var_spread"), 1)
                            wait("var_scale_ready")
                            V.tensor_tensor(cum[:], bank[:, 5, :], cum[:], ALU.mult).then_inc(S("y_normed"), 1)
                            dve.wait_ge(S("proj_stored"), p * UNITS + (12 + 2 * h))
                            wait("oa_stored")
                            link(V.scalar_tensor_tensor(out=oa[:], in0=gaT[:, tok], scalar=1.0, in1=oa[:],
                                                        op0=ALU.add, op1=ALU.mult))
                            link(V.scalar_tensor_tensor(out=g_out[:], in0=gbT[:, tok], scalar=1.0, in1=g_out[:],
                                                        op0=ALU.add, op1=ALU.mult))
                            wait("y_affine")
                            link(V.tensor_add(cum[:], cum[:], vm[:]))
                            link(V.tensor_mul(cum[:], cum[:], g_out[:]))
                            dve.wait_ge(s_mw[h], p * 16 + 16)
                            V.tensor_add(mrg[h][:], cum[:], oa[:]).then_inc(S("merged_ready"), 1)
                            wait("merged_ready")
                        dve.sem_inc(S("pair_done"), 1)
                        assert step[0] == DVE_STEPS, f"DVE_STEPS {step[0]}"

            with nc.Block() as block:
                @block.sync
                def _(sp):
                    for used in sems.values():
                        sp.sem_clear(used)
            own.close()

        mixer()

        def finish():
            scope = ExitStack()
            open_work(scope)
            r = Region(after_x)
            yT, rows = r(KT, T), r(8, D)
            nrm = Norm(xT, r, "final_norm", T, dst=yT)
            s_tr, s_ev, s_out = s_x_tr, s_x_ev, sem("out_written")
            with nc.Block() as block:
                @block.sync
                def _(sp):
                    for t in range(8):
                        sp.wait_ge(s_ev, 16 + 2 * t + 2)
                        sp.dma_start(out[t * P:(t + 1) * P, :], rows[:, t, :]).then_inc(s_out, 16)
                    sp.wait_ge(s_out, 128)

                @block.gpsimd
                def _(pool):
                    nrm.pool(pool)

                @block.scalar
                def _(act):
                    nrm.act(act)

                @block.tensor
                def _(pe):
                    nrm.pe(pe)
                    nrm.wait(pe)
                    for g in range(16):
                        if g >= 6:
                            pe.wait_ge(s_ev, 16 + g - 5)
                        for j in range(4):
                            kt = 4 * (g % 2) + j
                            last = nc.tensor.transpose(bank[:, g % 6, j * P:(j + 1) * P],
                                                       yT[:, kt, (g // 2) * P:(g // 2 + 1) * P], c("ident"))
                        last.then_inc(s_tr, 1)

                @block.vector
                def _(dve):
                    nrm.dve(dve)
                    for g in range(16):
                        dve.wait_ge(s_tr, 16 + g + 1)
                        nc.vector.tensor_copy(rows[:, g // 2, (g % 2) * HALF:(g % 2 + 1) * HALF],
                                              bank[:, g % 6, :]).then_inc(s_ev, 1)
            scope.close()
        scope.close()

        def cross():
            scope = ExitStack()
            part_words = 2 * (KT * T + 2 * KT * P)
            f32_words = SBUF_WORDS - BASE - part_words
            work[0] = scope.enter_context(nc.sbuf_tensor("cross_work", [P, f32_words], F32))

            def two_parts(name, *dims):
                return [scope.enter_context(nc.sbuf_tensor(f"{name}_{part}", [P, *dims], F32R))
                        for part in ("high", "low")]

            src = two_parts("source", KT, T)
            pw = two_parts("panel", 2, KT, P)
            r = Region(after_x)
            oT = r(KT, T)
            raw = [r(KT, P) for _ in range(2)]
            kT, v_all = r(2 * XH, NMEM), r(MT, D)
            rm_ = Region(r.at)
            mem_rows, memT = rm_(MT, D), rm_(KT, NMEM)
            kv_w = [rm_(KT, P) for _ in range(3)]
            nm = Norm(memT, rm_, "mem_norm", NMEM, dst=memT)
            rc = Region(r.at)
            qh, vh, mx, den = rc(2, T), rc(MT, NMEM), rc(8), rc(8)
            rn = Region(rc.at)
            prob, prob_t = rc(8, NMEM), rc(MT, T)
            nx = Norm(xT, rn, "cross_norm", T, parts=src)
            assert max(rm_.at, rc.at, rn.at) <= BASE + f32_words
            s_in, s_tr, s_ev = sem("mem_loaded"), sem("mem_transposed"), sem("mem_stored")
            s_kvw = [sem(f"kv_panel_loaded{j}") for j in range(3)]
            s_kv, s_kvs = sem("kv_ready"), sem("kv_stored")
            s_merged = [sem(f"merged_reloaded{j}") for j in range(2)]
            s_x = sem("x_reloaded")
            s_pan = [sem(f"cross_panel_loaded{j}") for j in range(2)]
            s_whigh, s_wlow, s_ready = sem("panel_high"), sem("panel_low"), sem("panel_products_ready")
            s_shigh, s_slow, s_padd = sem("source_high"), sem("source_low"), sem("project_added")
            w_out, w_co, wq, wkv = panels(d["w_out"]), panels(d["w_co"]), panels(d["w_cq"]), panels(d["w_ckv"])

            def flat(t):
                return t.rearrange("p a b -> p (a b)")

            def load(sp, slot, view):
                sp.dma_start(raw[slot][:], view).then_inc(s_pan[slot], 16)

            def round_high(act, slot, k, pair):
                act.wait_ge(s_pan[slot], pair * 16 + 16)
                if not (isinstance(k, int) and k < 2):
                    act.wait_ge(s_ready, k - 1)
                nc.scalar.activation(pw[0][:, slot], raw[slot][:], ACT.Copy).then_inc(s_whigh, 1)

            def subtract_low(pool, slot, k):
                pool.wait_ge(s_whigh, k + 1)
                nc.gpsimd.tensor_tensor(pw[1][:, slot], raw[slot][:], pw[0][:, slot].bitcast(F32),
                                        ALU.subtract).then_inc(s_wlow, 1)

            def round_source(act, n, kt):
                nc.scalar.activation(src[0][:, kt], oT[:, kt], ACT.Copy).then_inc(s_shigh, 1)

            def subtract_source(pool, n, kt):
                pool.wait_ge(s_shigh, KT * n + kt + 1)
                nc.gpsimd.tensor_tensor(src[1][:, kt], oT[:, kt], src[0][:, kt].bitcast(F32),
                                        ALU.subtract).then_inc(s_slow, 1)

            EARLY = 2 * (XH - 1)

            THREE = ((0, 0), (0, 1), (1, 0))

            with nc.Block() as block:
                @block.sync
                def _(sp):
                    def load_kv(j):
                        sp.dma_start(kv_w[j % 3][:], wkv[:, :, j * P:(j + 1) * P]).then_inc(s_kvw[j % 3], 16)

                    sp.dma_start(mem_rows[:], d["mem"].rearrange("(t p) c -> p t c", p=P)).then_inc(s_in, 16)
                    for j in range(3):
                        load_kv(j)
                    for j in range(2):
                        load(sp, j, w_out[:, :, j * P:(j + 1) * P])
                        sp.dma_start(flat(oT[:, 4 * j:4 * j + 4, :]),
                                     m_spill[:, 4 * j * T:4 * (j + 1) * T]).then_inc(s_merged[j], 16)
                    for j in range(3, 16):
                        sp.wait_ge(s_kv, j - 2)
                        load_kv(j)
                    sp.dma_start(flat(xT), x_spill[:, :]).then_inc(s_x, 16)

                @block.tensor
                def _(pe):
                    pe.wait_ge(s_in, 16)
                    for g in range(4):
                        for j in range(4):
                            kt = 2 * g + j // 2
                            last = nc.tensor.transpose(bank[:, g, j * P:(j + 1) * P],
                                                       mem_rows[:, j % 2, kt * P:(kt + 1) * P], c("ident"))
                        last.then_inc(s_tr, 1)
                    nm.pe(pe)
                    nm.wait(pe)
                    for j in range(16):
                        pe.wait_ge(s_kvw[j % 3], 16 * (j // 3 + 1))
                        if j >= 6:
                            pe.wait_ge(s_kvs, j - 5)
                        w = kv_w[j % 3]
                        for m in range(1 if j < 8 else MT):
                            for kt in range(KT):
                                if j < 8:
                                    o, lhs, rhs = bank[:, j % 6, 0:NMEM], w[:, kt], memT[:, kt, :]
                                else:
                                    o, lhs, rhs = (bank[:, j % 6, m * P:(m + 1) * P], memT[:, kt, m * P:(m + 1) * P],
                                                   w[:, kt])
                                last = nc.tensor.matmul(o, lhs, rhs, start=kt == 0, stop=kt == KT - 1)
                        last.then_inc(s_kv, 1)

                @block.gpsimd
                def _(pool):
                    nm.pool(pool)
                    subtract_low(pool, 0, 0)
                    for kt in range(KT):
                        subtract_source(pool, 0, kt)
                        if kt == 3:
                            subtract_low(pool, 1, 1)

                @block.scalar
                def _(act):
                    act.wait_ge(s_ev, 4)
                    nm.act(act)
                    round_high(act, 0, 0, 0)
                    for j in range(16):
                        if 2 <= j < 2 + KT:
                            if (j - 2) % 4 == 0:
                                act.wait_ge(s_merged[(j - 2) // 4], 16)
                            round_source(act, 0, j - 2)
                        if j == 6:
                            round_high(act, 1, 1, 0)
                        act.wait_ge(s_kv, j + 1)
                        src_bank = bank[:, j % 6, 0:NMEM]
                        if j < 8:
                            nc.scalar.activation(kT[:, j, :], src_bank, ACT.Copy).then_inc(s_kvs, 1)
                        else:
                            nc.scalar.activation(v_all[:, :, (j - 8) * P:(j - 7) * P],
                                                 src_bank.rearrange("p (a b) -> p a b", b=P),
                                                 ACT.Copy).then_inc(s_kvs, 1)

                @block.vector
                def _(dve):
                    for g in range(4):
                        dve.wait_ge(s_tr, g + 1)
                        nc.vector.tensor_copy(flat(memT[:, 2 * g:2 * g + 2, :]), bank[:, g, :]).then_inc(s_ev, 1)
                    nm.dve(dve)
                    nm.wait(dve)

            def project(done, w):
                k0 = 16 * done
                with nc.Block() as block:
                    @block.sync
                    def _(sp):
                        for o in range(2, KT):
                            sp.wait_ge(s_wlow, k0 + o - 1)
                            load(sp, o % 2, w[:, :, o * P:(o + 1) * P])
                        if not done:
                            for t in range(2):
                                sp.wait_ge(s_wlow, k0 + KT + t - 1)
                                load(sp, t, wq[:, :, t * P:(t + 1) * P])

                    @block.scalar
                    def _(act):
                        for kt in range(EARLY if done else KT, KT):
                            round_source(act, 1, kt)
                        for o in range(2, KT + 2):
                            if o < KT:
                                round_high(act, o % 2, k0 + o, k0 // 2 + o // 2)
                            if not done:
                                act.wait_ge(s_padd, o - 1)
                                nx.square(act, o - 2)

                    @block.gpsimd
                    def _(pool):
                        for kt in range(EARLY if done else KT, KT):
                            subtract_source(pool, 1, kt)
                        for o in range(2, KT):
                            subtract_low(pool, o % 2, k0 + o)

                    @block.tensor
                    def _(pe):
                        for o in range(KT):
                            pe.wait_ge(s_wlow, k0 + o + 1)
                            if o >= 4:
                                pe.wait_ge(s_padd, KT * done + o - 3)
                            for kt in range(KT):
                                if o == 0:
                                    pe.wait_ge(s_slow, KT * done + kt + 1)
                                for n in range(2):
                                    for wp, hp in THREE:
                                        last = nc.tensor.matmul(bank[:, 2 * (o % 4) + n, :], pw[wp][:, o % 2, kt],
                                                                src[hp][:, kt, n * HALF:(n + 1) * HALF],
                                                                start=kt + wp + hp == 0,
                                                                stop=kt == KT - 1 and wp == 1)
                            last.then_inc(s_ready, 1)

                    @block.vector
                    def _(dve):
                        if not done:
                            dve.wait_ge(s_x, 16)
                        for o in range(KT):
                            dve.wait_ge(s_ready, k0 + o + 1)
                            nc.vector.tensor_tensor(xT[:, o, :], flat(bank[:, 2 * (o % 4):2 * (o % 4) + 2, :]),
                                                    xT[:, o, :], ALU.add).then_inc(s_padd, 1)
                            if not done and o >= 2:
                                nx.add_square(dve, o - 1)
                        if not done:
                            nx.add_square(dve, KT - 1)
                        dve.wait_ge(s_padd, KT * done + KT)

            project(0, w_out)

            s_qs, s_vs = sem("cross_q_stored"), sem("cross_v_stored")
            s_sc, s_sh, s_exp, s_norm = sem("cross_scores"), sem("cross_shifted"), sem("cross_exp"), sem("cross_probs")
            s_pt, s_pts, s_o, s_os = (sem("cross_probs_transposed"), sem("cross_probs_t_stored"), sem("cross_out"),
                                      sem("cross_out_stored"))
            s_step = sem("cross_dve_step")
            with nc.Block() as block:
                @block.sync
                def _(sp):
                    with sp.Fori(1, XH) as i:
                        for t in range(2):
                            sp.wait_ge(s_wlow, i * 2 + (KT + t - 1))
                            load(sp, t, wq[:, :, t * P:][:, :, ds(i * NMEM, P)])
                    for t in range(2):
                        sp.wait_ge(s_wlow, 2 * KT + t - 1)
                        load(sp, t, w_co[:, :, t * P:(t + 1) * P])

                @block.tensor
                def _(pe):
                    mm = nc.tensor.matmul

                    def project_q(i, t, first):
                        pe.wait_ge(s_wlow, i * 2 + (KT + t + 1))
                        for kt in range(KT):
                            if first:
                                nx.wait(pe, kt if t == 0 else KT - 1)
                            for n in range(2):
                                for wp, hp in THREE:
                                    last = mm(bank[:, 4 + 2 * t + n, :], pw[wp][:, t, kt],
                                              src[hp][:, kt, n * HALF:(n + 1) * HALF], start=kt + wp + hp == 0,
                                              stop=kt == KT - 1 and wp == 1)
                        last.then_inc(s_ready, 1)

                    def head(i, last_head):
                        pe.wait_ge(s_qs, i * 2 + 2)
                        for t in range(8):
                            for k in range(2):
                                last = mm(bank[:, t // 2, (t % 2) * NMEM:(t % 2 + 1) * NMEM],
                                          qh[:, k, t * P:(t + 1) * P], flat(kT)[:, ds(i * (2 * NMEM) + k * NMEM, NMEM)],
                                          start=k == 0, stop=k == 1)
                        last.then_inc(s_sc, 1)
                        pe.wait_ge(s_os, i * 2 + 2)
                        if not last_head:
                            for t in range(2):
                                project_q(i + 1, t, False)
                        pe.wait_ge(s_norm, i + 1)
                        for m in range(MT):
                            for t in range(8):
                                last = nc.tensor.transpose(bank[:, 2 * m + t // 4, (t % 4) * P:(t % 4 + 1) * P],
                                                           prob[:, t, m * P:(m + 1) * P], c("ident"))
                            last.then_inc(s_pt, 1)
                        pe.wait_ge(s_vs, i + 1)
                        pe.wait_ge(s_pts, i * 2 + 2)
                        if not last_head:
                            pe.wait_ge(s_qs, i * 2 + 4)
                        for t in range(2):
                            for n in range(2):
                                for m in range(MT):
                                    last = mm(bank[:, 4 + 2 * t + n, :], vh[:, m, t * P:(t + 1) * P],
                                              prob_t[:, m, n * HALF:(n + 1) * HALF], start=m == 0, stop=m == MT - 1)
                            last.then_inc(s_o, 1)

                    nx.pe(pe)
                    for t in range(2):
                        project_q(0, t, True)
                    with pe.Fori(0, XH - 1) as i:
                        head(i, False)
                    head(XH - 1, True)

                @block.gpsimd
                def _(pool):
                    for t in range(2):
                        subtract_low(pool, t, KT + t)
                    nx.pool(pool)
                    with pool.Fori(1, XH + 1) as i:
                        for t in range(2):
                            subtract_low(pool, t, i * 2 + (KT + t))
                    for kt in range(EARLY):
                        subtract_source(pool, 1, kt)

                @block.scalar
                def _(act):
                    A = nc.scalar.activation

                    def store_q(i, t):
                        act.wait_ge(s_ready, i * 2 + (KT + t + 1))
                        A(qh[:, t, :], flat(bank[:, 4 + 2 * t:6 + 2 * t, :]), ACT.Copy).then_inc(s_qs, 1)

                    def head(i, last_head):
                        A(vh[:], v_all[:, :, ds(i * NMEM, NMEM)], ACT.Copy).then_inc(s_vs, 1)
                        act.wait_ge(s_sh, i + 1)
                        A(flat(prob), flat(prob), ACT.Exp, scale=1.0 / 16).then_inc(s_exp, 1)
                        if not last_head:
                            for t in range(2):
                                store_q(i + 1, t)
                                round_high(act, t, i * 2 + (KT + 4 + t), i + (KT // 2 + 2))
                        else:
                            act.wait_ge(s_ready, KT + 2 * XH)
                            for kt in range(EARLY):
                                act.wait_ge(s_os, 2 + kt + 1)
                                round_source(act, 1, kt)
                        for m in range(MT):
                            act.wait_ge(s_pt, i * 2 + (m + 1))
                            A(prob_t[:, m, :], flat(bank[:, 2 * m:2 * m + 2, :]), ACT.Copy).then_inc(s_pts, 1)
                        act.wait_ge(s_o, i * 2 + 2)

                    for t in range(2):
                        round_high(act, t, KT + t, KT // 2)
                    nx.act(act, squared_before=True)
                    for t in range(2):
                        store_q(0, t)
                        round_high(act, t, KT + 2 + t, KT // 2 + 1)
                    with act.Fori(0, XH - 1) as i:
                        head(i, False)
                    head(XH - 1, True)

                @block.vector
                def _(dve):
                    V = nc.vector
                    dve.sem_inc(s_os, 2)
                    nx.dve(dve, squared_before=True)
                    with dve.Fori(0, XH) as i:
                        step = [0]

                        def link(ins):
                            step[0] += 1
                            ins.then_inc(s_step, 1)
                            dve.wait_ge(s_step, i * 3 + step[0])

                        dve.wait_ge(s_sc, i + 1)
                        sc = bank[:, 0:4, :].rearrange("p a (b c) -> p (a b) c", c=NMEM)
                        link(V.tensor_reduce(mx[:], sc, AX.X, ALU.max))
                        V.tensor_tensor(prob[:], sc, mx[:].unsqueeze(2).broadcast_to([P, 8, NMEM]),
                                        ALU.subtract).then_inc(s_sh, 1)
                        dve.wait_ge(s_exp, i + 1)
                        link(V.tensor_reduce(den[:], prob[:], AX.X, ALU.add))
                        link(V.reciprocal(den[:], den[:]))
                        V.tensor_tensor(prob[:], prob[:], den[:].unsqueeze(2).broadcast_to([P, 8, NMEM]),
                                        ALU.mult).then_inc(s_norm, 1)
                        for t in range(2):
                            dve.wait_ge(s_o, i * 2 + (t + 1))
                            V.tensor_scalar(flat(oT[:, ds(i * 2 + t, 1), :]), flat(bank[:, 4 + 2 * t:6 + 2 * t, :]),
                                            1.0, None, ALU.mult).then_inc(s_os, 1)
                    dve.wait_ge(s_os, 2 * XH + 2)

            project(1, w_co)
            scope.close()

        cross()
        ffn(1, d["w_gate2"], d["w_up2"], d["w_down2"], "ffn2_norm")

        finish()


def kernel(**inputs):
    import concourse.bacc as _bacc
    from concourse.bass_utils import run_bass_kernel_spmd as _run

    def col(v):
        return np.ascontiguousarray(np.reshape(v, (-1, P)).T)

    g = {k: np.asarray(v) for k, v in inputs.items()}
    mu = g["rwkv_mu"][0]
    vec = {"ffn1_norm": g["ffn1_norm"][0], "mix_norm": g["mix_norm"][0], "cross_norm": g["cross_norm"][0],
           "mem_norm": g["mem_norm"][0], "ffn2_norm": g["ffn2_norm"][0], "final_norm": g["final_norm"],
           "mu_r": mu[0:D], "mu_k": mu[D:2 * D], "mu_v": mu[2 * D:3 * D], "w0": g["rwkv_w0"][0],
           "a0": g["rwkv_a0"][0], "k_k": g["rwkv_k_k"][0], "k_a": g["rwkv_k_a"][0],
           "r_k": np.reshape(g["rwkv_r_k"][0], (-1,)), "ln_w": g["rwkv_ln_w"][0], "ln_b": g["rwkv_ln_b"][0],
           "sink": np.repeat(g["attn_sinks"][0], CH)}
    arrays = {
        "x": g["x"][0], "mem": g["mem"][0], "consts": constants()[0],
        "params": np.concatenate([col(vec[n]) for n in PAR], 1),
        "params_u": col(mu[3 * D:3 * D + 2 * P]),
        "w_gate1": g["ffn1_w_gate"][0], "w_up1": g["ffn1_w_up"][0], "w_down1": g["ffn1_w_down"][0],
        "w_in": g["w_in"][0], "w2": g["rwkv_w2"][0], "a2": g["rwkv_a2"][0], "g2": g["rwkv_g2"][0],
        "w_out": g["w_out"][0], "w_cq": g["w_cq"][0], "w_ckv": g["w_ckv"][0], "w_co": g["w_co"][0],
        "w_gate2": g["ffn2_w_gate"][0], "w_up2": g["ffn2_w_up"][0], "w_down2": g["ffn2_w_down"][0],
    }
    arrays = {k: np.ascontiguousarray(v) for k, v in arrays.items()}
    nc = _bacc.Bacc("TRN2", target_bir_lowering=False, num_devices=1)
    d = {n: nc.dram_tensor(n, v.shape, mybir.dt.from_np(v.dtype), kind="ExternalInput").ap()
         for n, v in arrays.items()}
    out = nc.dram_tensor("out", (T, D), F32, kind="ExternalOutput").ap()
    x_spill = nc.dram_tensor("x_spill", (P, KT * T), F32, kind="Internal").ap()
    m_spill = nc.dram_tensor("m_spill", (P, KT * T), F32, kind="Internal").ap()
    build(nc, d, out, x_spill, m_spill)
    r = _run(nc, [arrays], core_ids=[0])
    return r.results[0]["out"].reshape(1, T, D)
```
